# Optimizing a Trainium2 kernel written in Bass

```python
import math
import jax, jax.numpy as jnp
from jax import lax
import numpy as np

D_MODEL = 2048
BATCH = 1
SEQ = 256
DEPTH = 1

N_BRANCH = 4
BRANCH_W = D_MODEL // N_BRANCH
NSA_HEADS = 8
NSA_KV_GROUPS = 2
NSA_HEAD_DIM = BRANCH_W // NSA_HEADS
CMP_LEN = 32
CMP_STRIDE = 16
SLC_BLOCK = 64
SLC_TOP_N = 16
WIN = 512
Q_BLOCK = 128
S5_GROUP = 16
S5_GROUPS = BRANCH_W // S5_GROUP
S5_STATE = 64
POOL_WINDOWS = (2, 4, 8, 16)
POOL_GROUPS = len(POOL_WINDOWS)
POOL_GROUP = BRANCH_W // POOL_GROUPS
RET_HEADS = 4
RET_HEAD_DIM = BRANCH_W // RET_HEADS
RET_CHUNK = 128
D_FF = 4 * D_MODEL
PLE_DIM = 256
NORM_EPS = 1e-6
NEG_INF = -1e30
FORCE_BONUS = 1e4

NSA_Q_COLS = NSA_HEADS * NSA_HEAD_DIM
NSA_KV_COLS = 6 * NSA_KV_GROUPS * NSA_HEAD_DIM
NSA_GATE_COLS = 3 * NSA_HEADS
SPLIT_SIZES = (NSA_Q_COLS, NSA_KV_COLS, NSA_GATE_COLS, BRANCH_W, BRANCH_W,
               BRANCH_W, BRANCH_W, BRANCH_W, BRANCH_W, N_BRANCH * D_MODEL)
IN_COLS = sum(SPLIT_SIZES)

kernel_name = "hybrid_nsa_s5_pool_retention_block"

def rms_norm(x, g):
    x32 = x.astype(jnp.float32)
    y = x32 * lax.rsqrt(jnp.mean(x32 * x32, axis=-1, keepdims=True) + NORM_EPS)
    return (y * g.astype(jnp.float32)).astype(x.dtype)

def masked_softmax(s, mask, axis):
    s = jnp.where(mask, s, NEG_INF)
    e = jnp.exp(s - jnp.max(s, axis=axis, keepdims=True)) * mask
    return e / jnp.maximum(jnp.sum(e, axis=axis, keepdims=True), 1e-30)

def nsa_mixer(q, kv, gates, w_cmp_k, w_cmp_v):
    B, S, _ = q.shape
    H, G, dh = NSA_HEADS, NSA_KV_GROUPS, NSA_HEAD_DIM
    R = H // G
    f32 = jnp.float32
    q = q.reshape(B, S, G, R, dh)
    kv6 = kv.reshape(B, S, 6, G, dh)
    k_cmp, v_cmp, k_slc, v_slc, k_win, v_win = [kv6[:, :, i] for i in range(6)]
    gates = jax.nn.sigmoid(gates.astype(f32)).reshape(B, S, 3, G, R)
    scale = dh ** -0.5

    n_cmp = (S - CMP_LEN) // CMP_STRIDE + 1
    blk_idx = jnp.arange(n_cmp)[:, None] * CMP_STRIDE + jnp.arange(CMP_LEN)[None, :]
    kc = jnp.einsum('bnlgd,lde->bnge', k_cmp[:, blk_idx], w_cmp_k)
    vc = jnp.einsum('bnlgd,lde->bnge', v_cmp[:, blk_idx], w_cmp_v)
    cmp_end = blk_idx[:, -1]

    n_slc = S // SLC_BLOCK
    top_n = min(SLC_TOP_N, n_slc)
    slc_start = jnp.arange(n_slc) * SLC_BLOCK
    overlap = ((blk_idx[:, 0][:, None] < slc_start[None, :] + SLC_BLOCK)
               & (cmp_end[:, None] >= slc_start[None, :])).astype(f32)
    ks_blocks = k_slc.reshape(B, n_slc, SLC_BLOCK, G, dh).transpose(0, 3, 1, 2, 4)
    vs_blocks = v_slc.reshape(B, n_slc, SLC_BLOCK, G, dh).transpose(0, 3, 1, 2, 4)
    b_ix = jnp.arange(B)[:, None, None, None]
    g_ix = jnp.arange(G)[None, :, None, None]

    k_win_p = jnp.pad(k_win, ((0, 0), (WIN, 0), (0, 0), (0, 0)))
    v_win_p = jnp.pad(v_win, ((0, 0), (WIN, 0), (0, 0), (0, 0)))

    def query_block(c):
        start = c * Q_BLOCK
        t = start + jnp.arange(Q_BLOCK)
        qb = lax.dynamic_slice_in_dim(q, start, Q_BLOCK, axis=1)
        gb = lax.dynamic_slice_in_dim(gates, start, Q_BLOCK, axis=1)

        s = jnp.einsum('bqgrd,bngd->bgrqn', qb, kc).astype(f32) * scale
        p_cmp = masked_softmax(s, cmp_end[None, :] <= t[:, None], axis=-1)
        o_cmp = jnp.einsum('bgrqn,bngd->bqgrd', p_cmp.astype(vc.dtype), vc)

        imp = jnp.einsum('bgrqn,nj->bgqj', p_cmp, overlap)
        j = jnp.arange(n_slc)
        forced = (j[None, :] == 0) | (j[None, :] == (t // SLC_BLOCK)[:, None])
        valid = slc_start[None, :] <= t[:, None]
        imp = jnp.where(valid, imp + jnp.where(forced, FORCE_BONUS, 0.0), NEG_INF)
        _, sel = lax.top_k(imp, top_n)
        ks = ks_blocks[b_ix, g_ix, sel]
        vs = vs_blocks[b_ix, g_ix, sel]
        s = jnp.einsum('bqgrd,bgqnld->bgrqnl', qb, ks).astype(f32) * scale
        key_pos = sel[..., None] * SLC_BLOCK + jnp.arange(SLC_BLOCK)
        mask = (key_pos <= t[:, None, None])[:, :, None]
        p_slc = masked_softmax(s, mask, axis=(-2, -1))
        o_slc = jnp.einsum('bgrqnl,bgqnld->bqgrd', p_slc.astype(vs.dtype), vs)

        kw = lax.dynamic_slice_in_dim(k_win_p, start, Q_BLOCK + WIN, axis=1)
        vw = lax.dynamic_slice_in_dim(v_win_p, start, Q_BLOCK + WIN, axis=1)
        pos = start - WIN + jnp.arange(Q_BLOCK + WIN)
        mask = ((pos[None, :] <= t[:, None]) & (pos[None, :] > t[:, None] - WIN)
                & (pos[None, :] >= 0))
        s = jnp.einsum('bqgrd,bkgd->bgrqk', qb, kw).astype(f32) * scale
        p_win = masked_softmax(s, mask, axis=-1)
        o_win = jnp.einsum('bgrqk,bkgd->bqgrd', p_win.astype(vw.dtype), vw)

        o = (gb[:, :, 0, :, :, None] * o_cmp + gb[:, :, 1, :, :, None] * o_slc
             + gb[:, :, 2, :, :, None] * o_win)
        return o.astype(q.dtype)

    out = lax.map(query_block, jnp.arange(S // Q_BLOCK))
    return out.transpose(1, 0, 2, 3, 4, 5).reshape(B, S, H * dh)

def _linear_recurrence(l, r):
    a_l, b_l = l
    a_r, b_r = r
    return a_l * a_r, a_r * b_l + b_r

def s5_mixer(u, a_re, a_im, log_dt, b_re, b_im, c_re, c_im, d_skip, w_glu):
    B, S, _ = u.shape
    f32 = jnp.float32
    u32 = u.astype(f32).reshape(B, S, S5_GROUPS, S5_GROUP)
    A = lax.complex(a_re.astype(f32), a_im.astype(f32))
    dt = jnp.exp(log_dt.astype(f32))[:, None]
    A_bar = jnp.exp(A * dt)
    Bm = lax.complex(b_re.astype(f32), b_im.astype(f32))
    B_bar = ((A_bar - 1.0) / A)[..., None] * Bm
    Bu = jnp.einsum('gnc,bsgc->bsgn', B_bar, u32.astype(jnp.complex64))
    a = jnp.broadcast_to(A_bar, Bu.shape)
    _, h = lax.associative_scan(_linear_recurrence, (a, Bu), axis=1)
    Cm = lax.complex(c_re.astype(f32), c_im.astype(f32))
    y = jnp.real(jnp.einsum('gcn,bsgn->bsgc', Cm, h))
    y = y + d_skip.astype(f32).reshape(S5_GROUPS, S5_GROUP) * u32
    y = jax.nn.gelu(y).reshape(B, S, BRANCH_W).astype(u.dtype)
    ga, gb = jnp.split(y @ w_glu, 2, axis=-1)
    return ga * jax.nn.sigmoid(gb)

def pool_mixer(u, w_pool, pool_scale):
    B, S, _ = u.shape
    f32 = jnp.float32
    u32 = u.astype(f32).reshape(B, S, POOL_GROUPS, POOL_GROUP)
    csum = jnp.concatenate([jnp.zeros((B, 1, POOL_GROUPS, POOL_GROUP), f32),
                            jnp.cumsum(u32, axis=1)], axis=1)
    t = jnp.arange(S)
    pooled = []
    for gi, w in enumerate(POOL_WINDOWS):
        cg = csum[:, :, gi]
        lower = jnp.concatenate([jnp.zeros((B, w - 1, POOL_GROUP), f32), cg[:, :S - w + 1]], axis=1)
        count = jnp.minimum(t + 1, w).astype(f32)[:, None]
        pooled.append((cg[:, 1:] - lower) / count)
    pooled = jnp.stack(pooled, axis=2)
    y = jnp.einsum('bsgc,gcd->bsgd', (pooled - u32).astype(u.dtype), w_pool)
    return y.reshape(B, S, BRANCH_W) * pool_scale

def _rotate_every_two(x):
    x1 = x[..., ::2]
    x2 = x[..., 1::2]
    return jnp.stack((-x2, x1), axis=-1).reshape(x.shape)

def retention_mixer(q, k, v, gate):
    B, S, _ = q.shape
    H, dh, C = RET_HEADS, RET_HEAD_DIM, RET_CHUNK
    f32 = jnp.float32
    q = q.astype(f32).reshape(B, S, H, dh)
    k = k.astype(f32).reshape(B, S, H, dh)
    v = v.astype(f32).reshape(B, S, H, dh)
    angle = jnp.repeat(1.0 / (10000.0 ** jnp.linspace(0.0, 1.0, dh // 2)), 2)
    ang = jnp.arange(S, dtype=f32)[:, None] * angle[None, :]
    sin, cos = jnp.sin(ang)[:, None, :], jnp.cos(ang)[:, None, :]
    q = q * cos + _rotate_every_two(q) * sin
    k = (k * cos + _rotate_every_two(k) * sin) * dh ** -0.5
    n_ch = S // C

    def chunks(x):
        return x.reshape(B, n_ch, C, H, dh).transpose(1, 0, 3, 2, 4)

    log_g = jnp.log(1.0 - 2.0 ** (-5.0 - jnp.arange(H, dtype=f32)))
    idx = jnp.arange(C, dtype=f32)
    rel = idx[:, None] - idx[None, :]
    decay = jnp.where(rel >= 0, jnp.exp(jnp.maximum(rel, 0.0)[None] * log_g[:, None, None]), 0.0)
    xi = jnp.exp((idx + 1.0)[None, :] * log_g[:, None])[..., None]
    zeta = jnp.exp((C - 1.0 - idx)[None, :] * log_g[:, None])[..., None]
    g_chunk = jnp.exp(C * log_g)[:, None, None]

    def step(state, inp):
        qc, kc, vc = inp
        inner = jnp.einsum('bhnm,bhme->bhne', jnp.einsum('bhnd,bhmd->bhnm', qc, kc) * decay, vc)
        cross = jnp.einsum('bhnd,bhde->bhne', qc, state) * xi
        state = state * g_chunk + jnp.einsum('bhmd,bhme->bhde', kc * zeta, vc)
        return state, inner + cross

    state0 = jnp.zeros((B, H, dh, dh), f32)
    _, y = lax.scan(step, state0, (chunks(q), chunks(k), chunks(v)))
    y = y.transpose(1, 0, 3, 2, 4).reshape(B, S, H, dh)
    y = y * lax.rsqrt(jnp.mean(y * y, axis=-1, keepdims=True) + NORM_EPS)
    return (jax.nn.silu(gate.astype(f32)) * y.reshape(B, S, H * dh)).astype(gate.dtype)

def setup_inputs(seed: int = 0) -> dict:
    key = jax.random.key(seed)
    ks = jax.random.split(key, 32)
    f32 = jnp.float32
    L = DEPTH

    def nrm(k, shape, scale):
        return jax.random.normal(k, shape, f32) * scale

    return {
        "x": nrm(ks[0], (BATCH, SEQ, D_MODEL), 1.0),
        "p": nrm(ks[1], (DEPTH, BATCH, SEQ, PLE_DIM), 1.0),
        "g_mix": 1.0 + nrm(ks[2], (L, D_MODEL), 0.1),
        "w_in": nrm(ks[3], (L, D_MODEL, IN_COLS), D_MODEL ** -0.5),
        "w_cmp_k": nrm(ks[4], (L, CMP_LEN, NSA_HEAD_DIM, NSA_HEAD_DIM), (CMP_LEN * NSA_HEAD_DIM) ** -0.5),
        "w_cmp_v": nrm(ks[5], (L, CMP_LEN, NSA_HEAD_DIM, NSA_HEAD_DIM), (CMP_LEN * NSA_HEAD_DIM) ** -0.5),
        "s5_a_re": -0.5 + nrm(ks[6], (L, S5_GROUPS, S5_STATE), 0.01),
        "s5_a_im": math.pi * jnp.arange(S5_STATE, dtype=f32)[None, None, :] + nrm(ks[7], (L, S5_GROUPS, S5_STATE), 0.01),
        "s5_log_dt": jax.random.uniform(ks[8], (L, S5_GROUPS), f32, math.log(1e-3), math.log(1e-1)),
        "s5_b_re": nrm(ks[9], (L, S5_GROUPS, S5_STATE, S5_GROUP), (2 * S5_GROUP) ** -0.5),
        "s5_b_im": nrm(ks[10], (L, S5_GROUPS, S5_STATE, S5_GROUP), (2 * S5_GROUP) ** -0.5),
        "s5_c_re": nrm(ks[11], (L, S5_GROUPS, S5_GROUP, S5_STATE), (2 * S5_STATE) ** -0.5),
        "s5_c_im": nrm(ks[12], (L, S5_GROUPS, S5_GROUP, S5_STATE), (2 * S5_STATE) ** -0.5),
        "s5_d": nrm(ks[13], (L, BRANCH_W), 1.0),
        "s5_w_glu": nrm(ks[14], (L, BRANCH_W, 2 * BRANCH_W), BRANCH_W ** -0.5),
        "pool_w": nrm(ks[15], (L, POOL_GROUPS, POOL_GROUP, POOL_GROUP), POOL_GROUP ** -0.5),
        "pool_scale": 1.0 + nrm(ks[16], (L, BRANCH_W), 0.1),
        "w_branch": nrm(ks[17], (L, N_BRANCH, BRANCH_W, D_MODEL), BRANCH_W ** -0.5),
        "w_out": nrm(ks[18], (L, D_MODEL, D_MODEL), D_MODEL ** -0.5),
        "g_mlp": 1.0 + nrm(ks[19], (L, D_MODEL), 0.1),
        "w_mlp_up": nrm(ks[20], (L, D_MODEL, D_FF), D_MODEL ** -0.5),
        "w_mlp_down": nrm(ks[21], (L, D_FF, D_MODEL), D_FF ** -0.5),
        "w_ple_gate": nrm(ks[22], (L, D_MODEL, D_MODEL), D_MODEL ** -0.5),
        "w_ple_proj": nrm(ks[23], (L, PLE_DIM, D_MODEL), PLE_DIM ** -0.5),
        "g_final": 1.0 + nrm(ks[24], (D_MODEL,), 0.1),
    }

def reference(x, p, g_mix, w_in, w_cmp_k, w_cmp_v, s5_a_re, s5_a_im, s5_log_dt, s5_b_re, s5_b_im,
              s5_c_re, s5_c_im, s5_d, s5_w_glu, pool_w, pool_scale, w_branch, w_out, g_mlp,
              w_mlp_up, w_mlp_down, w_ple_gate, w_ple_proj, g_final):
    B, S, D = x.shape
    offsets = [0]
    for size in SPLIT_SIZES:
        offsets.append(offsets[-1] + size)
    h = x
    for i in range(DEPTH):
        u = rms_norm(h, g_mix[i])
        z = u @ w_in[i]
        (z_nsa_q, z_nsa_kv, z_nsa_g, z_s5, z_pool, z_rq, z_rk, z_rv, z_rg, z_merge) = [
            z[..., offsets[j]:offsets[j + 1]] for j in range(len(SPLIT_SIZES))]

        o_nsa = nsa_mixer(z_nsa_q, z_nsa_kv, z_nsa_g, w_cmp_k[i], w_cmp_v[i])
        o_s5 = s5_mixer(z_s5, s5_a_re[i], s5_a_im[i], s5_log_dt[i], s5_b_re[i], s5_b_im[i],
                        s5_c_re[i], s5_c_im[i], s5_d[i], s5_w_glu[i])
        o_pool = pool_mixer(z_pool, pool_w[i], pool_scale[i])
        o_ret = retention_mixer(z_rq, z_rk, z_rv, z_rg)

        merge_gates = jax.nn.sigmoid(z_merge.reshape(B, S, N_BRANCH, D))
        merged = jnp.zeros_like(h)
        for j, o in enumerate((o_nsa, o_s5, o_pool, o_ret)):
            merged = merged + merge_gates[:, :, j] * (o @ w_branch[i, j])
        h = h + merged @ w_out[i]

        v = rms_norm(h, g_mlp[i])
        h = h + jnp.square(jax.nn.relu(v @ w_mlp_up[i])) @ w_mlp_down[i]

        h = h + jax.nn.sigmoid(h @ w_ple_gate[i]) * (p[i] @ w_ple_proj[i])
    return rms_norm(h, g_final)


_drawn_inputs = setup_inputs


def setup_inputs(seed=0):
    import zlib

    import numpy as np

    out = dict(_drawn_inputs(seed))
    spreads = {}
    factors = {'s5_a_re': 64.0,
     's5_a_im': 53.112,
     's5_log_dt': 53.128,
     's5_b_re': 64.0,
     's5_b_im': 64.0,
     's5_c_re': 64.0,
     's5_c_im': 64.0}
    for name, (base, spread) in spreads.items():
        noise = np.random.default_rng([zlib.crc32(name.encode()), seed]).standard_normal(out[name].shape)
        drawn = base * np.exp(spread * noise) if base else spread * noise
        out[name] = __import__('jax').numpy.asarray(drawn.astype(out[name].dtype))
    for name, factor in factors.items():
        out[name] = (out[name] * factor).astype(out[name].dtype)
    return out
```

```python
import math
from contextlib import ExitStack

import numpy as np

import concourse.bass as bass
from concourse import mybir

F32 = mybir.dt.float32
F32R = mybir.dt.float32r
ALU = mybir.AluOpType
ACT = mybir.ActivationFunctionType
AX_X = mybir.AxisListType.X

P = 128
D = 2048
S = 256
TT = S // P
KT = D // P
CW = 512
TK = 2
TPU = KT // TK
BW = D // 4
NH, NG, DH = 8, 2, 64
R = NH // NG
NCMP = (S - 32) // 16 + 1
CP = 32
RH, RD = 4, 128
SG, SN, SC = 32, 64, 16
ST = SG * SN // P
TH = P
EPS = 1e-6
NEG = -1e30
FF = 4 * D
NFG = FF // D
PD = 256

Q0 = 0
KV0 = Q0 + NH * DH
NG0 = KV0 + 6 * NG * DH
S50 = NG0 + 3 * NH
PL0 = S50 + BW
RQ0 = PL0 + BW
RK0 = RQ0 + BW
RV0 = RK0 + BW
RG0 = RV0 + BW
ZS = RG0 + BW
NZ = -(-ZS // CW)
ZLAST = ZS - (NZ - 1) * CW

U_GP = NZ
U_MB = U_GP + 1
NCH = D // CW
U_WO = U_MB + NCH * 5
U_FF = U_WO + NCH
U_PG = U_FF + NFG * 2 * NCH
U_END = U_PG + NCH
TILES = U_END * TPU
G_GP = NZ
G_MB = G_GP + 2 + NCH
G_WO = G_MB + NCH * 8
G_FF = G_WO + NCH
G_PG = G_FF + NFG * 2 * NCH
TP_RET, TP_GLU, TP_M = 0, 1, 2
TP_H = TP_M + NCH
TP_FF = TP_H + NCH
TP_P = TP_FF + NFG * NCH
RING = 4
AHEAD = RING - 1


def hybrid_layer(nc, a, out):
    ctx = ExitStack()
    with ctx:
        offset = [-(-nc.sbuf_base // 32) * 32]
        names = [0]

        def at(off, shape, dt=F32):
            names[0] += 1
            return nc.alloc_sbuf_tensor_at(f"sb{names[0]}", [P, *shape], dt, offset=off).ap()

        def size(shape):
            return 4 * int(np.prod(shape))

        class Region:

            def __init__(self, off, nbytes):
                self.off, self.end = off, off + nbytes

            def __call__(self, *shape, dt=F32):
                off, self.off = self.off, -(-(self.off + size(shape)) // 32) * 32
                assert self.off <= self.end, (self.off, self.end)
                return at(off, shape, dt)

        def region(nbytes):
            off = offset[0]
            offset[0] += nbytes
            return off, nbytes

        KB = 1024
        always = Region(*region(54 * KB))
        ra = region(32 * KB)
        rb = region(32 * KB)
        rc = region(ZS * 2 * 4)
        rd = region(nc.sbuf_top - offset[0] - 32)

        raw = always(RING, TK * CW)
        whi = always(RING, TK * CW, dt=F32R)
        wlo = always(RING, TK * CW, dt=F32R)
        ident = always(P)
        g_mix = always(KT)
        g_mlp = always(KT)
        rstd = always(3, TT)
        ssq = always(3, TT)
        p_raw = always(TK, S)
        s5p = always(3, ST)
        small = always(40, ST)

        r = Region(*ra)
        u_hi, u_lo = r(KT, S, dt=F32R), r(KT, S, dt=F32R)
        r = Region(*ra)
        v_hi, v_lo = r(KT, S, dt=F32R), r(KT, S, dt=F32R)
        r = Region(*rb)
        o_hi, o_lo = r(KT, S, dt=F32R), r(KT, S, dt=F32R)
        r = Region(*rb)
        f_hi, f_lo = r(KT, S, dt=F32R), r(KT, S, dt=F32R)
        r = Region(*rc)
        z = r(TT, ZS)
        r = Region(*rc)
        m_hi, m_lo = r(KT, S, dt=F32R), r(KT, S, dt=F32R)
        r = Region(*rd)
        xin = r(TT, D)
        xt = r(KT, S)
        xsq = r(TT, D)
        r = Region(*rd)
        y_hi, y_lo = r(4, S, dt=F32R), r(4, S, dt=F32R)
        p_hi, p_lo = r(TK, S, dt=F32R), r(TK, S, dt=F32R)
        s5_b = r(2, 4, P)
        s5_c = r(2, ST, 32)
        s5_d = r(4)
        mix_at = r.off
        m = Region(mix_at, rd[0] + rd[1] - mix_at)
        band = m(4, 2, S)
        w_pool = m(4, P)
        pool_s = m(4)
        pool_t = m(4, S)
        w_cmp = m(32, P)
        kv_ct = m(NG, S)
        m = Region(mix_at, rd[0] + rd[1] - mix_at)
        q_t = m(4, S)
        k_t = m(2, S)
        kvc = m(NG, R, CP)
        xg = m(NG, P)
        xk = m(P)
        kc_t = m(CP)
        pc = m(TT, NH, CP)
        pc_t = m(NG, TT, P)
        ngate = m(TT, 3 * NH)
        cmask = m(2, TT, CP)
        tri = m(P)
        prob = m(2, 6 * P)
        prob_t = m(2, 6 * P)
        stat = m(NH, 16)
        cstat = m(4, TT, NH)
        m = Region(mix_at, rd[0] + rd[1] - mix_at)
        rot = m(2, TT, P)
        decay = m(RH, 3 * P)
        rtmp = m(BW)
        rq_t = m(RH, S)
        rk_t = m(RH, S)
        rs_t = m(2, 3 * P)
        rgate = m(TT, BW)
        ry = m(TT, BW)
        rjunk = m(P)
        rstat = m(3, TT * RH)
        m = Region(mix_at, rd[0] + rd[1] - mix_at)
        u5_t = m(4, S)
        gr, gi, fr, fi = m(4, TH), m(4, TH), m(4, TH), m(4, TH)
        vr, vi, t1, t2 = m(4, TH), m(4, TH), m(4, TH), m(4, TH)
        sr, si = m(4, TH), m(4, TH)
        y5 = m(S)
        r = Region(*rd)
        scratch = r(3, TT * CW)
        prodt, merged = scratch[:, 0, :], scratch[:, 1, :]
        relu = [scratch[:, 1, :], scratch[:, 2, :]]
        junk = at(rd[0], [D])
        pp = r(TT, D)
        gates_off = r.off
        gates = r(4, TT * CW)
        glu_s, glu_o = gates[:, 0, :], gates[:, 1, :]
        h = at(gates_off, [TT, D])
        pgate = at(rb[0], [4, TT * CW])
        g_fin = at(rc[0], [D])

        psum = [ctx.enter_context(nc.psum_tensor(f"ps{i}", [P, 2 * CW], F32)) for i in range(4)]
        acc = psum[:2]
        aux = psum[2:]

        def sem(name):
            return ctx.enter_context(nc.semaphore(name))

        raw_in = [sem(f"raw_in{i}") for i in range(RING)]
        hi_done = sem("hi_done")
        lo_done = sem("lo_done")
        tile_used = sem("tile_used")
        grp_free = sem("grp_free")
        tp_in = sem("tp_in")
        tp_hi = sem("tp_hi")
        tp_lo = sem("tp_lo")
        x_in = sem("x_in")
        xt_in = sem("xt_in")
        x_lo = sem("x_lo")
        x_hi = sem("x_hi")
        p_in = sem("p_in")
        const_in = sem("const_in")
        pool_in = sem("pool_in")
        cmp_in = sem("cmp_in")
        mask_in = sem("mask_in")
        ret_in = sem("ret_in")
        h_in = sem("h_in")
        fin_in = sem("fin_in")
        out_sem = sem("out_stored")
        ssq_done = sem("ssq_done")
        var_done = sem("var_done")
        std_done = sem("std_done")
        rstd_done = sem("rstd_done")
        pt_in = sem("pt_in")
        pt_hi = sem("pt_hi")
        pt_lo = sem("pt_lo")
        dve = sem("dve_step")
        pl = sem("pool_step")
        z_dve = sem("z_dve")
        sg = {n: sem(n) for n in (
            "pool_band pool_copied pool_mixed pool_hi pool_lo "
            "cmp_tr cmp_copied cmp_sum cmp_sb xg_tr xg_sb kc_tr kc_sb q_tr q_sb k_tr k_sb "
            "ngate_done cs_done cs_sub cs_exp pc_done pc_tr pc_sb "
            "sc_done sc_max sc_exp sc_scaled pt_tr pt_sb pv_done nsa_hi nsa_lo "
            "rot_done rq_tr rq_sb rk_tr rk_sb rs_done rs_dec ry_done ry_ssq ry_var ry_std rgate_done ret_done "
            "s5_dt s5_arg s5_exp s5_th s5_sin tab_done u5_tr u5_sb bu_done bu_used sh_done c_done y5_done y5_gelu y5_hi y5_lo "
            "glu_sig glu_done relu_done sq_done pg_sig merged_done br_tmp").split()}

        C = CW

        def tile_source(t_unit, kind, i, j):
            rows = slice(j * TK * P, (j + 1) * TK * P)
            return {
                "z": lambda: a["w_in"][rows, bass.ds(i * C, C)] if not isinstance(i, int)
                else a["w_in"][rows, i * C:(i + 1) * C],
            }[kind]().rearrange("(k p) n -> p k n", p=P)

        def cols(w, r0, c0, width=C):
            rows = slice(r0, r0 + TK * P) if isinstance(r0, int) else bass.ds(r0, TK * P)
            cs = slice(c0, c0 + width) if isinstance(c0, int) else bass.ds(c0, width)
            return w[rows, cs].rearrange("(k p) n -> p k n", p=P)

        def load_tile(sp, u, j, src, width=C):
            if not isinstance(u, int) or u * TPU + j >= RING:
                sp.wait_ge(lo_done, u * TPU + (j - RING + 1))
            s = j % RING
            sp.dma_start(raw[:, s, :].rearrange("p (k n) -> p k n", k=TK)[:, :, 0:width], src)\
                .then_inc(raw_in[s], 16)

        def split_hi(act, u, j):
            if isinstance(u, int) and u * TPU + j >= TILES:
                return
            act.wait_ge(raw_in[j % RING], u * (16 * TPU // RING) + 16 * (j // RING + 1))
            if not isinstance(u, int) or u * TPU + j >= RING:
                act.wait_ge(tile_used, u * TPU + (j - RING + 1))
            act.activation(whi[:, j % RING, :], raw[:, j % RING, :], ACT.Copy).then_inc(hi_done, 1)

        def split_lo(eng, u, j):
            if isinstance(u, int) and u * TPU + j >= TILES:
                return
            eng.wait_ge(hi_done, u * TPU + (j + 1))
            eng.tensor_tensor(wlo[:, j % RING, :], raw[:, j % RING, :], whi[:, j % RING, :].bitcast(F32),
                              ALU.subtract).then_inc(lo_done, 1)

        def products(pe, u, j, g, par, x_hi, x_lo, kt, first, last, width=C):
            if first:
                if not isinstance(g, int) or g >= 2:
                    pe.wait_ge(grp_free, 2 * g - 2)
            pe.wait_ge(lo_done, u * TPU + (j + 1))
            s = j % RING
            for k in range(TK):
                w_h = whi[:, s, k * C:k * C + width]
                w_l = wlo[:, s, k * C:k * C + width]
                for tt in range(TT):
                    o = acc[par][:, tt * C:tt * C + width]
                    xh = x_hi[:, kt + k, tt * P:(tt + 1) * P]
                    xl = x_lo[:, kt + k, tt * P:(tt + 1) * P]
                    pe.matmul(o, xh, w_h, start=first and k == 0, stop=False)
                    pe.matmul(o, xh, w_l, start=False, stop=False)
                    mm = pe.matmul(o, xl, w_h, start=False, stop=last and k == TK - 1)
            mm.then_inc(tile_used, 1)

        def group_ready(eng, u, j):
            eng.wait_ge(tile_used, u * TPU + (j + 1))

        def quad_in(pe, n, par, src):
            if not isinstance(n, int) or n >= 2:
                pe.wait_ge(tp_lo, n - 1)
            for k in range(4):
                for tt in range(TT):
                    mm = pe.transpose(aux[par][:, k * S + tt * P:k * S + (tt + 1) * P], src(k, tt), ident[:, :])
            mm.then_inc(tp_in, 1)

        def quad_hi(act, n, par, dst, scale=None):
            act.wait_ge(tp_in, n + 1)
            if scale is None:
                act.activation(dst.rearrange("p k t -> p (k t)"), aux[par][:, :], ACT.Copy).then_inc(tp_hi, 1)
                return
            for k in range(4):
                i = act.activation(dst[:, k, :], aux[par][:, k * S:(k + 1) * S], ACT.Copy, scale=scale[:, k:k + 1])
            i.then_inc(tp_hi, 1)

        def quad_lo(v, n, par, dst, hi, scale=None):
            v.wait_ge(tp_hi, n + 1)
            if scale is None:
                v.tensor_tensor(dst.rearrange("p k t -> p (k t)"), aux[par][:, :],
                                hi.rearrange("p k t -> p (k t)").bitcast(F32), ALU.subtract).then_inc(tp_lo, 1)
                return
            for k in range(4):
                i = v.scalar_tensor_tensor(out=dst[:, k, :], in0=aux[par][:, k * S:(k + 1) * S],
                                           scalar=scale[:, k:k + 1], in1=hi[:, k, :].bitcast(F32),
                                           op0=ALU.mult, op1=ALU.subtract)
            i.then_inc(tp_lo, 1)

        def features(x, tt, k):
            return x[:, tt, k * P:(k + 1) * P]

        block = ctx.enter_context(nc.Block())

        @block.sync
        def _(sp):
            sp.dma_start(ident[:, :], a["ident"]).then_inc(const_in, 16)
            sp.dma_start(g_mix[:, :], a["g_mix"]).then_inc(const_in, 16)
            sp.dma_start(g_mlp[:, :], a["g_mlp"]).then_inc(const_in, 16)
            sp.dma_start(s5p[:, :, :], a["s5p"]).then_inc(const_in, 16)
            sp.dma_start(xt[:, :, :], a["xt"].rearrange("(k p) t -> p k t", p=P)).then_inc(xt_in, 16)
            for i in range(NZ):
                width = C if i < NZ - 1 else ZLAST
                for j in range(TPU):
                    load_tile(sp, i, j, cols(a["w_mix"], j * TK * P, i * C, width), width)
                    if i == 0 and j == 3:
                        sp.dma_start(xin[:, :, :], a["x"].rearrange("(t p) d -> p t d", p=P)).then_inc(x_in, 16)
                        sp.dma_start(p_raw[:, :, :], a["pt"].rearrange("(k p) t -> p k t", p=P)).then_inc(p_in, 16)
            sp.wait_ge(x_lo, 1)
            sp.wait_ge(ssq_done, TT)
            sp.dma_start(band[:, :, :, :], a["band"]).then_inc(pool_in, 16)
            sp.dma_start(w_pool[:, :, :], a["w_pool"].rearrange("g c d -> c g d")).then_inc(pool_in, 16)
            sp.dma_start(pool_s[:, :], a["pool_scale"]).then_inc(pool_in, 16)
            sp.dma_start(w_cmp[:, :, :], a["w_cmp"]).then_inc(cmp_in, 16)
            sp.dma_start(s5_b[:, :, :, :], a["s5_b"]).then_inc(cmp_in, 16)
            sp.dma_start(s5_c[:, :, :, :], a["s5_c"]).then_inc(cmp_in, 16)
            sp.dma_start(s5_d[:, :], a["s5_d"]).then_inc(cmp_in, 16)
            sp.wait_ge(sg["pool_lo"], 1)
            sp.wait_ge(sg["cmp_sum"], 1)
            sp.dma_start(cmask[:, :, :, :], a["cmask"]).then_inc(mask_in, 16)
            sp.dma_start(tri[:, :], a["tri"]).then_inc(mask_in, 16)
            sp.wait_ge(sg["nsa_lo"], 2)
            sp.dma_start(rot[:, :, :, :], a["rot"]).then_inc(ret_in, 16)
            sp.dma_start(decay[:, :, :], a["decay"]).then_inc(ret_in, 16)
            for j in range(TPU):
                if j < 4:
                    src = cols(a["w_glu"], (j % 2) * TK * P, (j // 2) * C)
                else:
                    src = cols(a["w_pp"], 0, (j - 4) * C)
                load_tile(sp, U_GP, j, src)
            for n in range(NCH):
                for b in range(4):
                    for j in range(TPU):
                        load_tile(sp, U_MB + 5 * n + b, j, cols(a["w_in"], j * TK * P, ZS + b * D + n * C))
                for j in range(TPU):
                    load_tile(sp, U_MB + 5 * n + 4, j, cols(a["w_branch"], j * TK * P, n * C))
            for n in range(NCH):
                for j in range(TPU):
                    load_tile(sp, U_WO + n, j, cols(a["w_out"], j * TK * P, n * C))
                if n == 0:
                    sp.wait_ge(sg["merged_done"], NCH)
                    sp.dma_start(h[:, :, :], a["x"].rearrange("(t p) d -> p t d", p=P)).then_inc(h_in, 16)
            with sp.Fori(0, NFG) as g:
                for n in range(NCH):
                    for j in range(TPU):
                        load_tile(sp, g * (2 * NCH) + (U_FF + n), j, cols(a["w_up"], j * TK * P, g * D + n * C))
                for n in range(NCH):
                    for j in range(TPU):
                        load_tile(sp, g * (2 * NCH) + (U_FF + NCH + n), j,
                                  cols(a["w_down"], g * D + j * TK * P, n * C))
            sp.dma_start(g_fin[:, :], a["g_final"]).then_inc(fin_in, 16)
            for n in range(NCH):
                for j in range(TPU):
                    load_tile(sp, U_PG + n, j, cols(a["w_pg"], j * TK * P, n * C))
            sp.wait_ge(z_dve, 1)
            sp.dma_start(out.rearrange("(t p) d -> p t d", p=P), h[:, :, :]).then_inc(out_sem, 16)
            sp.wait_ge(out_sem, 16)

        @block.tensor
        def _(pe):
            pe.wait_ge(const_in, 64)
            pe.wait_ge(x_lo, 1)
            for i in range(NZ):
                width = C if i < NZ - 1 else ZLAST
                for j in range(TPU):
                    products(pe, i, j, i, i % 2, u_hi, u_lo, j * TK, j == 0, j == TPU - 1, width)
            pe.wait_ge(grp_free, 2 * NZ)
            pe.wait_ge(pool_in, 48)
            for g in range(4):
                pe.matmul(aux[0][:, g * S:(g + 1) * S], z[:, 0, PL0 + g * P:PL0 + (g + 1) * P],
                          band[:, g, 0, :], start=True, stop=False)
                mm = pe.matmul(aux[0][:, g * S + P:(g + 1) * S], z[:, 1, PL0 + g * P:PL0 + (g + 1) * P],
                               band[:, g, 1, P:S], start=False, stop=True)
            mm.then_inc(sg["pool_band"], 1)
            for g in range(NG):
                for tt in range(TT):
                    mm = pe.transpose(aux[1][:, g * S + tt * P:g * S + (tt + 1) * P],
                                      z[:, tt, KV0 + g * P:KV0 + (g + 1) * P], ident[:, :])
            mm.then_inc(sg["cmp_tr"], 1)
            pe.wait_ge(sg["pool_copied"], 1)
            for g in range(4):
                mm = pe.matmul(aux[0][:, g * S:(g + 1) * S], w_pool[:, g, :], pool_t[:, g, :], start=True, stop=True)
            mm.then_inc(sg["pool_mixed"], 1)
            pe.wait_ge(cmp_in, 64)
            pe.wait_ge(sg["cmp_copied"], 1)
            o = aux[1][:, C:C + NG * NCMP].rearrange("p (g n) -> p g n", g=NG)
            for l in range(32):
                mm = pe.matmul(o, w_cmp[:, l, :], kv_ct[:, :, l:l + 16 * (NCMP - 1) + 1:16],
                               start=l == 0, stop=l == 31)
            mm.then_inc(sg["cmp_sum"], 1)
            pe.wait_ge(sg["pool_lo"], 1)
            for k in range(4):
                for tt in range(TT):
                    mm = pe.transpose(aux[0][:, k * S + tt * P:k * S + (tt + 1) * P],
                                      z[:, tt, Q0 + k * P:Q0 + (k + 1) * P], ident[:, :])
            mm.then_inc(sg["q_tr"], 1)
            pe.wait_ge(sg["cmp_sb"], 1)
            for g in range(NG):
                mm = pe.transpose(aux[1][:, g * P:(g + 1) * P], kvc[:, g, :, :], ident[:, :])
            mm.then_inc(sg["xg_tr"], 1)
            pe.wait_ge(sg["xg_sb"], 1)
            pe.transpose(aux[1][:, C:C + CP], xk[0:CP, :], ident[0:CP, 0:CP]).then_inc(sg["kc_tr"], 1)
            pe.wait_ge(sg["q_sb"], 1)
            for i in range(2):
                c0 = KV0 + (2 + 2 * i) * P
                for tt in range(TT):
                    o = i * S + tt * P
                    mm = pe.transpose(aux[0][:, o:o + P], z[:, tt, c0:c0 + P], ident[:, :])
            mm.then_inc(sg["k_tr"], 1)
            pe.wait_ge(sg["kc_sb"], 1)
            for g in range(NG):
                for tt in range(TT):
                    for rr in range(R):
                        o = g * C + (tt * R + rr) * CP
                        mm = pe.matmul(aux[1][:, o:o + CP], q_t[g * DH:(g + 1) * DH, rr, tt * P:(tt + 1) * P],
                                       kc_t[g * DH:(g + 1) * DH, :], start=True, stop=True)
            mm.then_inc(sg["cs_done"], 1)
            pe.wait_ge(sg["k_sb"], 1)

            def scores(hd):
                lo = DH * (hd % 2)
                if hd >= 1:
                    pe.wait_ge(sg["sc_exp"], 4 * hd)
                for tt in (1, 0):
                    for i in range(2):
                        n = (tt + 1) * P
                        o = (0 if tt else C) + i * n
                        mm = pe.matmul(aux[0][:, o:o + n], q_t[lo:lo + DH, hd // 2, tt * P:(tt + 1) * P],
                                       k_t[lo:lo + DH, i, 0:n], start=True, stop=True)
                mm.then_inc(sg["sc_done"], 1)

            scores(0)
            pe.wait_ge(sg["pc_done"], 1)
            for g in range(NG):
                for tt in range(TT):
                    o = (g * TT + tt) * P
                    mm = pe.transpose(aux[1][:, o:o + P], pc[:, tt, g * R:(g + 1) * R, :], ident[:, :])
            mm.then_inc(sg["pc_tr"], 1)
            pe.wait_ge(sg["pc_sb"], 1)
            for hd in range(NH):
                pe.wait_ge(sg["sc_scaled"], hd + 1)
                if hd >= 1:
                    pe.wait_ge(sg["pt_sb"], 2 * hd)
                blocks = [(i, b) for i in range(2) for b in range(3)]
                for n, (i, b) in enumerate(blocks):
                    src = prob[:, hd % 2, :]
                    s0 = 4 * P + i * P if b == 0 else i * 2 * P + (b - 1) * P
                    o = aux[1][:, n * P:(n + 1) * P] if n < 4 else aux[0][:, C + 2 * P + (n - 4) * P:C + 2 * P + (n - 3) * P]
                    mm = pe.transpose(o, src[:, s0:s0 + P], ident[:, :])
                mm.then_inc(sg["pt_tr"], 1)
                pe.wait_ge(sg["pt_sb"], 2 * hd + 2)
                if hd + 1 < NH:
                    scores(hd + 1)
                lo = DH * (hd % 2)
                g = hd % 2
                if hd == 4:
                    pe.wait_ge(sg["nsa_lo"], 1)
                o = aux[1][lo:lo + DH, C + (hd // 2 % 2) * S:C + (hd // 2 % 2 + 1) * S]
                first = True
                for i in range(2):
                    v0 = KV0 + (3 + 2 * i) * P + g * DH
                    for kt in range(2):
                        b = prob_t[:, hd % 2, (3 * i + 2 * kt) * P:(3 * i + 2 + kt) * P]
                        pe.matmul(o[:, kt * P:S], z[:, kt, v0:v0 + DH], b, start=first, stop=False)
                        first = False
                rr = hd // 2
                pe.matmul(o, xg[rr * CP:(rr + 1) * CP, g, DH:P], pc_t[rr * CP:(rr + 1) * CP, g, :, :],
                          start=False, stop=True).then_inc(sg["pv_done"], 1)
            pe.wait_ge(sg["nsa_lo"], 2)
            pe.wait_ge(sg["rot_done"], 4)
            for k in range(4):
                for tt in range(TT):
                    mm = pe.transpose(aux[0][:, k * S + tt * P:k * S + (tt + 1) * P],
                                      z[:, tt, RQ0 + k * P:RQ0 + (k + 1) * P], ident[:, :])
            mm.then_inc(sg["rq_tr"], 1)
            for k in range(4):
                for tt in range(TT):
                    mm = pe.transpose(aux[1][:, k * S + tt * P:k * S + (tt + 1) * P],
                                      z[:, tt, RK0 + k * P:RK0 + (k + 1) * P], ident[:, :])
            mm.then_inc(sg["rk_tr"], 1)
            pe.wait_ge(sg["rq_sb"], 1)
            pe.wait_ge(sg["rk_sb"], 1)

            def ret_scores(hd):
                if hd >= 2:
                    pe.wait_ge(sg["rs_dec"], hd - 1)
                b = (hd % 2) * C
                pe.matmul(aux[0][:, b:b + S], rk_t[:, hd, 0:P], rq_t[:, hd, :], start=True, stop=True)
                pe.matmul(aux[0][:, b + S:b + 3 * P], rk_t[:, hd, P:S], rq_t[:, hd, P:S],
                          start=True, stop=True).then_inc(sg["rs_done"], 1)

            ret_scores(0)
            for hd in range(RH):
                if hd + 1 < RH:
                    ret_scores(hd + 1)
                pe.wait_ge(sg["rs_dec"], hd + 1)
                if hd:
                    pe.wait_ge(sg["ry_ssq"], TT * hd)
                s_ = rs_t[:, hd % 2, :]
                v = lambda tt: z[:, tt, RV0 + hd * P:RV0 + (hd + 1) * P]
                pe.matmul(aux[1][:, hd * P:(hd + 1) * P], s_[:, 0:P], v(0), start=True, stop=True)
                pe.matmul(aux[1][:, C + hd * P:C + (hd + 1) * P], s_[:, P:2 * P], v(0), start=True, stop=False)
                pe.matmul(aux[1][:, C + hd * P:C + (hd + 1) * P], s_[:, 2 * P:3 * P], v(1),
                          start=False, stop=True).then_inc(sg["ry_done"], 1)
            for k in range(4):
                for tt in range(TT):
                    mm = pe.transpose(aux[0][:, k * S + tt * P:k * S + (tt + 1) * P],
                                      z[:, tt, S50 + k * P:S50 + (k + 1) * P], ident[:, :])
            mm.then_inc(sg["u5_tr"], 1)
            pe.wait_ge(sg["ret_done"], 1)
            quad_in(pe, TP_RET, 1, lambda k, tt: features(ry, tt, k))
            pe.wait_ge(tp_lo, TP_RET + 1)
            pe.wait_ge(sg["u5_sb"], 1)
            for q in range(4):
                for hf in range(TT):
                    n = q * TT + hf
                    if n:
                        pe.wait_ge(sg["bu_used"], n)
                    for i in range(4):
                        if n or i:
                            pe.wait_ge(sg["bu_done"], 4 * n + i)
                        for im in range(2):
                            o = im * C + i * P
                            mm = pe.matmul(aux[0][:, o:o + P], s5_b[32 * i:32 * i + 32, im, q, :],
                                           u5_t[32 * i:32 * i + 32, q, hf * P:(hf + 1) * P], start=True, stop=True)
                        mm.then_inc(sg["bu_done"], 1)
                    if hf == 0 and q >= 2:
                        pe.wait_ge(sg["y5_done"], q - 1)
                    pe.wait_ge(sg["sh_done"], n + 1)
                    for i in range(4):
                        o = aux[1][32 * i:32 * i + 32, (q % 2) * C + hf * P:(q % 2) * C + (hf + 1) * P]
                        pe.matmul(o, s5_c[:, 0, 4 * q + i, :], vr[:, i, :], start=True, stop=False)
                        mm = pe.matmul(o, s5_c[:, 1, 4 * q + i, :], vi[:, i, :], start=False, stop=True)
                    mm.then_inc(sg["c_done"], 1)
            pe.wait_ge(sg["y5_lo"], 4)
            pe.wait_ge(pt_lo, 1)
            for j in range(TPU):
                if j < 4:
                    products(pe, U_GP, j, G_GP + j // 2, (G_GP + j // 2) % 2, y_hi, y_lo, (j % 2) * TK,
                             j % 2 == 0, j % 2 == 1)
                else:
                    products(pe, U_GP, j, G_GP + j - 2, (G_GP + j - 2) % 2, p_hi, p_lo, 0, True, True)
            pe.wait_ge(sg["glu_done"], 1)
            quad_in(pe, TP_GLU, 0, lambda k, tt: glu_o[:, tt * C + k * P:tt * C + (k + 1) * P])
            pe.wait_ge(tp_lo, TP_GLU + 1)
            for n in range(NCH):
                for b in range(4):
                    for j in range(TPU):
                        g = G_MB + 8 * n + b
                        products(pe, U_MB + 5 * n + b, j, g, g % 2, u_hi, u_lo, j * TK, j == 0, j == TPU - 1)
                for j in range(TPU):
                    g = G_MB + 8 * n + 4 + j // 2
                    products(pe, U_MB + 5 * n + 4, j, g, g % 2, o_hi, o_lo, j * TK, j % 2 == 0, j % 2 == 1)
                pe.wait_ge(sg["merged_done"], n + 1)
                quad_in(pe, TP_M + n, (TP_M + n) % 2, lambda k, tt: merged[:, tt * C + k * P:tt * C + (k + 1) * P])
            pe.wait_ge(tp_lo, TP_M + NCH)
            for n in range(NCH):
                for j in range(TPU):
                    g = G_WO + n
                    products(pe, U_WO + n, j, g, g % 2, m_hi, m_lo, j * TK, j == 0, j == TPU - 1)
                    if j == 4 and n:
                        pe.wait_ge(grp_free, 2 * (G_WO + n))
                        quad_in(pe, TP_H + n - 1, (TP_H + n - 1) % 2, lambda k, tt: features(h, tt, 4 * (n - 1) + k))
            pe.wait_ge(grp_free, 2 * (G_WO + NCH))
            quad_in(pe, TP_H + 3, (TP_H + 3) % 2, lambda k, tt: features(h, tt, 12 + k))
            pe.wait_ge(tp_lo, TP_H + NCH)
            with pe.Fori(0, NFG) as g:
                for n in range(2 * NCH):
                    up = n < NCH
                    for j in range(TPU):
                        if n == NCH and j == TPU - 2:
                            pe.wait_ge(tp_lo, g * NCH + (TP_FF + NCH))
                        products(pe, g * (2 * NCH) + (U_FF + n), j, g * (2 * NCH) + (G_FF + n), (G_FF + n) % 2,
                                 v_hi if up else f_hi, v_lo if up else f_lo, j * TK, j == 0, j == TPU - 1)
                        if j == 3 and 1 <= n <= NCH:
                            pe.wait_ge(sg["sq_done"], g * NCH + n)
                            rl = relu[(n - 1) % 2]
                            quad_in(pe, g * NCH + (TP_FF + n - 1), (TP_FF + n - 1) % 2,
                                    lambda k, tt: rl[:, tt * C + k * P:tt * C + (k + 1) * P])
            for k in range(4):
                pe.wait_ge(grp_free, 2 * (G_PG - NCH + k + 1))
                quad_in(pe, TP_P + k, (TP_P + k) % 2, lambda kk, tt: features(h, tt, 4 * k + kk))
            pe.wait_ge(tp_lo, TP_P + 4)
            for n in range(NCH):
                for j in range(TPU):
                    g = G_PG + n
                    products(pe, U_PG + n, j, g, g % 2, v_hi, v_lo, j * TK, j == 0, j == TPU - 1)

        @block.scalar
        def _(act):
            act.wait_ge(xt_in, 16)
            act.wait_ge(const_in, 64)
            for k in range(KT):
                i = act.activation(u_hi[:, k, :], xt[:, k, :], ACT.Copy, scale=g_mix[:, k:k + 1])
                if k % 4 == 3:
                    i.then_inc(x_hi, 1)
            for j in range(AHEAD):
                split_hi(act, 0, j)
            act.wait_ge(x_in, 16)
            for tt in range(TT):
                act.activation(xsq[:, tt, :], xin[:, tt, :], ACT.Square, accum_out=ssq[:, 0, tt:tt + 1])\
                    .then_inc(ssq_done, 1)
            act.wait_ge(var_done, 1)
            act.activation(rstd[:, 0, :], ssq[:, 0, :], ACT.Sqrt).then_inc(std_done, 1)
            act.wait_ge(rstd_done, 1)
            for i in range(NZ):
                for j in range(TPU):
                    if i * TPU + j + AHEAD < NZ * TPU:
                        split_hi(act, i, j + AHEAD)
                group_ready(act, i, TPU - 1)
                width = C if i < NZ - 1 else ZLAST
                act.activation(z[:, 0, i * C:i * C + width], acc[i % 2][:, 0:width], ACT.Copy,
                               scale=rstd[:, 0, 0:1]).then_inc(grp_free, 1)
            act.activation(small[:, 0, :], s5p[:, 2, :], ACT.Exp).then_inc(sg["s5_dt"], 1)
            act.wait_ge(sg["s5_arg"], 1)
            act.activation(small[:, 2, :], small[:, 1, :], ACT.Exp).then_inc(sg["s5_exp"], 1)
            act.wait_ge(sg["s5_th"], 1)
            act.activation(small[:, 8, :], small[:, 6, :], ACT.Sin).then_inc(sg["s5_sin"], 1)
            act.activation(small[:, 9, :], small[:, 7, :], ACT.Sin).then_inc(sg["s5_sin"], 1)
            act.wait_ge(sg["pool_band"], 1)
            act.activation(pool_t[:, :, :].rearrange("p g t -> p (g t)"), aux[0][:, :], ACT.Copy)\
                .then_inc(sg["pool_copied"], 1)
            act.wait_ge(sg["pool_mixed"], 1)
            for g in range(4):
                act.activation(o_hi[:, 8 + g, :], aux[0][:, g * S:(g + 1) * S], ACT.Copy, scale=pool_s[:, g:g + 1])\
                    .then_inc(sg["pool_hi"], 1)
            act.wait_ge(sg["q_tr"], 1)
            act.activation(q_t[:, :, :].rearrange("p k t -> p (k t)"), aux[0][:, :], ACT.Copy, scale=DH ** -0.5)\
                .then_inc(sg["q_sb"], 1)
            act.wait_ge(sg["k_tr"], 1)
            act.activation(k_t[:, :, :].rearrange("p k t -> p (k t)"), aux[0][:, 0:2 * S], ACT.Copy).then_inc(sg["k_sb"], 1)
            act.wait_ge(sg["cmp_sb"], 1)
            act.activation(ngate[:, :, :], z[:, :, NG0:NG0 + 3 * NH], ACT.Sigmoid).then_inc(sg["ngate_done"], 1)
            act.wait_ge(sg["cs_sub"], 1)
            act.activation(pc[:, :, :, :].rearrange("p t h n -> p (t h n)"),
                           pc[:, :, :, :].rearrange("p t h n -> p (t h n)"), ACT.Exp).then_inc(sg["cs_exp"], 1)

            for hd in range(NH):
                act.wait_ge(sg["sc_max"], hd + 1)
                if hd >= 2:
                    act.wait_ge(sg["pt_tr"], hd - 1)
                for n, (o, w) in enumerate(((0, S), (S, S), (C, P), (C + P, P))):
                    act.activation(prob[:, hd % 2, o:o + w], aux[0][:, o:o + w], ACT.Exp, bias=stat[:, hd, n:n + 1],
                                   accum_out=stat[:, hd, 4 + n:5 + n]).then_inc(sg["sc_exp"], 1)
                act.wait_ge(sg["pt_tr"], hd + 1)
                if hd >= 2:
                    act.wait_ge(sg["pv_done"], hd - 1)
                act.activation(prob_t[:, hd % 2, 0:C], aux[1][:, 0:C], ACT.Copy).then_inc(sg["pt_sb"], 1)
                act.activation(prob_t[:, hd % 2, C:6 * P], aux[0][:, C + S:2 * C], ACT.Copy).then_inc(sg["pt_sb"], 1)
                if hd % 4 == 3:
                    act.wait_ge(sg["pv_done"], hd + 1)
                    k = hd // 4 * 2
                    act.activation(o_hi[:, k:k + 2, :].rearrange("p k t -> p (k t)"), aux[1][:, C:2 * C], ACT.Copy)\
                        .then_inc(sg["nsa_hi"], 1)
                    act.wait_ge(sg["nsa_lo"], hd // 4 + 1)
            act.wait_ge(sg["rq_tr"], 1)
            act.activation(rq_t[:, :, :].rearrange("p k t -> p (k t)"), aux[0][:, :], ACT.Copy).then_inc(sg["rq_sb"], 1)
            act.wait_ge(sg["rk_tr"], 1)
            act.activation(rk_t[:, :, :].rearrange("p k t -> p (k t)"), aux[1][:, :], ACT.Copy).then_inc(sg["rk_sb"], 1)
            act.activation(rgate[:, :, :], z[:, :, RG0:RG0 + BW], ACT.Silu).then_inc(sg["rgate_done"], 1)
            for hd in range(RH):
                act.wait_ge(sg["ry_done"], hd + 1)
                for tt in range(TT):
                    if hd or tt:
                        act.wait_ge(sg["ry_ssq"], hd * TT + tt)
                    act.activation(rjunk[:, :], aux[1][:, tt * C + hd * P:tt * C + (hd + 1) * P], ACT.Square,
                                   accum_out=rstat[:, 0, tt * RH + hd:tt * RH + hd + 1]).then_inc(sg["ry_ssq"], 1)
            act.wait_ge(sg["ry_var"], 1)
            act.activation(rstat[:, 1, :], rstat[:, 0, :], ACT.Sqrt).then_inc(sg["ry_std"], 1)
            act.wait_ge(sg["ret_done"], 1)
            quad_hi(act, TP_RET, 1, o_hi[:, 12:16, :])
            act.wait_ge(tp_lo, TP_RET + 1)
            act.wait_ge(sg["u5_tr"], 1)
            act.activation(u5_t[:, :, :].rearrange("p k t -> p (k t)"), aux[0][:, :], ACT.Copy).then_inc(sg["u5_sb"], 1)
            for q in range(4):
                act.wait_ge(sg["y5_done"], q + 1)
                act.activation(y5[:, :], y5[:, :], ACT.Gelu_apprx_tanh).then_inc(sg["y5_gelu"], 1)
                act.wait_ge(sg["y5_gelu"], q + 1)
                act.activation(y_hi[:, q, :], y5[:, :], ACT.Copy).then_inc(sg["y5_hi"], 1)
            act.wait_ge(p_in, 16)
            act.activation(p_hi[:, :, :], p_raw[:, :, :], ACT.Copy).then_inc(pt_hi, 1)
            for j in range(AHEAD):
                split_hi(act, U_GP, j)
            for j in range(TPU):
                split_hi(act, U_GP, j + AHEAD)
                if j == 3:
                    group_ready(act, U_GP, 3)
                    g = G_GP + 1
                    act.activation(glu_s, acc[g % 2][:, :], ACT.Sigmoid).then_inc(sg["glu_sig"], 1)
            quad_hi(act, TP_GLU, 0, o_hi[:, 4:8, :])
            for n in range(NCH):
                for b in range(4):
                    u = U_MB + 5 * n + b
                    g = G_MB + 8 * n + b
                    for j in range(TPU):
                        split_hi(act, u, j + AHEAD)
                    group_ready(act, u, TPU - 1)
                    if n:
                        act.wait_ge(sg["merged_done"], n)
                    for tt in range(TT):
                        act.activation(gates[:, b, tt * C:(tt + 1) * C], acc[g % 2][:, tt * C:(tt + 1) * C],
                                       ACT.Sigmoid, scale=rstd[:, 0, tt:tt + 1]).then_inc(grp_free, 1)
                for j in range(TPU):
                    split_hi(act, U_MB + 5 * n + 4, j + AHEAD)
                quad_hi(act, TP_M + n, (TP_M + n) % 2, m_hi[:, 4 * n:4 * n + 4, :])
            for n in range(NCH):
                for j in range(TPU):
                    split_hi(act, U_WO + n, j + AHEAD)
                    if j == 5 and n:
                        quad_hi(act, TP_H + n - 1, (TP_H + n - 1) % 2, v_hi[:, 4 * n - 4:4 * n, :],
                                g_mlp[:, 4 * n - 4:4 * n])
            quad_hi(act, TP_H + 3, (TP_H + 3) % 2, v_hi[:, 12:16, :], g_mlp[:, 12:16])
            act.wait_ge(tp_lo, TP_H + NCH)
            for tt in range(TT):
                if tt:
                    act.wait_ge(ssq_done, TT + tt)
                act.activation(junk[:, :], h[:, tt, :], ACT.Square, accum_out=ssq[:, 1, tt:tt + 1])\
                    .then_inc(ssq_done, 1)
            act.wait_ge(var_done, 2)
            act.activation(rstd[:, 1, :], ssq[:, 1, :], ACT.Sqrt).then_inc(std_done, 1)
            act.wait_ge(rstd_done, 2)
            with act.Fori(0, NFG) as g:
                for n in range(2 * NCH):
                    u = g * (2 * NCH) + (U_FF + n)
                    for j in range(TPU):
                        split_hi(act, u, j + AHEAD)
                        if j == 5 and 1 <= n <= NCH:
                            quad_hi(act, g * NCH + (TP_FF + n - 1), (TP_FF + n - 1) % 2, f_hi[:, 4 * n - 4:4 * n, :])
                    if n < NCH:
                        group_ready(act, u, TPU - 1)
                        for tt in range(TT):
                            act.activation(relu[n % 2][:, tt * C:(tt + 1) * C],
                                           acc[(G_FF + n) % 2][:, tt * C:(tt + 1) * C], ACT.Relu,
                                           scale=rstd[:, 1, tt:tt + 1]).then_inc(grp_free, 1)
            for k in range(4):
                quad_hi(act, TP_P + k, (TP_P + k) % 2, v_hi[:, 4 * k:4 * k + 4, :])
            for n in range(NCH):
                for j in range(TPU):
                    split_hi(act, U_PG + n, j + AHEAD)
                group_ready(act, U_PG + n, TPU - 1)
                act.activation(pgate[:, n, :], acc[(G_PG + n) % 2][:, :], ACT.Sigmoid).then_inc(grp_free, 2)
            for tt in range(TT):
                act.wait_ge(sg["pg_sig"], 1)
                act.activation(pp[:, tt, :], h[:, tt, :], ACT.Square, accum_out=ssq[:, 2, tt:tt + 1])\
                    .then_inc(ssq_done, 1)
            act.wait_ge(var_done, 3)
            act.activation(rstd[:, 2, :], ssq[:, 2, :], ACT.Sqrt).then_inc(std_done, 1)

        @block.gpsimd
        def _(gp):
            done = [0]

            def link(ins):
                done[0] += 1
                ins.then_inc(pl, 1)
                gp.wait_ge(pl, done[0])

        @block.vector
        def _(v):
            done = [0]

            def link(ins):
                done[0] += 1
                ins.then_inc(dve, 1)
                v.wait_ge(dve, done[0])

            def inv_std(n, count):
                v.wait_ge(ssq_done, TT * (n + 1))
                v.tensor_scalar(ssq[:, n, :], ssq[:, n, :], 1.0 / count, EPS, ALU.mult, ALU.add).then_inc(var_done, 1)
                v.wait_ge(std_done, n + 1)
                v.reciprocal(rstd[:, n, :], rstd[:, n, :]).then_inc(rstd_done, 1)

            for k in range(KT):
                if k % 4 == 0:
                    v.wait_ge(x_hi, k // 4 + 1)
                i = v.scalar_tensor_tensor(out=u_lo[:, k, :], in0=xt[:, k, :], scalar=g_mix[:, k:k + 1],
                                           in1=u_hi[:, k, :].bitcast(F32), op0=ALU.mult, op1=ALU.subtract)
            i.then_inc(x_lo, 1)
            for j in range(AHEAD):
                split_lo(v, 0, j)
            inv_std(0, D)
            v.wait_ge(rstd_done, 1)
            for i in range(NZ):
                for j in range(TPU):
                    if i * TPU + j + AHEAD < NZ * TPU:
                        split_lo(v, i, j + AHEAD)
                group_ready(v, i, TPU - 1)
                width = C if i < NZ - 1 else ZLAST
                v.tensor_scalar(z[:, 1, i * C:i * C + width], acc[i % 2][:, C:C + width], rstd[:, 0, 1:2], None,
                                ALU.mult).then_inc(grp_free, 1)
            sm = lambda i: small[:, i, :]
            v.wait_ge(sg["s5_dt"], 1)
            v.tensor_tensor(sm(1), s5p[:, 0, :], sm(0), ALU.mult).then_inc(sg["s5_arg"], 1)
            link(v.tensor_tensor(sm(3), s5p[:, 1, :], sm(0), ALU.mult))
            magic = 1.5 * 2.0 ** 23
            link(v.tensor_scalar(sm(4), sm(3), 1.0 / (2 * math.pi), magic, ALU.mult, ALU.add))
            link(v.tensor_scalar(sm(4), sm(4), -magic, None, ALU.add))
            p1 = 6.28125
            p2 = math.floor((2 * math.pi - p1) * 2 ** 20) / 2 ** 20
            p3 = 2 * math.pi - p1 - p2
            src = 3
            for part in (p1, p2, p3):
                link(v.scalar_tensor_tensor(out=sm(5), in0=sm(4), scalar=-part, in1=sm(src), op0=ALU.mult, op1=ALU.add))
                src = 5
            top = float(np.nextafter(np.float32(math.pi), np.float32(0)))
            link(v.tensor_scalar(sm(6), sm(5), top, -top, ALU.min, ALU.max))
            link(v.tensor_scalar(sm(7), sm(6), -1.0, None, ALU.mult))
            link(v.tensor_tensor(sm(7), sm(6), sm(7), ALU.max))
            v.tensor_scalar(sm(7), sm(7), -1.0, math.pi / 2, ALU.mult, ALU.add).then_inc(sg["s5_th"], 1)
            v.wait_ge(sg["pool_hi"], 4)
            for g in range(4):
                i = v.scalar_tensor_tensor(out=o_lo[:, 8 + g, :], in0=aux[0][:, g * S:(g + 1) * S],
                                           scalar=pool_s[:, g:g + 1], in1=o_hi[:, 8 + g, :].bitcast(F32),
                                           op0=ALU.mult, op1=ALU.subtract)
            i.then_inc(sg["pool_lo"], 1)
            v.wait_ge(sg["cmp_tr"], 1)
            v.tensor_copy(kv_ct[:, :, :].rearrange("p g t -> p (g t)"), aux[1][:, 0:NG * S]).then_inc(sg["cmp_copied"], 1)
            v.wait_ge(sg["s5_sin"], 2)
            v.wait_ge(sg["s5_exp"], 1)
            link(v.tensor_tensor(sm(10), sm(2), sm(9), ALU.mult))
            link(v.tensor_scalar(sm(10), sm(10), -1.0, None, ALU.add))
            link(v.tensor_tensor(sm(11), sm(2), sm(8), ALU.mult))
            link(v.tensor_tensor(sm(12), s5p[:, 0, :], s5p[:, 0, :], ALU.mult))
            link(v.tensor_tensor(sm(13), s5p[:, 1, :], s5p[:, 1, :], ALU.mult))
            link(v.tensor_tensor(sm(14), sm(12), sm(13), ALU.add))
            link(v.reciprocal(sm(14), sm(14)))
            link(v.tensor_tensor(sm(12), sm(10), s5p[:, 0, :], ALU.mult))
            link(v.tensor_tensor(sm(13), sm(11), s5p[:, 1, :], ALU.mult))
            link(v.tensor_tensor(sm(12), sm(12), sm(13), ALU.add))
            link(v.tensor_tensor(sm(15), sm(12), sm(14), ALU.mult))
            link(v.tensor_tensor(sm(12), sm(11), s5p[:, 0, :], ALU.mult))
            link(v.tensor_tensor(sm(13), sm(10), s5p[:, 1, :], ALU.mult))
            link(v.tensor_tensor(sm(12), sm(12), sm(13), ALU.subtract))
            link(v.tensor_tensor(sm(16), sm(12), sm(14), ALU.mult))
            link(v.tensor_copy(sm(20), sm(9)))
            link(v.tensor_copy(sm(21), sm(8)))
            for k in range(6):
                c0, s0, c1, s1 = (20 + 2 * k + i for i in range(4))
                link(v.tensor_tensor(sm(12), sm(c0), sm(c0), ALU.mult))
                link(v.tensor_tensor(sm(13), sm(s0), sm(s0), ALU.mult))
                link(v.tensor_tensor(sm(c1), sm(12), sm(13), ALU.subtract))
                link(v.tensor_tensor(sm(12), sm(c0), sm(s0), ALU.mult))
                link(v.tensor_scalar(sm(s1), sm(12), 2.0, None, ALU.mult))
            v.wait_ge(sg["cmp_sum"], 1)
            v.wait_ge(sg["pool_lo"], 1)
            link(v.memset(kvc[:, :, :, :], 0.0))
            for g in range(NG):
                src = aux[1][:, C + g * NCMP:C + (g + 1) * NCMP].rearrange("p (o n) -> p o n", o=1)
                i = v.tensor_copy(kvc[:, g, :, 0:NCMP], src.to_broadcast([P, R, NCMP]))
            i.then_inc(sg["cmp_sb"], 1)
            v.wait_ge(sg["xg_tr"], 1)
            v.tensor_copy(xg[:, :, :].rearrange("p g e -> p (g e)"), aux[1][:, 0:NG * P])
            v.tensor_copy(xk[0:CP, :].rearrange("p (g e) -> p g e", g=NG),
                          aux[1][0:CP, 0:NG * P].rearrange("p (g e) -> p g e", g=NG)[:, :, 0:DH]).then_inc(sg["xg_sb"], 1)
            v.wait_ge(sg["kc_tr"], 1)
            v.tensor_copy(kc_t[:, :], aux[1][:, C:C + CP]).then_inc(sg["kc_sb"], 1)
            v.wait_ge(sg["cs_done"], 1)
            v.wait_ge(mask_in, 32)
            sc = aux[1][:, :].rearrange("p (g x) -> p g x", g=NG)[:, :, 0:TT * R * CP]\
                .rearrange("p g (t r n) -> p t g r n", t=TT, r=R)

            def bc_mask(which, tt):
                return cmask[:, which, tt:tt + 1, :].to_broadcast([P, NH, CP])

            for tt in range(TT):
                link(v.tensor_tensor(pc[:, tt, :, :].rearrange("p (g r) n -> p g r n", g=NG), sc[:, tt, :, :, :],
                                     bc_mask(0, tt).rearrange("p (g r) n -> p g r n", g=NG), ALU.add))
            link(v.tensor_reduce(cstat[:, 0, :, :], pc[:, :, :, :], AX_X, ALU.max))
            for tt in range(TT):
                i = v.tensor_tensor(pc[:, tt, :, :], pc[:, tt, :, :],
                                    cstat[:, 0, tt, :].rearrange("p (h o) -> p h o", o=1).to_broadcast([P, NH, CP]),
                                    ALU.subtract)
                link(i)
            v.sem_inc(sg["cs_sub"], 1)
            v.wait_ge(sg["cs_exp"], 1)
            for tt in range(TT):
                link(v.tensor_tensor(pc[:, tt, :, :], pc[:, tt, :, :], bc_mask(1, tt), ALU.mult))
            link(v.tensor_reduce(cstat[:, 1, :, :], pc[:, :, :, :], AX_X, ALU.add))
            link(v.tensor_scalar(cstat[:, 2, :, :], cstat[:, 1, :, :], 1e-30, None, ALU.max))
            link(v.reciprocal(cstat[:, 3, :, :], cstat[:, 2, :, :]))
            v.wait_ge(sg["ngate_done"], 1)
            link(v.tensor_tensor(cstat[:, 2, :, :], cstat[:, 3, :, :], ngate[:, :, 0:NH], ALU.mult))
            for tt in range(TT):
                i = v.tensor_tensor(pc[:, tt, :, :], pc[:, tt, :, :],
                                    cstat[:, 2, tt, :].rearrange("p (h o) -> p h o", o=1).to_broadcast([P, NH, CP]),
                                    ALU.mult)
                link(i)
            v.sem_inc(sg["pc_done"], 1)
            v.wait_ge(sg["pc_tr"], 1)
            v.tensor_copy(pc_t[:, :, :, :].rearrange("p g t q -> p (g t q)"), aux[1][:, 0:C]).then_inc(sg["pc_sb"], 1)
            for hd in range(NH):
                v.wait_ge(sg["sc_done"], hd + 1)
                s1 = aux[0][:, 0:C].rearrange("p (i k) -> p i k", i=2)
                s0 = aux[0][:, C:C + S].rearrange("p (i k) -> p i k", i=2)
                tri2 = tri[:, :].rearrange("p (o k) -> p o k", o=1).to_broadcast([P, 2, P])
                link(v.tensor_tensor(s1[:, :, P:S], s1[:, :, P:S], tri2, ALU.add))
                link(v.tensor_tensor(s0, s0, tri2, ALU.add))
                v.tensor_reduce(stat[:, hd, 0:2], s1, AX_X, ALU.max, negate=True)
                v.tensor_reduce(stat[:, hd, 2:4], s0, AX_X, ALU.max, negate=True).then_inc(sg["sc_max"], 1)
                v.wait_ge(sg["sc_exp"], 4 * hd + 4)
                link(v.reciprocal(stat[:, hd, 8:12], stat[:, hd, 4:8]))
                for n, tt in enumerate((1, 0)):
                    link(v.tensor_tensor(stat[:, hd, 12 + 2 * n:14 + 2 * n], stat[:, hd, 8 + 2 * n:10 + 2 * n],
                                         ngate[:, tt, NH + hd % 2 * R + hd // 2:3 * NH:NH], ALU.mult))
                for n, (o, w) in enumerate(((0, S), (S, S), (C, P), (C + P, P))):
                    i = v.tensor_scalar(prob[:, hd % 2, o:o + w], prob[:, hd % 2, o:o + w], stat[:, hd, 12 + n:13 + n],
                                        None, ALU.mult)
                i.then_inc(sg["sc_scaled"], 1)
                if hd % 4 == 3:
                    k = hd // 4 * 2
                    v.wait_ge(sg["nsa_hi"], hd // 4 + 1)
                    v.tensor_tensor(o_lo[:, k:k + 2, :].rearrange("p k t -> p (k t)"), aux[1][:, C:2 * C],
                                    o_hi[:, k:k + 2, :].rearrange("p k t -> p (k t)").bitcast(F32), ALU.subtract)\
                        .then_inc(sg["nsa_lo"], 1)
            v.wait_ge(ret_in, 32)
            pairs = lambda x: x.rearrange("p (h d) -> p h d", h=RH)
            for c0 in (RQ0, RK0):
                for tt in range(TT):
                    x = z[:, tt, c0:c0 + BW]
                    sw = x.rearrange("p (h i two) -> p h i two", h=RH, two=2)[:, :, :, ::-1]
                    sn = rot[:, 1, tt:tt + 1, :].to_broadcast([P, RH, P])
                    cs = rot[:, 0, tt:tt + 1, :].to_broadcast([P, RH, P])
                    link(v.tensor_tensor(rtmp[:, :].rearrange("p (h i two) -> p h i two", h=RH, two=2), sw,
                                         sn.rearrange("p h (i two) -> p h i two", two=2), ALU.mult))
                    link(v.tensor_tensor(pairs(x), pairs(x), cs, ALU.mult))
                    link(v.tensor_tensor(x, x, rtmp[:, :], ALU.add))
                    v.sem_inc(sg["rot_done"], 1)
            for hd in range(RH):
                v.wait_ge(sg["rs_done"], hd + 1)
                if hd >= 2:
                    v.wait_ge(sg["ry_done"], hd - 1)
                b = (hd % 2) * C
                v.tensor_tensor(rs_t[:, hd % 2, :], aux[0][:, b:b + 3 * P], decay[:, hd, :], ALU.mult)\
                    .then_inc(sg["rs_dec"], 1)
            v.wait_ge(sg["ry_ssq"], TT * RH)
            v.tensor_scalar(rstat[:, 0, :], rstat[:, 0, :], 1.0 / RD, EPS, ALU.mult, ALU.add).then_inc(sg["ry_var"], 1)
            v.wait_ge(sg["ry_std"], 1)
            link(v.reciprocal(rstat[:, 2, :], rstat[:, 1, :]))
            v.wait_ge(sg["rgate_done"], 1)
            for tt in range(TT):
                for hd in range(RH):
                    i = v.scalar_tensor_tensor(out=ry[:, tt, hd * P:(hd + 1) * P],
                                               in0=aux[1][:, tt * C + hd * P:tt * C + (hd + 1) * P],
                                               scalar=rstat[:, 2, tt * RH + hd:tt * RH + hd + 1],
                                               in1=rgate[:, tt, hd * P:(hd + 1) * P], op0=ALU.mult, op1=ALU.mult)
            i.then_inc(sg["ret_done"], 1)
            quad_lo(v, TP_RET, 1, o_lo[:, 12:16, :], o_hi[:, 12:16, :])
            v.wait_ge(tp_lo, TP_RET + 1)
            for q in range(4):
                pw = lambda i, n: small[:, i, 4 * q:4 * q + 4].rearrange("p (i o) -> p i o", o=1).to_broadcast([P, 4, n])
                link(v.memset(gr[:, :, 0:1], 1.0))
                link(v.memset(gi[:, :, 0:1], 0.0))
                n = 1
                for k in range(7):
                    c_, s_ = pw(20 + 2 * k, n), pw(21 + 2 * k, n)
                    link(v.tensor_tensor(t1[:, :, 0:n], gr[:, :, 0:n], c_, ALU.mult))
                    link(v.tensor_tensor(t2[:, :, 0:n], gi[:, :, 0:n], s_, ALU.mult))
                    link(v.tensor_tensor(gr[:, :, n:2 * n], t1[:, :, 0:n], t2[:, :, 0:n], ALU.subtract))
                    link(v.tensor_tensor(t1[:, :, 0:n], gr[:, :, 0:n], s_, ALU.mult))
                    link(v.tensor_tensor(t2[:, :, 0:n], gi[:, :, 0:n], c_, ALU.mult))
                    link(v.tensor_tensor(gi[:, :, n:2 * n], t1[:, :, 0:n], t2[:, :, 0:n], ALU.add))
                    n *= 2
                c_, s_ = pw(15, TH), pw(16, TH)
                A3 = lambda x: x[:, :, :]
                link(v.tensor_tensor(A3(t1), A3(gr), c_, ALU.mult))
                link(v.tensor_tensor(A3(t2), A3(gi), s_, ALU.mult))
                link(v.tensor_tensor(A3(fr), A3(t1), A3(t2), ALU.add))
                link(v.tensor_tensor(A3(t1), A3(gr), s_, ALU.mult))
                link(v.tensor_tensor(A3(t2), A3(gi), c_, ALU.mult))
                link(v.tensor_tensor(A3(fi), A3(t1), A3(t2), ALU.subtract))
                for hf in range(TT):
                    n = q * TT + hf
                    v.wait_ge(sg["bu_done"], 4 * (n + 1))
                    br = aux[0][:, 0:C].rearrange("p (i t) -> p i t", i=4)
                    bi = aux[0][:, C:2 * C].rearrange("p (i t) -> p i t", i=4)
                    if n:
                        v.wait_ge(sg["c_done"], n)
                    link(v.tensor_tensor(A3(t1), br, A3(fr), ALU.mult))
                    link(v.tensor_tensor(A3(t2), bi, A3(fi), ALU.mult))
                    link(v.tensor_tensor(A3(vr), A3(t1), A3(t2), ALU.subtract))
                    link(v.tensor_tensor(A3(t1), bi, A3(fr), ALU.mult))
                    link(v.tensor_tensor(A3(t2), br, A3(fi), ALU.mult))
                    v.sem_inc(sg["bu_used"], 1)
                    link(v.tensor_tensor(A3(vi), A3(t1), A3(t2), ALU.add))
                    for i in range(4):
                        r_ = small[:, 2, 4 * q + i:4 * q + i + 1].to_broadcast([P, TH])
                        for src, dst, st in ((vr, sr, 34), (vi, si, 35)):
                            init = 0.0 if hf == 0 else small[:, st, i:i + 1]
                            link(v.tensor_tensor_scan(dst[:, i, :], r_, src[:, i, :], init, ALU.mult, ALU.add))
                    link(v.tensor_tensor(A3(t1), A3(gr), A3(sr), ALU.mult))
                    link(v.tensor_tensor(A3(t2), A3(gi), A3(si), ALU.mult))
                    link(v.tensor_tensor(A3(vr), A3(t1), A3(t2), ALU.subtract))
                    link(v.tensor_tensor(A3(t1), A3(gr), A3(si), ALU.mult))
                    link(v.tensor_tensor(A3(t2), A3(gi), A3(sr), ALU.mult))
                    link(v.scalar_tensor_tensor(out=A3(vi), in0=A3(t1), scalar=-1.0, in1=A3(t2),
                                                op0=ALU.mult, op1=ALU.subtract))
                    v.sem_inc(sg["sh_done"], 1)
                    if hf == 0:
                        hr, hi_ = vr[:, :, TH - 1], vi[:, :, TH - 1]
                        c1, s1 = small[:, 20, 4 * q:4 * q + 4], small[:, 21, 4 * q:4 * q + 4]
                        a_, b_ = small[:, 36, 0:4], small[:, 37, 0:4]
                        link(v.tensor_tensor(a_, hr, c1, ALU.mult))
                        link(v.tensor_tensor(b_, hi_, s1, ALU.mult))
                        link(v.tensor_tensor(small[:, 34, 0:4], a_, b_, ALU.add))
                        link(v.tensor_tensor(a_, hr, s1, ALU.mult))
                        link(v.tensor_tensor(b_, hi_, c1, ALU.mult))
                        link(v.tensor_tensor(small[:, 35, 0:4], a_, b_, ALU.subtract))
                v.wait_ge(sg["c_done"], 2 * q + 2)
                v.wait_ge(sg["y5_lo"], q) if q else None
                v.scalar_tensor_tensor(out=y5[:, :], in0=u5_t[:, q, :], scalar=s5_d[:, q:q + 1],
                                       in1=aux[1][:, (q % 2) * C:(q % 2) * C + S], op0=ALU.mult, op1=ALU.add)\
                    .then_inc(sg["y5_done"], 1)
                v.wait_ge(sg["y5_hi"], q + 1)
                v.tensor_tensor(y_lo[:, q, :], y5[:, :], y_hi[:, q, :].bitcast(F32), ALU.subtract)\
                    .then_inc(sg["y5_lo"], 1)
            v.wait_ge(pt_hi, 1)
            v.tensor_tensor(p_lo[:, :, :], p_raw[:, :, :], p_hi[:, :, :].bitcast(F32), ALU.subtract).then_inc(pt_lo, 1)
            for j in range(AHEAD):
                split_lo(v, U_GP, j)
            for j in range(TPU):
                split_lo(v, U_GP, j + AHEAD)
                if j == 3:
                    v.wait_ge(sg["glu_sig"], 1)
                    link(v.tensor_tensor(glu_o, acc[G_GP % 2][:, :], glu_s, ALU.mult))
                    v.sem_inc(grp_free, 4)
                    v.sem_inc(sg["glu_done"], 1)
                if j >= 4:
                    group_ready(v, U_GP, j)
                    g = G_GP + j - 2
                    n = j - 4
                    v.tensor_copy(pp[:, :, n * C:(n + 1) * C], acc[g % 2][:, :].rearrange("p (t n) -> p t n", t=TT))\
                        .then_inc(grp_free, 2)
            quad_lo(v, TP_GLU, 0, o_lo[:, 4:8, :], o_hi[:, 4:8, :])
            for n in range(NCH):
                for b in range(4):
                    for j in range(TPU):
                        split_lo(v, U_MB + 5 * n + b, j + AHEAD)
                for j in range(TPU):
                    split_lo(v, U_MB + 5 * n + 4, j + AHEAD)
                    if j % 2 == 1:
                        b = j // 2
                        g = G_MB + 8 * n + 4 + b
                        group_ready(v, U_MB + 5 * n + 4, j)
                        if b == 0:
                            v.wait_ge(grp_free, 2 * (G_MB + 8 * n + 4))
                            if n:
                                v.wait_ge(tp_in, TP_M + n)
                            link(v.tensor_tensor(merged[:, :], acc[g % 2][:, :], gates[:, b, :], ALU.mult))
                            v.sem_inc(grp_free, 2)
                        else:
                            link(v.tensor_tensor(prodt[:, :], acc[g % 2][:, :], gates[:, b, :], ALU.mult))
                            v.sem_inc(grp_free, 2)
                            link(v.tensor_tensor(merged[:, :], merged[:, :], prodt[:, :], ALU.add))
                v.sem_inc(sg["merged_done"], 1)
                quad_lo(v, TP_M + n, (TP_M + n) % 2, m_lo[:, 4 * n:4 * n + 4, :], m_hi[:, 4 * n:4 * n + 4, :])
            for n in range(NCH):
                for j in range(TPU):
                    split_lo(v, U_WO + n, j + AHEAD)
                    if j == 5 and n:
                        quad_lo(v, TP_H + n - 1, (TP_H + n - 1) % 2, v_lo[:, 4 * n - 4:4 * n, :],
                                v_hi[:, 4 * n - 4:4 * n, :], g_mlp[:, 4 * n - 4:4 * n])
                group_ready(v, U_WO + n, TPU - 1)
                if n == 0:
                    v.wait_ge(h_in, 16)
                hc = h[:, :, n * C:(n + 1) * C]
                v.tensor_tensor(hc, acc[(G_WO + n) % 2][:, :].rearrange("p (t n) -> p t n", t=TT), hc, ALU.add)\
                    .then_inc(grp_free, 2)
            quad_lo(v, TP_H + 3, (TP_H + 3) % 2, v_lo[:, 12:16, :], v_hi[:, 12:16, :], g_mlp[:, 12:16])
            inv_std(1, D)
            with v.Fori(0, NFG) as g:
                for n in range(2 * NCH):
                    u = g * (2 * NCH) + (U_FF + n)
                    for j in range(TPU):
                        split_lo(v, u, j + AHEAD)
                        if j == 5 and 1 <= n <= NCH:
                            quad_lo(v, g * NCH + (TP_FF + n - 1), (TP_FF + n - 1) % 2, f_lo[:, 4 * n - 4:4 * n, :],
                                    f_hi[:, 4 * n - 4:4 * n, :])
                    if n < NCH:
                        v.wait_ge(grp_free, g * (4 * NCH) + 2 * (G_FF + n + 1))
                        rl = relu[n % 2]
                        v.tensor_tensor(rl[:, :], rl[:, :], rl[:, :], ALU.mult).then_inc(sg["sq_done"], 1)
                    else:
                        group_ready(v, u, TPU - 1)
                        c0 = (n - NCH) * C
                        hc = h[:, :, c0:c0 + C]
                        v.tensor_tensor(hc, acc[(G_FF + n) % 2][:, :].rearrange("p (t n) -> p t n", t=TT), hc,
                                        ALU.add).then_inc(grp_free, 2)
            for k in range(4):
                quad_lo(v, TP_P + k, (TP_P + k) % 2, v_lo[:, 4 * k:4 * k + 4, :], v_hi[:, 4 * k:4 * k + 4, :])
            for n in range(NCH):
                for j in range(TPU):
                    split_lo(v, U_PG + n, j + AHEAD)
                v.wait_ge(grp_free, 2 * (G_PG + n + 1))
                ga = pgate[:, n, :].rearrange("p (t n) -> p t n", t=TT)
                hc = h[:, :, n * C:(n + 1) * C]
                link(v.tensor_tensor(ga, ga, pp[:, :, n * C:(n + 1) * C], ALU.mult))
                link(v.tensor_tensor(hc, hc, ga, ALU.add))
            v.sem_inc(sg["pg_sig"], 1)
            inv_std(2, D)
            v.wait_ge(rstd_done, 3)
            v.wait_ge(fin_in, 16)
            for tt in range(TT):
                i = v.scalar_tensor_tensor(out=h[:, tt, :], in0=h[:, tt, :], scalar=rstd[:, 2, tt:tt + 1],
                                           in1=g_fin[:, :], op0=ALU.mult, op1=ALU.mult)
            i.then_inc(z_dve, 1)


def band_matrix():
    t = np.arange(S)
    out = np.zeros((S, 4, S), np.float32)
    for g, w in enumerate((2, 4, 8, 16)):
        inside = (t[None, :] >= t[:, None]) & (t[None, :] < t[:, None] + w)
        out[:, g] = inside / np.minimum(t + 1, w)[None, :] - (t[None, :] == t[:, None])
    return np.ascontiguousarray(out.reshape(TT, P, 4, S).transpose(1, 2, 0, 3))


def rotation():
    angle = np.repeat(1.0 / 10000.0 ** np.linspace(0.0, 1.0, RD // 2), 2)
    angle = np.arange(S)[:, None] * angle[None, :]
    sign = np.where(np.arange(RD) % 2 == 0, -1.0, 1.0)
    both = np.stack([np.cos(angle), np.sin(angle) * sign]).reshape(2, TT, P, RD)
    return np.ascontiguousarray(both.transpose(2, 0, 1, 3).astype(np.float32))


def decays():
    gamma = 1.0 - 2.0 ** (-5.0 - np.arange(RH))
    rel = np.arange(S)[None, :] - np.arange(P)[:, None]
    d = np.where(rel >= 0, gamma[:, None, None] ** np.maximum(rel, 0), 0.0) * RD ** -0.5
    d = np.concatenate([d, d[:, :, :P]], axis=2)
    return np.ascontiguousarray(d.transpose(1, 0, 2).astype(np.float32))


def compressed_mask():
    t, n = np.arange(S)[:, None], np.arange(CP)[None, :]
    seen = (n < NCMP) & (16 * n + 31 <= t)
    both = np.stack([np.where(seen, 0.0, NEG), seen.astype(np.float64)]).reshape(2, TT, P, CP)
    return np.ascontiguousarray(both.transpose(2, 0, 1, 3).astype(np.float32))


def kernel(x, p, g_mix, w_in, w_cmp_k, w_cmp_v, s5_a_re, s5_a_im, s5_log_dt, s5_b_re, s5_b_im,
           s5_c_re, s5_c_im, s5_d, s5_w_glu, pool_w, pool_scale, w_branch, w_out, g_mlp,
           w_mlp_up, w_mlp_down, w_ple_gate, w_ple_proj, g_final):
    import concourse.bacc as bacc
    from concourse.bass_utils import run_bass_kernel_spmd

    f32 = np.float32
    x, p = np.asarray(x), np.asarray(p)

    def by_partition(v):
        return np.ascontiguousarray(np.asarray(v).reshape(-1, P).T)

    def states(v):
        return np.asarray(v)[0].reshape(ST, P).T

    w_cmp = np.zeros((P, 32, P), f32)
    w_cmp[:DH, :, :DH] = np.asarray(w_cmp_k)[0].transpose(1, 0, 2)
    w_cmp[DH:, :, DH:] = np.asarray(w_cmp_v)[0].transpose(1, 0, 2)
    s5_b = np.zeros((4, 2, SC, 2, 4, 2, SN), f32)
    s5_c = np.zeros((2, SN, 2, ST, 2, SC), f32)
    for im, (b, c) in enumerate(((s5_b_re, s5_c_re), (s5_b_im, s5_c_im))):
        b = np.asarray(b)[0].reshape(4, 4, 2, SN, SC)
        c = np.asarray(c)[0].reshape(ST, 2, SC, SN)
        for j in range(2):
            s5_b[:, j, :, im, :, j, :] = b[:, :, j].transpose(1, 3, 0, 2)
            s5_c[j, :, im, :, j, :] = c[:, j].transpose(2, 0, 1)
    dt = np.broadcast_to(np.asarray(s5_log_dt)[0][:, None], (SG, SN)).reshape(ST, P).T
    causal = np.arange(P)[None, :] <= np.arange(P)[:, None]
    head_order = np.arange(NH * DH).reshape(NG, R, DH).transpose(1, 0, 2).ravel()
    pair_order = np.arange(2 * NG * DH).reshape(2, NG, DH).transpose(1, 0, 2).ravel()
    order = np.concatenate([Q0 + head_order, KV0 + pair_order, np.arange(KV0 + 2 * P, ZS)])
    w_in = np.asarray(w_in)[0]
    w_branch = np.asarray(w_branch)[0].reshape(D, D)
    w_branch = np.concatenate([w_branch[head_order], w_branch[BW:]])
    arrays = {
        "x": x[0], "xt": x[0].T, "pt": p[0, 0].T,
        "g_mix": by_partition(g_mix), "g_mlp": by_partition(g_mlp),
        "g_final": np.broadcast_to(np.asarray(g_final)[None, :], (P, D)),
        "w_in": w_in, "w_mix": w_in[:, order], "w_glu": np.asarray(s5_w_glu)[0], "w_pp": np.asarray(w_ple_proj)[0],
        "w_branch": w_branch, "w_out": np.asarray(w_out)[0],
        "w_up": np.asarray(w_mlp_up)[0], "w_down": np.asarray(w_mlp_down)[0], "w_pg": np.asarray(w_ple_gate)[0],
        "w_pool": np.asarray(pool_w)[0], "pool_scale": by_partition(pool_scale), "w_cmp": w_cmp,
        "s5p": np.stack([states(s5_a_re), states(s5_a_im), dt], axis=1),
        "s5_b": s5_b.reshape(P, 2, 4, P), "s5_c": s5_c.reshape(P, 2, ST, 32), "s5_d": by_partition(s5_d),
        "ident": np.eye(P, dtype=f32), "band": band_matrix(), "rot": rotation(), "decay": decays(),
        "cmask": compressed_mask(), "tri": np.where(causal, 0.0, NEG).astype(f32),
    }
    arrays = {f"in_{k}": np.ascontiguousarray(v) for k, v in arrays.items()}
    nc = bacc.Bacc("TRN2", target_bir_lowering=False, num_devices=1)
    aps = {k[3:]: nc.dram_tensor(k, v.shape, mybir.dt.from_np(v.dtype), kind="ExternalInput").ap()
           for k, v in arrays.items()}
    out = nc.dram_tensor("out", (S, D), F32, kind="ExternalOutput").ap()
    hybrid_layer(nc, aps, out)
    r = run_bass_kernel_spmd(nc, [arrays], core_ids=[0])
    return r.results[0]["out"].reshape(1, S, D)
```

```python
import math
from contextlib import ExitStack

import numpy as np

import concourse.bass as bass
from concourse import mybir

F32 = mybir.dt.float32
F32R = mybir.dt.float32r
ALU = mybir.AluOpType
ACT = mybir.ActivationFunctionType
AX_X = mybir.AxisListType.X

P = 128
D = 2048
S = 256
TT = S // P
KT = D // P
CW = 512
TK = 2
NCH = D // CW
TPU = KT // TK
BW = D // 4
NH, NG, DH = 8, 2, 64
R = NH // NG
NCMP = (S - 32) // 16 + 1
CP = 32
RH, RD = 4, 128
SG, SN, SC = 32, 64, 16
ST = SG * SN // P
TH = P
EPS = 1e-6
NEG = -1e30
FF = 4 * D
NFG = FF // D
PD = 256

Q0 = 0
KV0 = Q0 + NH * DH
NG0 = KV0 + 6 * NG * DH
S50 = NG0 + 3 * NH
PL0 = S50 + BW
RQ0 = PL0 + BW
RK0 = RQ0 + BW
RV0 = RK0 + BW
RG0 = RV0 + BW
ZS = RG0 + BW
NZ = -(-ZS // CW)
ZLAST = ZS - (NZ - 1) * CW

U_MG = NZ
U_GP = U_MG + 4 * NCH
U_BR = U_GP + 1
U_WO = U_BR + NCH
U_FF = U_WO + NCH
U_PG = U_FF + NFG * 2 * NCH
U_END = U_PG + NCH
TILES = U_END * TPU
T_MG = U_MG * TPU
G_MG = NZ
G_GP = G_MG + 4 * NCH
G_BR = G_GP + 2 + NCH
G_WO = G_BR + 4 * NCH
G_FF = G_WO + NCH
G_PG = G_FF + NFG * 2 * NCH
TP_RET, TP_GLU, TP_M = 0, 1, 2
TP_H = TP_M + NCH
TP_FF = TP_H + NCH
TP_P = TP_FF + NFG * NCH
RING = 4
AHEAD = RING - 1
LOADED = 7

A_BAND, A_POOL, A_QTR, A_KTR, A_CS, A_PCT = 2, 4, 7, 8, 9, 13
A_HEAD = [14 + 4 * i for i in range(NH)]
A_RTR = A_HEAD[-1] + 5
A_RS = [A_RTR + 2 + i for i in range(RH)]
A_U5 = A_RS[-1] + 2
A_RQUAD = A_U5 + 2
A_S5 = [A_RQUAD + 1 + 15 * i for i in range(4)]
A_END = 4 * NCH * TPU


def hybrid_layer(nc, a, out):
    ctx = ExitStack()
    with ctx:
        offset = [-(-nc.sbuf_base // 32) * 32]
        names = [0]

        def at(off, shape, dt=F32):
            names[0] += 1
            return nc.alloc_sbuf_tensor_at(f"sb{names[0]}", [P, *shape], dt, offset=off).ap()

        def size(shape):
            return 4 * int(np.prod(shape))

        class Region:

            def __init__(self, off, nbytes):
                self.off, self.end = off, off + nbytes

            def __call__(self, *shape, dt=F32):
                off, self.off = self.off, -(-(self.off + size(shape)) // 32) * 32
                assert self.off <= self.end, (self.off, self.end)
                return at(off, shape, dt)

        def region(nbytes):
            off = offset[0]
            offset[0] += nbytes
            return off, nbytes

        KB = 1024
        always = Region(*region(54 * KB))
        ra = region(32 * KB)
        rb = region(32 * KB)
        rc = region(ZS * 2 * 4)
        rd = region(nc.sbuf_top - offset[0] - 32)

        raw = always(RING, TK * CW)
        whi = always(RING, TK * CW, dt=F32R)
        wlo = always(RING, TK * CW, dt=F32R)
        ident = always(P)
        g_mix = always(KT)
        g_mlp = always(KT)
        s5_d = always(4)
        rstd = always(3, TT)
        ssq = always(3, TT)
        p_raw = always(TK, S)
        s5p = always(3, ST)
        small = always(40, ST)

        r = Region(*ra)
        u_hi, u_lo = r(KT, S, dt=F32R), r(KT, S, dt=F32R)
        r = Region(*ra)
        v_hi, v_lo = r(KT, S, dt=F32R), r(KT, S, dt=F32R)
        r = Region(*rb)
        o_hi, o_lo = r(KT, S, dt=F32R), r(KT, S, dt=F32R)
        r = Region(*rb)
        f_hi, f_lo = r(KT, S, dt=F32R), r(KT, S, dt=F32R)
        r = Region(*rc)
        z = r(TT, ZS)
        r = Region(*rc)
        m_hi, m_lo = r(KT, S, dt=F32R), r(KT, S, dt=F32R)
        r = Region(*rd)
        xin = r(TT, D)
        xt = r(KT, S)
        xsq = r(TT, D)
        r = Region(*rd)
        y_hi, y_lo = r(4, S, dt=F32R), r(4, S, dt=F32R)
        p_hi, p_lo = r(TK, S, dt=F32R), r(TK, S, dt=F32R)
        s5_b = r(2, 4, P)
        s5_c = r(2, ST, 32)
        gstage = r(2, TT * CW)
        mix_at, mix_end = r.off, rd[0] + rd[1]
        m = Region(rd[0], 20 * KB)
        w_cmp = m(32, P)
        kv_ct = m(NG, S)
        m = Region(rd[0], 8 * KB)
        rot = m(2, TT, P)
        rtmp = m(BW)
        m = Region(mix_at, mix_end - mix_at)
        band = m(4, 2, S)
        w_pool = m(4, P)
        pool_s = m(4)
        pool_t = m(4, S)
        m = Region(mix_at, mix_end - mix_at)
        q_t = m(4, S)
        k_t = m(2, S)
        kvc = m(NG, R, CP)
        xg = m(NG, P)
        xk = m(P)
        kc_t = m(CP)
        pc = m(TT, NH, CP)
        pc_t = m(NG, TT, P)
        ngate = m(TT, 3 * NH)
        cmask = m(2, TT, CP)
        tri = m(P)
        prob = m(2, 6 * P)
        prob_t = m(2, 6 * P)
        stat = m(NH, 16)
        cstat = m(4, TT, NH)
        m = Region(mix_at, mix_end - mix_at)
        decay = m(RH, 3 * P)
        rq_t = m(RH, S)
        rk_t = m(RH, S)
        rs_t = m(2, 3 * P)
        rgate = m(TT, BW)
        ry = m(TT, BW)
        rjunk = m(P)
        rstat = m(3, TT * RH)
        m = Region(mix_at, mix_end - mix_at)
        u5_t = m(4, S)
        gr, gi, fr, fi = m(4, TH), m(4, TH), m(4, TH), m(4, TH)
        vr, vi, t1, t2 = m(4, TH), m(4, TH), m(4, TH), m(4, TH)
        sr, si = m(4, TH), m(4, TH)
        y5 = m(S)
        r = Region(*rd)
        scratch = r(3, TT * CW)
        prodt, merged = scratch[:, 0, :], scratch[:, 1, :]
        relu = [scratch[:, 1, :], scratch[:, 2, :]]
        junk = at(rd[0], [D])
        pp = r(TT, D)
        gates_off = r.off
        gates = r(4, TT * CW)
        glu_s, glu_o = r(TT * CW), r(TT * CW)
        h = at(gates_off, [TT, D])
        pgate = at(rb[0], [4, TT * CW])
        g_fin = at(rc[0], [D])

        psum = [ctx.enter_context(nc.psum_tensor(f"ps{i}", [P, 2 * CW], F32)) for i in range(4)]
        acc = psum[:2]
        aux = psum[2:]

        def sem(name):
            return ctx.enter_context(nc.semaphore(name))

        raw_in = [sem(f"raw_in{i}") for i in range(RING)]
        hi_done = sem("hi_done")
        lo_done = sem("lo_done")
        tile_used = sem("tile_used")
        grp_free = sem("grp_free")
        tp_in = sem("tp_in")
        tp_hi = sem("tp_hi")
        tp_lo = sem("tp_lo")
        x_in = sem("x_in")
        xt_in = [sem(f"xt_in{i}") for i in range(4)]
        x_lo = sem("x_lo")
        x_hi = sem("x_hi")
        p_in = sem("p_in")
        const_in = sem("const_in")
        pool_in = sem("pool_in")
        cmp_in = sem("cmp_in")
        mask_in = sem("mask_in")
        ret_in = sem("ret_in")
        h_in = sem("h_in")
        fin_in = sem("fin_in")
        s5_in = sem("s5_in")
        rot_in = sem("rot_in")
        gate_out = [sem(f"gate_out{i}") for i in range(2)]
        gate_in = [sem(f"gate_in{i}") for i in range(4)]
        gate_used = sem("gate_used")
        out_sem = sem("out_stored")
        ssq_done = sem("ssq_done")
        var_done = sem("var_done")
        std_done = sem("std_done")
        rstd_done = sem("rstd_done")
        pt_in = sem("pt_in")
        pt_hi = sem("pt_hi")
        pt_lo = sem("pt_lo")
        dve = sem("dve_step")
        pl = sem("pool_step")
        z_dve = sem("z_dve")
        sg = {n: sem(n) for n in (
            "pool_band pool_copied pool_mixed pool_hi pool_lo "
            "cmp_tr cmp_copied cmp_sum cmp_sb xg_tr xg_sb kc_tr kc_sb q_tr q_sb k_tr k_sb "
            "ngate_done cs_done cs_sub cs_exp pc_done pc_tr pc_sb "
            "sc_done sc_max sc_exp sc_scaled pt_tr pt_sb pv_done nsa_hi nsa_lo "
            "rot_done rq_tr rq_sb rk_tr rk_sb rs_done rs_dec ry_done ry_ssq ry_var ry_std rgate_done ret_done "
            "s5_dt s5_arg s5_exp s5_th s5_sin tab_done u5_tr u5_sb bu_done bu_used sh_done c_done y5_done y5_gelu y5_hi y5_lo "
            "glu_sig glu_done relu_done sq_done pg_sig merged_done br_tmp").split()}

        C = CW

        def tile_source(t_unit, kind, i, j):
            rows = slice(j * TK * P, (j + 1) * TK * P)
            return {
                "z": lambda: a["w_in"][rows, bass.ds(i * C, C)] if not isinstance(i, int)
                else a["w_in"][rows, i * C:(i + 1) * C],
            }[kind]().rearrange("(k p) n -> p k n", p=P)

        def cols(w, r0, c0, width=C):
            rows = slice(r0, r0 + TK * P) if isinstance(r0, int) else bass.ds(r0, TK * P)
            cs = slice(c0, c0 + width) if isinstance(c0, int) else bass.ds(c0, width)
            return w[rows, cs].rearrange("(k p) n -> p k n", p=P)

        def load_tile(sp, u, j, src, width=C):
            if not isinstance(u, int) or u * TPU + j >= RING:
                sp.wait_ge(lo_done, u * TPU + (j - RING + 1))
            s = j % RING
            sp.dma_start(raw[:, s, :].rearrange("p (k n) -> p k n", k=TK)[:, :, 0:width], src)\
                .then_inc(raw_in[s], 16)

        def split_hi(act, u, j):
            if isinstance(u, int) and u * TPU + j >= TILES:
                return
            act.wait_ge(raw_in[j % RING], u * (16 * TPU // RING) + 16 * (j // RING + 1))
            if not isinstance(u, int) or u * TPU + j >= RING:
                act.wait_ge(tile_used, u * TPU + (j - RING + 1))
            act.activation(whi[:, j % RING, :], raw[:, j % RING, :], ACT.Copy).then_inc(hi_done, 1)

        def split_lo(eng, u, j):
            if isinstance(u, int) and u * TPU + j >= TILES:
                return
            eng.wait_ge(hi_done, u * TPU + (j + 1))
            eng.tensor_tensor(wlo[:, j % RING, :], raw[:, j % RING, :], whi[:, j % RING, :].bitcast(F32),
                              ALU.subtract).then_inc(lo_done, 1)

        def products(pe, u, j, g, par, x_hi, x_lo, kt, first, last, width=C):
            if first:
                if not isinstance(g, int) or g >= 2:
                    pe.wait_ge(grp_free, 2 * g - 2)
            pe.wait_ge(lo_done, u * TPU + (j + 1))
            s = j % RING
            for k in range(TK):
                w_h = whi[:, s, k * C:k * C + width]
                w_l = wlo[:, s, k * C:k * C + width]
                for tt in range(TT):
                    o = acc[par][:, tt * C:tt * C + width]
                    xh = x_hi[:, kt + k, tt * P:(tt + 1) * P]
                    xl = x_lo[:, kt + k, tt * P:(tt + 1) * P]
                    pe.matmul(o, xh, w_h, start=first and k == 0, stop=False)
                    pe.matmul(o, xh, w_l, start=False, stop=False)
                    mm = pe.matmul(o, xl, w_h, start=False, stop=last and k == TK - 1)
            mm.then_inc(tile_used, 1)

        def group_ready(eng, u, j):
            eng.wait_ge(tile_used, u * TPU + (j + 1))

        def quad_in(pe, n, par, src):
            if not isinstance(n, int) or n >= 2:
                pe.wait_ge(tp_lo, n - 1)
            for k in range(4):
                for tt in range(TT):
                    mm = pe.transpose(aux[par][:, k * S + tt * P:k * S + (tt + 1) * P], src(k, tt), ident[:, :])
            mm.then_inc(tp_in, 1)

        def quad_hi(act, n, par, dst, scale=None):
            act.wait_ge(tp_in, n + 1)
            if scale is None:
                act.activation(dst.rearrange("p k t -> p (k t)"), aux[par][:, :], ACT.Copy).then_inc(tp_hi, 1)
                return
            for k in range(4):
                i = act.activation(dst[:, k, :], aux[par][:, k * S:(k + 1) * S], ACT.Copy, scale=scale[:, k:k + 1])
            i.then_inc(tp_hi, 1)

        def quad_lo(v, n, par, dst, hi, scale=None):
            v.wait_ge(tp_hi, n + 1)
            if scale is None:
                v.tensor_tensor(dst.rearrange("p k t -> p (k t)"), aux[par][:, :],
                                hi.rearrange("p k t -> p (k t)").bitcast(F32), ALU.subtract).then_inc(tp_lo, 1)
                return
            for k in range(4):
                i = v.scalar_tensor_tensor(out=dst[:, k, :], in0=aux[par][:, k * S:(k + 1) * S],
                                           scalar=scale[:, k:k + 1], in1=hi[:, k, :].bitcast(F32),
                                           op0=ALU.mult, op1=ALU.subtract)
            i.then_inc(tp_lo, 1)

        def features(x, tt, k):
            return x[:, tt, k * P:(k + 1) * P]

        def interleaved(step):
            at_tile = [0]

            def until(n):
                while at_tile[0] < min(n, A_END):
                    step(at_tile[0])
                    at_tile[0] += 1
            return until

        gate_mem = nc.dram_tensor("gate_mem", (4 * NCH, P, TT * CW), F32, kind="Internal").ap()
        block = ctx.enter_context(nc.Block())

        @block.sync
        def _(sp):
            sp.dma_start(ident[:, :], a["ident"]).then_inc(const_in, 16)
            sp.dma_start(g_mix[:, :], a["g_mix"]).then_inc(const_in, 16)
            sp.dma_start(g_mlp[:, :], a["g_mlp"]).then_inc(const_in, 16)
            sp.dma_start(s5p[:, :, :], a["s5p"]).then_inc(const_in, 16)
            sp.dma_start(s5_d[:, :], a["s5_d"]).then_inc(const_in, 16)
            for i in range(4):
                sp.dma_start(xt[:, 4 * i:4 * i + 4, :], a["xt"][4 * i * P:4 * (i + 1) * P, :]
                             .rearrange("(k p) t -> p k t", p=P)).then_inc(xt_in[i], 16)
            for i in range(NZ):
                width = C if i < NZ - 1 else ZLAST
                for j in range(TPU):
                    load_tile(sp, i, j, cols(a["w_mix"], j * TK * P, i * C, width), width)
                    if i == 0 and j == 3:
                        sp.dma_start(xin[:, :, :], a["x"].rearrange("(t p) d -> p t d", p=P)).then_inc(x_in, 16)
                        sp.dma_start(p_raw[:, :, :], a["pt"].rearrange("(k p) t -> p k t", p=P)).then_inc(p_in, 16)
            sp.wait_ge(x_lo, 8)
            sp.wait_ge(ssq_done, TT)
            sp.dma_start(band[:, :, :, :], a["band"]).then_inc(pool_in, 16)
            sp.dma_start(w_pool[:, :, :], a["w_pool"].rearrange("g c d -> c g d")).then_inc(pool_in, 16)
            sp.dma_start(pool_s[:, :], a["pool_scale"]).then_inc(pool_in, 16)
            sp.dma_start(w_cmp[:, :, :], a["w_cmp"]).then_inc(cmp_in, 16)

            def gate_tile(t):
                i, j = t // TPU, t % TPU
                load_tile(sp, U_MG + i, j, cols(a["w_in"], j * TK * P, ZS + (i % 4) * D + (i // 4) * C))
                if j == LOADED and i:
                    gate_store(i - 1)

            def gate_store(i):
                sp.wait_ge(grp_free, 2 * (G_MG + i + 1))
                sp.dma_start(gate_mem[i], gstage[:, i % 2, :]).then_inc(gate_out[i % 2], 16)

            until = interleaved(gate_tile)
            until(A_QTR + LOADED)
            sp.wait_ge(sg["pool_lo"], 1)
            sp.wait_ge(sg["cmp_sum"], 1)
            sp.dma_start(cmask[:, :, :, :], a["cmask"]).then_inc(mask_in, 16)
            sp.dma_start(tri[:, :], a["tri"]).then_inc(mask_in, 16)
            sp.dma_start(rot[:, :, :, :], a["rot"]).then_inc(rot_in, 16)
            sp.dma_start(s5_b[:, :, :, :], a["s5_b"]).then_inc(s5_in, 16)
            sp.dma_start(s5_c[:, :, :, :], a["s5_c"]).then_inc(s5_in, 16)
            until(A_RTR + LOADED - 2)
            sp.wait_ge(sg["nsa_lo"], 2)
            sp.dma_start(decay[:, :, :], a["decay"]).then_inc(ret_in, 16)
            until(A_END)
            for j in range(TPU):
                if j < 4:
                    src = cols(a["w_glu"], (j % 2) * TK * P, (j // 2) * C)
                else:
                    src = cols(a["w_pp"], 0, (j - 4) * C)
                load_tile(sp, U_GP, j, src)
            gate_store(4 * NCH - 1)

            def gate_load(n, b):
                sp.dma_start(gates[:, b, :], gate_mem[4 * n + b]).then_inc(gate_in[b], 16)

            for i in range(2):
                sp.wait_ge(gate_out[i], 16 * 2 * NCH)
            sp.wait_ge(sg["y5_lo"], 4)
            for b in range(4):
                gate_load(0, b)
            for n in range(NCH):
                for j in range(TPU):
                    load_tile(sp, U_BR + n, j, cols(a["w_branch"], j * TK * P, n * C))
                    if n and j % 2 == 0:
                        sp.wait_ge(gate_used, 4 * (n - 1) + j // 2 + 1)
                        gate_load(n, j // 2)
            for n in range(NCH):
                for j in range(TPU):
                    load_tile(sp, U_WO + n, j, cols(a["w_out"], j * TK * P, n * C))
                if n == 0:
                    sp.wait_ge(sg["merged_done"], NCH)
                    sp.dma_start(h[:, :, :], a["x"].rearrange("(t p) d -> p t d", p=P)).then_inc(h_in, 16)
            with sp.Fori(0, NFG) as g:
                for n in range(NCH):
                    for j in range(TPU):
                        load_tile(sp, g * (2 * NCH) + (U_FF + n), j, cols(a["w_up"], j * TK * P, g * D + n * C))
                for n in range(NCH):
                    for j in range(TPU):
                        load_tile(sp, g * (2 * NCH) + (U_FF + NCH + n), j,
                                  cols(a["w_down"], g * D + j * TK * P, n * C))
            sp.dma_start(g_fin[:, :], a["g_final"]).then_inc(fin_in, 16)
            for n in range(NCH):
                for j in range(TPU):
                    load_tile(sp, U_PG + n, j, cols(a["w_pg"], j * TK * P, n * C))
            sp.wait_ge(z_dve, 1)
            sp.dma_start(out.rearrange("(t p) d -> p t d", p=P), h[:, :, :]).then_inc(out_sem, 16)
            sp.wait_ge(out_sem, 16)

        @block.tensor
        def _(pe):
            pe.wait_ge(const_in, 80)
            for i in range(NZ):
                width = C if i < NZ - 1 else ZLAST
                for j in range(TPU):
                    if i == 0:
                        pe.wait_ge(x_lo, j + 1)
                    products(pe, i, j, i, i % 2, u_hi, u_lo, j * TK, j == 0, j == TPU - 1, width)

            def hidden_in(k):
                pe.wait_ge(grp_free, 2 * (G_WO + k + 1))
                quad_in(pe, TP_H + k, (TP_H + k) % 2, lambda kk, tt: features(h, tt, 4 * k + kk))

            def last_in(k):
                pe.wait_ge(grp_free, 2 * (G_PG - NCH + k + 1))
                quad_in(pe, TP_P + k, (TP_P + k) % 2, lambda kk, tt: features(h, tt, 4 * k + kk))

            def gate_tile(t):
                i, j = t // TPU, t % TPU
                products(pe, U_MG + i, j, G_MG + i, (G_MG + i) % 2, u_hi, u_lo, j * TK, j == 0, j == TPU - 1)

            until = interleaved(gate_tile)
            until(A_BAND)
            pe.wait_ge(grp_free, 2 * NZ)
            pe.wait_ge(pool_in, 48)
            for g in range(4):
                pe.matmul(aux[0][:, g * S:(g + 1) * S], z[:, 0, PL0 + g * P:PL0 + (g + 1) * P],
                          band[:, g, 0, :], start=True, stop=False)
                mm = pe.matmul(aux[0][:, g * S + P:(g + 1) * S], z[:, 1, PL0 + g * P:PL0 + (g + 1) * P],
                               band[:, g, 1, P:S], start=False, stop=True)
            mm.then_inc(sg["pool_band"], 1)
            for g in range(NG):
                for tt in range(TT):
                    mm = pe.transpose(aux[1][:, g * S + tt * P:g * S + (tt + 1) * P],
                                      z[:, tt, KV0 + g * P:KV0 + (g + 1) * P], ident[:, :])
            mm.then_inc(sg["cmp_tr"], 1)
            until(A_POOL)
            pe.wait_ge(sg["pool_copied"], 1)
            for g in range(4):
                mm = pe.matmul(aux[0][:, g * S:(g + 1) * S], w_pool[:, g, :], pool_t[:, g, :], start=True, stop=True)
            mm.then_inc(sg["pool_mixed"], 1)
            pe.wait_ge(cmp_in, 16)
            pe.wait_ge(sg["cmp_copied"], 1)
            o = aux[1][:, C:C + NG * NCMP].rearrange("p (g n) -> p g n", g=NG)
            for l in range(32):
                mm = pe.matmul(o, w_cmp[:, l, :], kv_ct[:, :, l:l + 16 * (NCMP - 1) + 1:16],
                               start=l == 0, stop=l == 31)
            mm.then_inc(sg["cmp_sum"], 1)
            until(A_QTR)
            pe.wait_ge(sg["pool_lo"], 1)
            for k in range(4):
                for tt in range(TT):
                    mm = pe.transpose(aux[0][:, k * S + tt * P:k * S + (tt + 1) * P],
                                      z[:, tt, Q0 + k * P:Q0 + (k + 1) * P], ident[:, :])
            mm.then_inc(sg["q_tr"], 1)
            pe.wait_ge(sg["cmp_sb"], 1)
            for g in range(NG):
                mm = pe.transpose(aux[1][:, g * P:(g + 1) * P], kvc[:, g, :, :], ident[:, :])
            mm.then_inc(sg["xg_tr"], 1)
            until(A_KTR)
            pe.wait_ge(sg["xg_sb"], 1)
            pe.transpose(aux[1][:, C:C + CP], xk[0:CP, :], ident[0:CP, 0:CP]).then_inc(sg["kc_tr"], 1)
            pe.wait_ge(sg["q_sb"], 1)
            for i in range(2):
                c0 = KV0 + (2 + 2 * i) * P
                for tt in range(TT):
                    o = i * S + tt * P
                    mm = pe.transpose(aux[0][:, o:o + P], z[:, tt, c0:c0 + P], ident[:, :])
            mm.then_inc(sg["k_tr"], 1)
            until(A_CS)
            pe.wait_ge(sg["kc_sb"], 1)
            for g in range(NG):
                for tt in range(TT):
                    for rr in range(R):
                        o = g * C + (tt * R + rr) * CP
                        mm = pe.matmul(aux[1][:, o:o + CP], q_t[g * DH:(g + 1) * DH, rr, tt * P:(tt + 1) * P],
                                       kc_t[g * DH:(g + 1) * DH, :], start=True, stop=True)
            mm.then_inc(sg["cs_done"], 1)
            pe.wait_ge(sg["k_sb"], 1)

            def scores(hd):
                lo = DH * (hd % 2)
                if hd >= 1:
                    pe.wait_ge(sg["sc_exp"], 4 * hd)
                for tt in (1, 0):
                    for i in range(2):
                        n = (tt + 1) * P
                        o = (0 if tt else C) + i * n
                        mm = pe.matmul(aux[0][:, o:o + n], q_t[lo:lo + DH, hd // 2, tt * P:(tt + 1) * P],
                                       k_t[lo:lo + DH, i, 0:n], start=True, stop=True)
                mm.then_inc(sg["sc_done"], 1)

            scores(0)
            until(A_PCT)
            pe.wait_ge(sg["pc_done"], 1)
            for g in range(NG):
                for tt in range(TT):
                    o = (g * TT + tt) * P
                    mm = pe.transpose(aux[1][:, o:o + P], pc[:, tt, g * R:(g + 1) * R, :], ident[:, :])
            mm.then_inc(sg["pc_tr"], 1)
            pe.wait_ge(sg["pc_sb"], 1)
            for hd in range(NH):
                until(A_HEAD[hd] + 3)
                pe.wait_ge(sg["sc_scaled"], hd + 1)
                if hd >= 1:
                    pe.wait_ge(sg["pt_sb"], 2 * hd)
                blocks = [(i, b) for i in range(2) for b in range(3)]
                for n, (i, b) in enumerate(blocks):
                    src = prob[:, hd % 2, :]
                    s0 = 4 * P + i * P if b == 0 else i * 2 * P + (b - 1) * P
                    o = aux[1][:, n * P:(n + 1) * P] if n < 4 else aux[0][:, C + 2 * P + (n - 4) * P:C + 2 * P + (n - 3) * P]
                    mm = pe.transpose(o, src[:, s0:s0 + P], ident[:, :])
                mm.then_inc(sg["pt_tr"], 1)
                until(A_HEAD[hd] + 4)
                pe.wait_ge(sg["pt_sb"], 2 * hd + 2)
                if hd + 1 < NH:
                    scores(hd + 1)
                lo = DH * (hd % 2)
                g = hd % 2
                if hd == 4:
                    pe.wait_ge(sg["nsa_lo"], 1)
                o = aux[1][lo:lo + DH, C + (hd // 2 % 2) * S:C + (hd // 2 % 2 + 1) * S]
                first = True
                for i in range(2):
                    v0 = KV0 + (3 + 2 * i) * P + g * DH
                    for kt in range(2):
                        b = prob_t[:, hd % 2, (3 * i + 2 * kt) * P:(3 * i + 2 + kt) * P]
                        pe.matmul(o[:, kt * P:S], z[:, kt, v0:v0 + DH], b, start=first, stop=False)
                        first = False
                rr = hd // 2
                pe.matmul(o, xg[rr * CP:(rr + 1) * CP, g, DH:P], pc_t[rr * CP:(rr + 1) * CP, g, :, :],
                          start=False, stop=True).then_inc(sg["pv_done"], 1)
            until(A_RTR)
            pe.wait_ge(sg["nsa_lo"], 2)
            pe.wait_ge(sg["rot_done"], 4)
            for k in range(4):
                for tt in range(TT):
                    mm = pe.transpose(aux[0][:, k * S + tt * P:k * S + (tt + 1) * P],
                                      z[:, tt, RQ0 + k * P:RQ0 + (k + 1) * P], ident[:, :])
            mm.then_inc(sg["rq_tr"], 1)
            for k in range(4):
                for tt in range(TT):
                    mm = pe.transpose(aux[1][:, k * S + tt * P:k * S + (tt + 1) * P],
                                      z[:, tt, RK0 + k * P:RK0 + (k + 1) * P], ident[:, :])
            mm.then_inc(sg["rk_tr"], 1)
            pe.wait_ge(sg["rq_sb"], 1)
            pe.wait_ge(sg["rk_sb"], 1)

            def ret_scores(hd):
                if hd >= 2:
                    pe.wait_ge(sg["rs_dec"], hd - 1)
                b = (hd % 2) * C
                pe.matmul(aux[0][:, b:b + S], rk_t[:, hd, 0:P], rq_t[:, hd, :], start=True, stop=True)
                pe.matmul(aux[0][:, b + S:b + 3 * P], rk_t[:, hd, P:S], rq_t[:, hd, P:S],
                          start=True, stop=True).then_inc(sg["rs_done"], 1)

            until(A_RS[0])
            ret_scores(0)
            for hd in range(RH):
                if hd + 1 < RH:
                    ret_scores(hd + 1)
                until(A_RS[hd] + 1)
                pe.wait_ge(sg["rs_dec"], hd + 1)
                if hd:
                    pe.wait_ge(sg["ry_ssq"], TT * hd)
                s_ = rs_t[:, hd % 2, :]
                v = lambda tt: z[:, tt, RV0 + hd * P:RV0 + (hd + 1) * P]
                pe.matmul(aux[1][:, hd * P:(hd + 1) * P], s_[:, 0:P], v(0), start=True, stop=True)
                pe.matmul(aux[1][:, C + hd * P:C + (hd + 1) * P], s_[:, P:2 * P], v(0), start=True, stop=False)
                pe.matmul(aux[1][:, C + hd * P:C + (hd + 1) * P], s_[:, 2 * P:3 * P], v(1),
                          start=False, stop=True).then_inc(sg["ry_done"], 1)
            until(A_U5)
            for k in range(4):
                for tt in range(TT):
                    mm = pe.transpose(aux[0][:, k * S + tt * P:k * S + (tt + 1) * P],
                                      z[:, tt, S50 + k * P:S50 + (k + 1) * P], ident[:, :])
            mm.then_inc(sg["u5_tr"], 1)
            until(A_RQUAD)
            pe.wait_ge(sg["ret_done"], 1)
            quad_in(pe, TP_RET, 1, lambda k, tt: features(ry, tt, k))
            pe.wait_ge(tp_lo, TP_RET + 1)
            pe.wait_ge(sg["u5_sb"], 1)
            pe.wait_ge(s5_in, 32)
            def s5_inputs(n):
                q, hf = n // TT, n % TT
                if n:
                    pe.wait_ge(sg["bu_used"], n)
                for i in range(4):
                    if n or i:
                        pe.wait_ge(sg["bu_done"], 4 * n + i)
                    for im in range(2):
                        o = im * C + i * P
                        mm = pe.matmul(aux[0][:, o:o + P], s5_b[32 * i:32 * i + 32, im, q, :],
                                       u5_t[32 * i:32 * i + 32, q, hf * P:(hf + 1) * P], start=True, stop=True)
                    mm.then_inc(sg["bu_done"], 1)

            def s5_outputs(n):
                q, hf = n // TT, n % TT
                if hf == 0 and q >= 2:
                    pe.wait_ge(sg["y5_done"], q - 1)
                pe.wait_ge(sg["sh_done"], n + 1)
                for i in range(4):
                    o = aux[1][32 * i:32 * i + 32, (q % 2) * C + hf * P:(q % 2) * C + (hf + 1) * P]
                    pe.matmul(o, s5_c[:, 0, 4 * q + i, :], vr[:, i, :], start=True, stop=False)
                    mm = pe.matmul(o, s5_c[:, 1, 4 * q + i, :], vi[:, i, :], start=False, stop=True)
                mm.then_inc(sg["c_done"], 1)

            s5_inputs(0)
            for n in range(4 * TT):
                until(A_S5[n // TT] + 7 + 5 * (n % TT))
                if n + 1 < 4 * TT:
                    s5_inputs(n + 1)
                until(A_S5[n // TT] + 9 + 5 * (n % TT))
                s5_outputs(n)
            until(A_END)
            pe.wait_ge(sg["y5_lo"], 4)
            pe.wait_ge(pt_lo, 1)
            for j in range(TPU):
                if j < 4:
                    products(pe, U_GP, j, G_GP + j // 2, (G_GP + j // 2) % 2, y_hi, y_lo, (j % 2) * TK,
                             j % 2 == 0, j % 2 == 1)
                else:
                    products(pe, U_GP, j, G_GP + j - 2, (G_GP + j - 2) % 2, p_hi, p_lo, 0, True, True)
                if j == 6:
                    pe.wait_ge(sg["glu_done"], 1)
                    quad_in(pe, TP_GLU, 1, lambda k, tt: glu_o[:, tt * C + k * P:tt * C + (k + 1) * P])

            def merged_in(n):
                pe.wait_ge(sg["merged_done"], n + 1)
                quad_in(pe, TP_M + n, n % 2, lambda k, tt: merged[:, tt * C + k * P:tt * C + (k + 1) * P])

            for n in range(NCH):
                for j in range(TPU):
                    g = G_BR + 4 * n + j // 2
                    if n == 0 and j == 2:
                        pe.wait_ge(tp_lo, TP_GLU + 1)
                    products(pe, U_BR + n, j, g, g % 2, o_hi, o_lo, j * TK, j % 2 == 0, j % 2 == 1)
                    if j == 1 and n:
                        merged_in(n - 1)
            for n in range(NCH):
                for j in range(TPU):
                    g = G_WO + n
                    if n == 0 and j in (0, TPU - 2):
                        pe.wait_ge(tp_lo, TP_M + (NCH if j else NCH - 1))
                    products(pe, U_WO + n, j, g, g % 2, m_hi, m_lo, j * TK, j == 0, j == TPU - 1)
                    if n == 0 and j == 1:
                        merged_in(NCH - 1)
                    if j == 3 and n:
                        hidden_in(n - 1)
            def mlp_group(g, first, final):
                for n in range(2 * NCH):
                    up = n < NCH
                    for j in range(TPU):
                        if first and n == 0 and j in (0, TPU - 2):
                            pe.wait_ge(tp_lo, TP_H + (NCH if j else NCH - 1))
                        if n == NCH and j in (0, TPU - 2):
                            pe.wait_ge(tp_lo, g * NCH + (TP_FF + (NCH if j else NCH - 1)))
                        products(pe, g * (2 * NCH) + (U_FF + n), j, g * (2 * NCH) + (G_FF + n), (G_FF + n) % 2,
                                 v_hi if up else f_hi, v_lo if up else f_lo, j * TK, j == 0, j == TPU - 1)
                        if first and n == 0 and j == 3:
                            hidden_in(NCH - 1)
                        if j == 3 and 1 <= n <= NCH:
                            pe.wait_ge(sg["sq_done"], g * NCH + n)
                            rl = relu[(n - 1) % 2]
                            quad_in(pe, g * NCH + (TP_FF + n - 1), (TP_FF + n - 1) % 2,
                                    lambda k, tt: rl[:, tt * C + k * P:tt * C + (k + 1) * P])
                        if final and j == 3 and n > NCH:
                            last_in(n - NCH - 1)

            mlp_group(0, True, False)
            with pe.Fori(1, NFG - 1) as g:
                mlp_group(g, False, False)
            mlp_group(NFG - 1, False, True)
            for n in range(NCH):
                for j in range(TPU):
                    g = G_PG + n
                    if n == 0 and j in (0, TPU - 2):
                        pe.wait_ge(tp_lo, TP_P + (NCH if j else NCH - 1))
                    products(pe, U_PG + n, j, g, g % 2, v_hi, v_lo, j * TK, j == 0, j == TPU - 1)
                    if n == 0 and j == 3:
                        last_in(NCH - 1)

        @block.scalar
        def _(act):
            act.wait_ge(const_in, 80)
            for k in range(KT):
                if k % 4 == 0:
                    act.wait_ge(xt_in[k // 4], 16)
                i = act.activation(u_hi[:, k, :], xt[:, k, :], ACT.Copy, scale=g_mix[:, k:k + 1])
                if k % TK == TK - 1:
                    i.then_inc(x_hi, 1)
            for j in range(AHEAD):
                split_hi(act, 0, j)
            act.wait_ge(x_in, 16)
            for tt in range(TT):
                act.activation(xsq[:, tt, :], xin[:, tt, :], ACT.Square, accum_out=ssq[:, 0, tt:tt + 1])\
                    .then_inc(ssq_done, 1)
            act.wait_ge(var_done, 1)
            act.activation(rstd[:, 0, :], ssq[:, 0, :], ACT.Sqrt).then_inc(std_done, 1)
            act.wait_ge(rstd_done, 1)
            for i in range(NZ):
                for j in range(TPU):
                    split_hi(act, i, j + AHEAD)
                group_ready(act, i, TPU - 1)
                width = C if i < NZ - 1 else ZLAST
                act.activation(z[:, 0, i * C:i * C + width], acc[i % 2][:, 0:width], ACT.Copy,
                               scale=rstd[:, 0, 0:1]).then_inc(grp_free, 1)
                if i == 1:
                    act.activation(small[:, 0, :], s5p[:, 2, :], ACT.Exp).then_inc(sg["s5_dt"], 1)
                if i == 2:
                    act.wait_ge(sg["s5_arg"], 1)
                    act.activation(small[:, 2, :], small[:, 1, :], ACT.Exp).then_inc(sg["s5_exp"], 1)
                if i == 3:
                    act.wait_ge(sg["s5_th"], 1)
                    act.activation(small[:, 8, :], small[:, 6, :], ACT.Sin).then_inc(sg["s5_sin"], 1)
                    act.activation(small[:, 9, :], small[:, 7, :], ACT.Sin).then_inc(sg["s5_sin"], 1)

            def gate_tile(t):
                i, j = t // TPU, t % TPU
                split_hi(act, U_MG + i, j + AHEAD)
                if j == TPU - 1:
                    group_ready(act, U_MG + i, j)
                    if i >= 2:
                        act.wait_ge(gate_out[i % 2], 16 * (i // 2))
                    for tt in range(TT):
                        act.activation(gstage[:, i % 2, tt * C:(tt + 1) * C],
                                       acc[(G_MG + i) % 2][:, tt * C:(tt + 1) * C],
                                       ACT.Sigmoid, scale=rstd[:, 0, tt:tt + 1]).then_inc(grp_free, 1)

            until = interleaved(gate_tile)
            until(A_BAND)
            act.wait_ge(sg["pool_band"], 1)
            act.activation(pool_t[:, :, :].rearrange("p g t -> p (g t)"), aux[0][:, :], ACT.Copy)\
                .then_inc(sg["pool_copied"], 1)
            until(A_POOL)
            act.wait_ge(sg["pool_mixed"], 1)
            for g in range(4):
                act.activation(o_hi[:, 8 + g, :], aux[0][:, g * S:(g + 1) * S], ACT.Copy, scale=pool_s[:, g:g + 1])\
                    .then_inc(sg["pool_hi"], 1)
            until(A_QTR)
            act.wait_ge(sg["q_tr"], 1)
            act.activation(q_t[:, :, :].rearrange("p k t -> p (k t)"), aux[0][:, :], ACT.Copy, scale=DH ** -0.5)\
                .then_inc(sg["q_sb"], 1)
            until(A_KTR)
            act.wait_ge(sg["k_tr"], 1)
            act.activation(k_t[:, :, :].rearrange("p k t -> p (k t)"), aux[0][:, 0:2 * S], ACT.Copy).then_inc(sg["k_sb"], 1)
            act.activation(ngate[:, :, :], z[:, :, NG0:NG0 + 3 * NH], ACT.Sigmoid).then_inc(sg["ngate_done"], 1)
            until(A_CS + 2)
            act.wait_ge(sg["cs_sub"], 1)
            act.activation(pc[:, :, :, :].rearrange("p t h n -> p (t h n)"),
                           pc[:, :, :, :].rearrange("p t h n -> p (t h n)"), ACT.Exp).then_inc(sg["cs_exp"], 1)

            for hd in range(NH):
                until(A_HEAD[hd] + 1)
                act.wait_ge(sg["sc_max"], hd + 1)
                if hd >= 2:
                    act.wait_ge(sg["pt_tr"], hd - 1)
                for n, (o, w) in enumerate(((0, S), (S, S), (C, P), (C + P, P))):
                    act.activation(prob[:, hd % 2, o:o + w], aux[0][:, o:o + w], ACT.Exp, bias=stat[:, hd, n:n + 1],
                                   accum_out=stat[:, hd, 4 + n:5 + n]).then_inc(sg["sc_exp"], 1)
                until(A_HEAD[hd] + 3)
                act.wait_ge(sg["pt_tr"], hd + 1)
                if hd >= 2:
                    act.wait_ge(sg["pv_done"], hd - 1)
                act.activation(prob_t[:, hd % 2, 0:C], aux[1][:, 0:C], ACT.Copy).then_inc(sg["pt_sb"], 1)
                act.activation(prob_t[:, hd % 2, C:6 * P], aux[0][:, C + S:2 * C], ACT.Copy).then_inc(sg["pt_sb"], 1)
                if hd % 4 == 3:
                    until(A_HEAD[hd] + 4)
                    act.wait_ge(sg["pv_done"], hd + 1)
                    k = hd // 4 * 2
                    act.activation(o_hi[:, k:k + 2, :].rearrange("p k t -> p (k t)"), aux[1][:, C:2 * C], ACT.Copy)\
                        .then_inc(sg["nsa_hi"], 1)
                    act.wait_ge(sg["nsa_lo"], hd // 4 + 1)
            until(A_RTR)
            act.wait_ge(sg["rq_tr"], 1)
            act.activation(rq_t[:, :, :].rearrange("p k t -> p (k t)"), aux[0][:, :], ACT.Copy).then_inc(sg["rq_sb"], 1)
            act.wait_ge(sg["rk_tr"], 1)
            act.activation(rk_t[:, :, :].rearrange("p k t -> p (k t)"), aux[1][:, :], ACT.Copy).then_inc(sg["rk_sb"], 1)
            act.activation(rgate[:, :, :], z[:, :, RG0:RG0 + BW], ACT.Silu).then_inc(sg["rgate_done"], 1)
            for hd in range(RH):
                until(A_RS[hd] + 1)
                act.wait_ge(sg["ry_done"], hd + 1)
                for tt in range(TT):
                    if hd or tt:
                        act.wait_ge(sg["ry_ssq"], hd * TT + tt)
                    act.activation(rjunk[:, :], aux[1][:, tt * C + hd * P:tt * C + (hd + 1) * P], ACT.Square,
                                   accum_out=rstat[:, 0, tt * RH + hd:tt * RH + hd + 1]).then_inc(sg["ry_ssq"], 1)
            act.wait_ge(sg["ry_var"], 1)
            act.activation(rstat[:, 1, :], rstat[:, 0, :], ACT.Sqrt).then_inc(sg["ry_std"], 1)
            until(A_RQUAD)
            act.wait_ge(sg["ret_done"], 1)
            quad_hi(act, TP_RET, 1, o_hi[:, 12:16, :])
            act.wait_ge(tp_lo, TP_RET + 1)
            act.wait_ge(sg["u5_tr"], 1)
            act.activation(u5_t[:, :, :].rearrange("p k t -> p (k t)"), aux[0][:, :], ACT.Copy).then_inc(sg["u5_sb"], 1)
            act.wait_ge(p_in, 16)
            act.activation(p_hi[:, :, :], p_raw[:, :, :], ACT.Copy).then_inc(pt_hi, 1)
            for q in range(4):
                until(A_S5[q] + 15)
                act.wait_ge(sg["y5_done"], q + 1)
                act.activation(y5[:, :], y5[:, :], ACT.Gelu_apprx_tanh).then_inc(sg["y5_gelu"], 1)
                act.wait_ge(sg["y5_gelu"], q + 1)
                act.activation(y_hi[:, q, :], y5[:, :], ACT.Copy).then_inc(sg["y5_hi"], 1)
            until(A_END)
            for j in range(TPU):
                split_hi(act, U_GP, j + AHEAD)
                if j == 3:
                    group_ready(act, U_GP, 3)
                    act.activation(glu_s, acc[(G_GP + 1) % 2][:, :], ACT.Sigmoid).then_inc(sg["glu_sig"], 1)
            quad_hi(act, TP_GLU, 1, o_hi[:, 4:8, :])

            def merged_hi(n):
                quad_hi(act, TP_M + n, n % 2, m_hi[:, 4 * n:4 * n + 4, :])

            def hidden_hi(k):
                quad_hi(act, TP_H + k, (TP_H + k) % 2, v_hi[:, 4 * k:4 * k + 4, :], g_mlp[:, 4 * k:4 * k + 4])

            def last_hi(k):
                quad_hi(act, TP_P + k, (TP_P + k) % 2, v_hi[:, 4 * k:4 * k + 4, :])

            for n in range(NCH):
                for j in range(TPU):
                    split_hi(act, U_BR + n, j + AHEAD)
                    if j == 2 and n:
                        merged_hi(n - 1)
            for n in range(NCH):
                for j in range(TPU):
                    split_hi(act, U_WO + n, j + AHEAD)
                    if n == 0 and j == 2:
                        merged_hi(NCH - 1)
                    if n and j == 4:
                        hidden_hi(n - 1)

            def mlp_group(g, first, final):
                for n in range(2 * NCH):
                    u = g * (2 * NCH) + (U_FF + n)
                    for j in range(TPU):
                        split_hi(act, u, j + AHEAD)
                        if j == 4 and 1 <= n <= NCH:
                            quad_hi(act, g * NCH + (TP_FF + n - 1), (TP_FF + n - 1) % 2, f_hi[:, 4 * n - 4:4 * n, :])
                        if first and n == 0 and j == 4:
                            hidden_hi(NCH - 1)
                            for tt in range(TT):
                                if tt:
                                    act.wait_ge(ssq_done, TT + tt)
                                act.activation(junk[:, :], h[:, tt, :], ACT.Square, accum_out=ssq[:, 1, tt:tt + 1])\
                                    .then_inc(ssq_done, 1)
                        if first and n == 0 and j == TPU - 1:
                            act.wait_ge(var_done, 2)
                            act.activation(rstd[:, 1, :], ssq[:, 1, :], ACT.Sqrt).then_inc(std_done, 1)
                            act.wait_ge(rstd_done, 2)
                        if final and j == 4 and n > NCH:
                            last_hi(n - NCH - 1)
                    if n < NCH:
                        group_ready(act, u, TPU - 1)
                        for tt in range(TT):
                            act.activation(relu[n % 2][:, tt * C:(tt + 1) * C],
                                           acc[(G_FF + n) % 2][:, tt * C:(tt + 1) * C], ACT.Relu,
                                           scale=rstd[:, 1, tt:tt + 1]).then_inc(grp_free, 1)

            mlp_group(0, True, False)
            with act.Fori(1, NFG - 1) as g:
                mlp_group(g, False, False)
            mlp_group(NFG - 1, False, True)
            for n in range(NCH):
                for j in range(TPU):
                    split_hi(act, U_PG + n, j + AHEAD)
                    if n == 0 and j == 4:
                        last_hi(NCH - 1)
                group_ready(act, U_PG + n, TPU - 1)
                act.activation(pgate[:, n, :], acc[(G_PG + n) % 2][:, :], ACT.Sigmoid).then_inc(grp_free, 2)
            for tt in range(TT):
                act.wait_ge(sg["pg_sig"], 1)
                act.activation(pp[:, tt, :], h[:, tt, :], ACT.Square, accum_out=ssq[:, 2, tt:tt + 1])\
                    .then_inc(ssq_done, 1)
            act.wait_ge(var_done, 3)
            act.activation(rstd[:, 2, :], ssq[:, 2, :], ACT.Sqrt).then_inc(std_done, 1)

        @block.gpsimd
        def _(gp):
            gp.wait_ge(lo_done, T_MG)
            with gp.Fori(0, 4 * NCH) as i:
                for j in range(TPU):
                    split_lo(gp, i + U_MG, j)

        @block.vector
        def _(v):
            done = [0]

            def link(ins):
                done[0] += 1
                ins.then_inc(dve, 1)
                v.wait_ge(dve, done[0])

            def inv_std(n, count):
                v.wait_ge(ssq_done, TT * (n + 1))
                v.tensor_scalar(ssq[:, n, :], ssq[:, n, :], 1.0 / count, EPS, ALU.mult, ALU.add).then_inc(var_done, 1)
                v.wait_ge(std_done, n + 1)
                v.reciprocal(rstd[:, n, :], rstd[:, n, :]).then_inc(rstd_done, 1)

            sm = lambda i: small[:, i, :]

            def s5_angles():
                v.wait_ge(sg["s5_dt"], 1)
                v.tensor_tensor(sm(1), s5p[:, 0, :], sm(0), ALU.mult).then_inc(sg["s5_arg"], 1)
                link(v.tensor_tensor(sm(3), s5p[:, 1, :], sm(0), ALU.mult))
                magic = 1.5 * 2.0 ** 23
                link(v.tensor_scalar(sm(4), sm(3), 1.0 / (2 * math.pi), magic, ALU.mult, ALU.add))
                link(v.tensor_scalar(sm(4), sm(4), -magic, None, ALU.add))
                p1 = 6.28125
                p2 = math.floor((2 * math.pi - p1) * 2 ** 20) / 2 ** 20
                p3 = 2 * math.pi - p1 - p2
                src = 3
                for part in (p1, p2, p3):
                    link(v.scalar_tensor_tensor(out=sm(5), in0=sm(4), scalar=-part, in1=sm(src), op0=ALU.mult, op1=ALU.add))
                    src = 5
                top = float(np.nextafter(np.float32(math.pi), np.float32(0)))
                link(v.tensor_scalar(sm(6), sm(5), top, -top, ALU.min, ALU.max))
                link(v.tensor_scalar(sm(7), sm(6), -1.0, None, ALU.mult))
                link(v.tensor_tensor(sm(7), sm(6), sm(7), ALU.max))
                v.tensor_scalar(sm(7), sm(7), -1.0, math.pi / 2, ALU.mult, ALU.add).then_inc(sg["s5_th"], 1)

            def s5_coefficients():
                v.wait_ge(sg["s5_sin"], 2)
                v.wait_ge(sg["s5_exp"], 1)
                link(v.tensor_tensor(sm(10), sm(2), sm(9), ALU.mult))
                link(v.tensor_scalar(sm(10), sm(10), -1.0, None, ALU.add))
                link(v.tensor_tensor(sm(11), sm(2), sm(8), ALU.mult))
                link(v.tensor_tensor(sm(12), s5p[:, 0, :], s5p[:, 0, :], ALU.mult))
                link(v.tensor_tensor(sm(13), s5p[:, 1, :], s5p[:, 1, :], ALU.mult))
                link(v.tensor_tensor(sm(14), sm(12), sm(13), ALU.add))
                link(v.reciprocal(sm(14), sm(14)))
                link(v.tensor_tensor(sm(12), sm(10), s5p[:, 0, :], ALU.mult))
                link(v.tensor_tensor(sm(13), sm(11), s5p[:, 1, :], ALU.mult))
                link(v.tensor_tensor(sm(12), sm(12), sm(13), ALU.add))
                link(v.tensor_tensor(sm(15), sm(12), sm(14), ALU.mult))
                link(v.tensor_tensor(sm(12), sm(11), s5p[:, 0, :], ALU.mult))
                link(v.tensor_tensor(sm(13), sm(10), s5p[:, 1, :], ALU.mult))
                link(v.tensor_tensor(sm(12), sm(12), sm(13), ALU.subtract))
                link(v.tensor_tensor(sm(16), sm(12), sm(14), ALU.mult))
                link(v.tensor_copy(sm(20), sm(9)))
                link(v.tensor_copy(sm(21), sm(8)))
                for k in range(6):
                    c0, s0, c1, s1 = (20 + 2 * k + i for i in range(4))
                    link(v.tensor_tensor(sm(12), sm(c0), sm(c0), ALU.mult))
                    link(v.tensor_tensor(sm(13), sm(s0), sm(s0), ALU.mult))
                    link(v.tensor_tensor(sm(c1), sm(12), sm(13), ALU.subtract))
                    link(v.tensor_tensor(sm(12), sm(c0), sm(s0), ALU.mult))
                    link(v.tensor_scalar(sm(s1), sm(12), 2.0, None, ALU.mult))

            for k in range(KT):
                if k % TK == 0:
                    v.wait_ge(x_hi, k // TK + 1)
                i = v.scalar_tensor_tensor(out=u_lo[:, k, :], in0=xt[:, k, :], scalar=g_mix[:, k:k + 1],
                                           in1=u_hi[:, k, :].bitcast(F32), op0=ALU.mult, op1=ALU.subtract)
                if k % TK == TK - 1:
                    i.then_inc(x_lo, 1)
            for j in range(AHEAD):
                split_lo(v, 0, j)
            inv_std(0, D)
            v.wait_ge(rstd_done, 1)
            for i in range(NZ):
                for j in range(TPU):
                    if i * TPU + j + AHEAD < NZ * TPU:
                        split_lo(v, i, j + AHEAD)
                group_ready(v, i, TPU - 1)
                width = C if i < NZ - 1 else ZLAST
                v.tensor_scalar(z[:, 1, i * C:i * C + width], acc[i % 2][:, C:C + width], rstd[:, 0, 1:2], None,
                                ALU.mult).then_inc(grp_free, 1)
                if i == 1:
                    s5_angles()
                if i == 4:
                    s5_coefficients()
            v.wait_ge(sg["pool_hi"], 4)
            for g in range(4):
                i = v.scalar_tensor_tensor(out=o_lo[:, 8 + g, :], in0=aux[0][:, g * S:(g + 1) * S],
                                           scalar=pool_s[:, g:g + 1], in1=o_hi[:, 8 + g, :].bitcast(F32),
                                           op0=ALU.mult, op1=ALU.subtract)
            i.then_inc(sg["pool_lo"], 1)
            v.wait_ge(sg["cmp_tr"], 1)
            v.tensor_copy(kv_ct[:, :, :].rearrange("p g t -> p (g t)"), aux[1][:, 0:NG * S]).then_inc(sg["cmp_copied"], 1)
            v.wait_ge(sg["cmp_sum"], 1)
            v.wait_ge(sg["pool_lo"], 1)
            link(v.memset(kvc[:, :, :, :], 0.0))
            for g in range(NG):
                src = aux[1][:, C + g * NCMP:C + (g + 1) * NCMP].rearrange("p (o n) -> p o n", o=1)
                i = v.tensor_copy(kvc[:, g, :, 0:NCMP], src.to_broadcast([P, R, NCMP]))
            i.then_inc(sg["cmp_sb"], 1)
            v.wait_ge(sg["xg_tr"], 1)
            v.tensor_copy(xg[:, :, :].rearrange("p g e -> p (g e)"), aux[1][:, 0:NG * P])
            v.tensor_copy(xk[0:CP, :].rearrange("p (g e) -> p g e", g=NG),
                          aux[1][0:CP, 0:NG * P].rearrange("p (g e) -> p g e", g=NG)[:, :, 0:DH]).then_inc(sg["xg_sb"], 1)
            v.wait_ge(sg["kc_tr"], 1)
            v.tensor_copy(kc_t[:, :], aux[1][:, C:C + CP]).then_inc(sg["kc_sb"], 1)
            v.wait_ge(sg["cs_done"], 1)
            v.wait_ge(mask_in, 32)
            sc = aux[1][:, :].rearrange("p (g x) -> p g x", g=NG)[:, :, 0:TT * R * CP]\
                .rearrange("p g (t r n) -> p t g r n", t=TT, r=R)

            def bc_mask(which, tt):
                return cmask[:, which, tt:tt + 1, :].to_broadcast([P, NH, CP])

            for tt in range(TT):
                link(v.tensor_tensor(pc[:, tt, :, :].rearrange("p (g r) n -> p g r n", g=NG), sc[:, tt, :, :, :],
                                     bc_mask(0, tt).rearrange("p (g r) n -> p g r n", g=NG), ALU.add))
            link(v.tensor_reduce(cstat[:, 0, :, :], pc[:, :, :, :], AX_X, ALU.max))
            for tt in range(TT):
                i = v.tensor_tensor(pc[:, tt, :, :], pc[:, tt, :, :],
                                    cstat[:, 0, tt, :].rearrange("p (h o) -> p h o", o=1).to_broadcast([P, NH, CP]),
                                    ALU.subtract)
                link(i)
            v.sem_inc(sg["cs_sub"], 1)
            v.wait_ge(sg["cs_exp"], 1)
            for tt in range(TT):
                link(v.tensor_tensor(pc[:, tt, :, :], pc[:, tt, :, :], bc_mask(1, tt), ALU.mult))
            link(v.tensor_reduce(cstat[:, 1, :, :], pc[:, :, :, :], AX_X, ALU.add))
            link(v.tensor_scalar(cstat[:, 2, :, :], cstat[:, 1, :, :], 1e-30, None, ALU.max))
            link(v.reciprocal(cstat[:, 3, :, :], cstat[:, 2, :, :]))
            v.wait_ge(sg["ngate_done"], 1)
            link(v.tensor_tensor(cstat[:, 2, :, :], cstat[:, 3, :, :], ngate[:, :, 0:NH], ALU.mult))
            for tt in range(TT):
                i = v.tensor_tensor(pc[:, tt, :, :], pc[:, tt, :, :],
                                    cstat[:, 2, tt, :].rearrange("p (h o) -> p h o", o=1).to_broadcast([P, NH, CP]),
                                    ALU.mult)
                link(i)
            v.sem_inc(sg["pc_done"], 1)
            v.wait_ge(sg["pc_tr"], 1)
            v.tensor_copy(pc_t[:, :, :, :].rearrange("p g t q -> p (g t q)"), aux[1][:, 0:C]).then_inc(sg["pc_sb"], 1)
            def rotate(i):
                c0, tt = (RQ0, RK0)[i // 2], i % 2
                x = z[:, tt, c0:c0 + BW]
                heads = x.rearrange("p (h d) -> p h d", h=RH)
                sw = x.rearrange("p (h i two) -> p h i two", h=RH, two=2)[:, :, :, ::-1]
                cs = rot[:, 0, tt:tt + 1, :].to_broadcast([P, RH, P])
                sn = rot[:, 1, tt:tt + 1, :].to_broadcast([P, RH, P])
                link(v.tensor_tensor(rtmp[:, :].rearrange("p (h i two) -> p h i two", h=RH, two=2), sw,
                                     sn.rearrange("p h (i two) -> p h i two", two=2), ALU.mult))
                link(v.tensor_tensor(heads, heads, cs, ALU.mult))
                v.tensor_tensor(x, x, rtmp[:, :], ALU.add).then_inc(sg["rot_done"], 1)

            for hd in range(NH):
                v.wait_ge(sg["sc_done"], hd + 1)
                s1 = aux[0][:, 0:C].rearrange("p (i k) -> p i k", i=2)
                s0 = aux[0][:, C:C + S].rearrange("p (i k) -> p i k", i=2)
                tri2 = tri[:, :].rearrange("p (o k) -> p o k", o=1).to_broadcast([P, 2, P])
                link(v.tensor_tensor(s1[:, :, P:S], s1[:, :, P:S], tri2, ALU.add))
                link(v.tensor_tensor(s0, s0, tri2, ALU.add))
                v.tensor_reduce(stat[:, hd, 0:2], s1, AX_X, ALU.max, negate=True)
                v.tensor_reduce(stat[:, hd, 2:4], s0, AX_X, ALU.max, negate=True).then_inc(sg["sc_max"], 1)
                v.wait_ge(sg["sc_exp"], 4 * hd + 4)
                link(v.reciprocal(stat[:, hd, 8:12], stat[:, hd, 4:8]))
                for n, tt in enumerate((1, 0)):
                    link(v.tensor_tensor(stat[:, hd, 12 + 2 * n:14 + 2 * n], stat[:, hd, 8 + 2 * n:10 + 2 * n],
                                         ngate[:, tt, NH + hd % 2 * R + hd // 2:3 * NH:NH], ALU.mult))
                for n, (o, w) in enumerate(((0, S), (S, S), (C, P), (C + P, P))):
                    i = v.tensor_scalar(prob[:, hd % 2, o:o + w], prob[:, hd % 2, o:o + w], stat[:, hd, 12 + n:13 + n],
                                        None, ALU.mult)
                i.then_inc(sg["sc_scaled"], 1)
                if hd < 4:
                    if hd == 0:
                        v.wait_ge(rot_in, 16)
                    else:
                        v.wait_ge(sg["rot_done"], hd)
                    rotate(hd)
                if hd % 4 == 3:
                    k = hd // 4 * 2
                    v.wait_ge(sg["nsa_hi"], hd // 4 + 1)
                    v.tensor_tensor(o_lo[:, k:k + 2, :].rearrange("p k t -> p (k t)"), aux[1][:, C:2 * C],
                                    o_hi[:, k:k + 2, :].rearrange("p k t -> p (k t)").bitcast(F32), ALU.subtract)\
                        .then_inc(sg["nsa_lo"], 1)
            v.wait_ge(ret_in, 16)
            for hd in range(RH):
                v.wait_ge(sg["rs_done"], hd + 1)
                if hd >= 2:
                    v.wait_ge(sg["ry_done"], hd - 1)
                b = (hd % 2) * C
                v.tensor_tensor(rs_t[:, hd % 2, :], aux[0][:, b:b + 3 * P], decay[:, hd, :], ALU.mult)\
                    .then_inc(sg["rs_dec"], 1)
            v.wait_ge(sg["ry_ssq"], TT * RH)
            v.tensor_scalar(rstat[:, 0, :], rstat[:, 0, :], 1.0 / RD, EPS, ALU.mult, ALU.add).then_inc(sg["ry_var"], 1)
            v.wait_ge(sg["ry_std"], 1)
            link(v.reciprocal(rstat[:, 2, :], rstat[:, 1, :]))
            v.wait_ge(sg["rgate_done"], 1)
            for tt in range(TT):
                for hd in range(RH):
                    i = v.scalar_tensor_tensor(out=ry[:, tt, hd * P:(hd + 1) * P],
                                               in0=aux[1][:, tt * C + hd * P:tt * C + (hd + 1) * P],
                                               scalar=rstat[:, 2, tt * RH + hd:tt * RH + hd + 1],
                                               in1=rgate[:, tt, hd * P:(hd + 1) * P], op0=ALU.mult, op1=ALU.mult)
            i.then_inc(sg["ret_done"], 1)
            quad_lo(v, TP_RET, 1, o_lo[:, 12:16, :], o_hi[:, 12:16, :])
            v.wait_ge(tp_lo, TP_RET + 1)
            for q in range(4):
                pw = lambda i, n: small[:, i, 4 * q:4 * q + 4].rearrange("p (i o) -> p i o", o=1).to_broadcast([P, 4, n])
                link(v.memset(gr[:, :, 0:1], 1.0))
                link(v.memset(gi[:, :, 0:1], 0.0))
                n = 1
                for k in range(7):
                    c_, s_ = pw(20 + 2 * k, n), pw(21 + 2 * k, n)
                    link(v.tensor_tensor(t1[:, :, 0:n], gr[:, :, 0:n], c_, ALU.mult))
                    link(v.tensor_tensor(t2[:, :, 0:n], gi[:, :, 0:n], s_, ALU.mult))
                    link(v.tensor_tensor(gr[:, :, n:2 * n], t1[:, :, 0:n], t2[:, :, 0:n], ALU.subtract))
                    link(v.tensor_tensor(t1[:, :, 0:n], gr[:, :, 0:n], s_, ALU.mult))
                    link(v.tensor_tensor(t2[:, :, 0:n], gi[:, :, 0:n], c_, ALU.mult))
                    link(v.tensor_tensor(gi[:, :, n:2 * n], t1[:, :, 0:n], t2[:, :, 0:n], ALU.add))
                    n *= 2
                c_, s_ = pw(15, TH), pw(16, TH)
                A3 = lambda x: x[:, :, :]
                link(v.tensor_tensor(A3(t1), A3(gr), c_, ALU.mult))
                link(v.tensor_tensor(A3(t2), A3(gi), s_, ALU.mult))
                link(v.tensor_tensor(A3(fr), A3(t1), A3(t2), ALU.add))
                link(v.tensor_tensor(A3(t1), A3(gr), s_, ALU.mult))
                link(v.tensor_tensor(A3(t2), A3(gi), c_, ALU.mult))
                link(v.tensor_tensor(A3(fi), A3(t1), A3(t2), ALU.subtract))
                for hf in range(TT):
                    n = q * TT + hf
                    v.wait_ge(sg["bu_done"], 4 * (n + 1))
                    br = aux[0][:, 0:C].rearrange("p (i t) -> p i t", i=4)
                    bi = aux[0][:, C:2 * C].rearrange("p (i t) -> p i t", i=4)
                    link(v.tensor_tensor(A3(t1), br, A3(fr), ALU.mult))
                    link(v.tensor_tensor(A3(t2), bi, A3(fi), ALU.mult))
                    if n:
                        v.wait_ge(sg["c_done"], n)
                    link(v.tensor_tensor(A3(vr), A3(t1), A3(t2), ALU.subtract))
                    link(v.tensor_tensor(A3(t1), bi, A3(fr), ALU.mult))
                    link(v.tensor_tensor(A3(t2), br, A3(fi), ALU.mult))
                    v.sem_inc(sg["bu_used"], 1)
                    link(v.tensor_tensor(A3(vi), A3(t1), A3(t2), ALU.add))
                    for i in range(4):
                        r_ = small[:, 2, 4 * q + i:4 * q + i + 1].to_broadcast([P, TH])
                        for src, dst, st in ((vr, sr, 34), (vi, si, 35)):
                            init = 0.0 if hf == 0 else small[:, st, i:i + 1]
                            link(v.tensor_tensor_scan(dst[:, i, :], r_, src[:, i, :], init, ALU.mult, ALU.add))
                    link(v.tensor_tensor(A3(t1), A3(gr), A3(sr), ALU.mult))
                    link(v.tensor_tensor(A3(t2), A3(gi), A3(si), ALU.mult))
                    link(v.tensor_tensor(A3(vr), A3(t1), A3(t2), ALU.subtract))
                    link(v.tensor_tensor(A3(t1), A3(gr), A3(si), ALU.mult))
                    link(v.tensor_tensor(A3(t2), A3(gi), A3(sr), ALU.mult))
                    link(v.scalar_tensor_tensor(out=A3(vi), in0=A3(t1), scalar=-1.0, in1=A3(t2),
                                                op0=ALU.mult, op1=ALU.subtract))
                    v.sem_inc(sg["sh_done"], 1)
                    if hf == 0:
                        hr, hi_ = vr[:, :, TH - 1], vi[:, :, TH - 1]
                        c1, s1 = small[:, 20, 4 * q:4 * q + 4], small[:, 21, 4 * q:4 * q + 4]
                        a_, b_ = small[:, 36, 0:4], small[:, 37, 0:4]
                        link(v.tensor_tensor(a_, hr, c1, ALU.mult))
                        link(v.tensor_tensor(b_, hi_, s1, ALU.mult))
                        link(v.tensor_tensor(small[:, 34, 0:4], a_, b_, ALU.add))
                        link(v.tensor_tensor(a_, hr, s1, ALU.mult))
                        link(v.tensor_tensor(b_, hi_, c1, ALU.mult))
                        link(v.tensor_tensor(small[:, 35, 0:4], a_, b_, ALU.subtract))
                v.wait_ge(sg["c_done"], 2 * q + 2)
                v.wait_ge(sg["y5_lo"], q) if q else None
                v.scalar_tensor_tensor(out=y5[:, :], in0=u5_t[:, q, :], scalar=s5_d[:, q:q + 1],
                                       in1=aux[1][:, (q % 2) * C:(q % 2) * C + S], op0=ALU.mult, op1=ALU.add)\
                    .then_inc(sg["y5_done"], 1)
                v.wait_ge(sg["y5_hi"], q + 1)
                v.tensor_tensor(y_lo[:, q, :], y5[:, :], y_hi[:, q, :].bitcast(F32), ALU.subtract)\
                    .then_inc(sg["y5_lo"], 1)
            v.wait_ge(pt_hi, 1)
            v.tensor_tensor(p_lo[:, :, :], p_raw[:, :, :], p_hi[:, :, :].bitcast(F32), ALU.subtract).then_inc(pt_lo, 1)
            v.wait_ge(lo_done, U_GP * TPU)
            for j in range(AHEAD):
                split_lo(v, U_GP, j)
            for j in range(TPU):
                split_lo(v, U_GP, j + AHEAD)
                if j == 3:
                    v.wait_ge(sg["glu_sig"], 1)
                    link(v.tensor_tensor(glu_o, acc[G_GP % 2][:, :], glu_s, ALU.mult))
                    v.sem_inc(grp_free, 4)
                    v.sem_inc(sg["glu_done"], 1)
                    for i in range(2):
                        v.wait_ge(gate_out[i], 16 * 2 * NCH)
                if j >= 4:
                    group_ready(v, U_GP, j)
                    g = G_GP + j - 2
                    n = j - 4
                    v.tensor_copy(pp[:, :, n * C:(n + 1) * C], acc[g % 2][:, :].rearrange("p (t n) -> p t n", t=TT))\
                        .then_inc(grp_free, 2)
            quad_lo(v, TP_GLU, 1, o_lo[:, 4:8, :], o_hi[:, 4:8, :])

            def merged_lo(n):
                quad_lo(v, TP_M + n, n % 2, m_lo[:, 4 * n:4 * n + 4, :], m_hi[:, 4 * n:4 * n + 4, :])

            def hidden_lo(k):
                quad_lo(v, TP_H + k, (TP_H + k) % 2, v_lo[:, 4 * k:4 * k + 4, :], v_hi[:, 4 * k:4 * k + 4, :],
                        g_mlp[:, 4 * k:4 * k + 4])

            def last_lo(k):
                quad_lo(v, TP_P + k, (TP_P + k) % 2, v_lo[:, 4 * k:4 * k + 4, :], v_hi[:, 4 * k:4 * k + 4, :])

            for n in range(NCH):
                for j in range(TPU):
                    split_lo(v, U_BR + n, j + AHEAD)
                    if j % 2 == 1:
                        b = j // 2
                        g = G_BR + 4 * n + b
                        group_ready(v, U_BR + n, j)
                        v.wait_ge(gate_in[b], 16 * (n + 1))
                        if b == 0:
                            if n:
                                v.wait_ge(tp_in, TP_M + n)
                            link(v.tensor_tensor(merged[:, :], acc[g % 2][:, :], gates[:, b, :], ALU.mult))
                            v.sem_inc(grp_free, 2)
                            v.sem_inc(gate_used, 1)
                        else:
                            link(v.tensor_tensor(prodt[:, :], acc[g % 2][:, :], gates[:, b, :], ALU.mult))
                            v.sem_inc(grp_free, 2)
                            v.sem_inc(gate_used, 1)
                            link(v.tensor_tensor(merged[:, :], merged[:, :], prodt[:, :], ALU.add))
                    if j == 2 and n:
                        merged_lo(n - 1)
                v.sem_inc(sg["merged_done"], 1)

            def add_residual(n, par):
                hc = h[:, :, n * C:(n + 1) * C]
                v.tensor_tensor(hc, acc[par][:, :].rearrange("p (t n) -> p t n", t=TT), hc, ALU.add)\
                    .then_inc(grp_free, 2)

            for n in range(NCH):
                for j in range(TPU):
                    split_lo(v, U_WO + n, j + AHEAD)
                    if n == 0 and j == 2:
                        merged_lo(NCH - 1)
                    if n and j == 4:
                        hidden_lo(n - 1)
                group_ready(v, U_WO + n, TPU - 1)
                if n == 0:
                    v.wait_ge(h_in, 16)
                add_residual(n, (G_WO + n) % 2)

            def mlp_group(g, first, final):
                for n in range(2 * NCH):
                    u = g * (2 * NCH) + (U_FF + n)
                    for j in range(TPU):
                        split_lo(v, u, j + AHEAD)
                        if j == 4 and 1 <= n <= NCH:
                            quad_lo(v, g * NCH + (TP_FF + n - 1), (TP_FF + n - 1) % 2, f_lo[:, 4 * n - 4:4 * n, :],
                                    f_hi[:, 4 * n - 4:4 * n, :])
                        if first and n == 0 and j == 4:
                            hidden_lo(NCH - 1)
                        if first and n == 0 and j == TPU - 1:
                            inv_std(1, D)
                        if final and j == 4 and n > NCH:
                            last_lo(n - NCH - 1)
                    if n < NCH:
                        v.wait_ge(grp_free, g * (4 * NCH) + 2 * (G_FF + n + 1))
                        rl = relu[n % 2]
                        v.tensor_tensor(rl[:, :], rl[:, :], rl[:, :], ALU.mult).then_inc(sg["sq_done"], 1)
                    else:
                        group_ready(v, u, TPU - 1)
                        add_residual(n - NCH, (G_FF + n) % 2)

            mlp_group(0, True, False)
            with v.Fori(1, NFG - 1) as g:
                mlp_group(g, False, False)
            mlp_group(NFG - 1, False, True)
            for n in range(NCH):
                for j in range(TPU):
                    split_lo(v, U_PG + n, j + AHEAD)
                    if n == 0 and j == 4:
                        last_lo(NCH - 1)
                v.wait_ge(grp_free, 2 * (G_PG + n + 1))
                ga = pgate[:, n, :].rearrange("p (t n) -> p t n", t=TT)
                hc = h[:, :, n * C:(n + 1) * C]
                link(v.tensor_tensor(ga, ga, pp[:, :, n * C:(n + 1) * C], ALU.mult))
                link(v.tensor_tensor(hc, hc, ga, ALU.add))
            v.sem_inc(sg["pg_sig"], 1)
            inv_std(2, D)
            v.wait_ge(rstd_done, 3)
            v.wait_ge(fin_in, 16)
            for tt in range(TT):
                i = v.scalar_tensor_tensor(out=h[:, tt, :], in0=h[:, tt, :], scalar=rstd[:, 2, tt:tt + 1],
                                           in1=g_fin[:, :], op0=ALU.mult, op1=ALU.mult)
            i.then_inc(z_dve, 1)


def band_matrix():
    t = np.arange(S)
    out = np.zeros((S, 4, S), np.float32)
    for g, w in enumerate((2, 4, 8, 16)):
        inside = (t[None, :] >= t[:, None]) & (t[None, :] < t[:, None] + w)
        out[:, g] = inside / np.minimum(t + 1, w)[None, :] - (t[None, :] == t[:, None])
    return np.ascontiguousarray(out.reshape(TT, P, 4, S).transpose(1, 2, 0, 3))


def rotation():
    angle = np.repeat(1.0 / 10000.0 ** np.linspace(0.0, 1.0, RD // 2), 2)
    angle = np.arange(S)[:, None] * angle[None, :]
    sign = np.where(np.arange(RD) % 2 == 0, -1.0, 1.0)
    both = np.stack([np.cos(angle), np.sin(angle) * sign]).reshape(2, TT, P, RD)
    return np.ascontiguousarray(both.transpose(2, 0, 1, 3).astype(np.float32))


def decays():
    gamma = 1.0 - 2.0 ** (-5.0 - np.arange(RH))
    rel = np.arange(S)[None, :] - np.arange(P)[:, None]
    d = np.where(rel >= 0, gamma[:, None, None] ** np.maximum(rel, 0), 0.0) * RD ** -0.5
    d = np.concatenate([d, d[:, :, :P]], axis=2)
    return np.ascontiguousarray(d.transpose(1, 0, 2).astype(np.float32))


def compressed_mask():
    t, n = np.arange(S)[:, None], np.arange(CP)[None, :]
    seen = (n < NCMP) & (16 * n + 31 <= t)
    both = np.stack([np.where(seen, 0.0, NEG), seen.astype(np.float64)]).reshape(2, TT, P, CP)
    return np.ascontiguousarray(both.transpose(2, 0, 1, 3).astype(np.float32))


def kernel(x, p, g_mix, w_in, w_cmp_k, w_cmp_v, s5_a_re, s5_a_im, s5_log_dt, s5_b_re, s5_b_im,
           s5_c_re, s5_c_im, s5_d, s5_w_glu, pool_w, pool_scale, w_branch, w_out, g_mlp,
           w_mlp_up, w_mlp_down, w_ple_gate, w_ple_proj, g_final):
    import concourse.bacc as bacc
    from concourse.bass_utils import run_bass_kernel_spmd

    f32 = np.float32
    x, p = np.asarray(x), np.asarray(p)

    def by_partition(v):
        return np.ascontiguousarray(np.asarray(v).reshape(-1, P).T)

    def states(v):
        return np.asarray(v)[0].reshape(ST, P).T

    w_cmp = np.zeros((P, 32, P), f32)
    w_cmp[:DH, :, :DH] = np.asarray(w_cmp_k)[0].transpose(1, 0, 2)
    w_cmp[DH:, :, DH:] = np.asarray(w_cmp_v)[0].transpose(1, 0, 2)
    s5_b = np.zeros((4, 2, SC, 2, 4, 2, SN), f32)
    s5_c = np.zeros((2, SN, 2, ST, 2, SC), f32)
    for im, (b, c) in enumerate(((s5_b_re, s5_c_re), (s5_b_im, s5_c_im))):
        b = np.asarray(b)[0].reshape(4, 4, 2, SN, SC)
        c = np.asarray(c)[0].reshape(ST, 2, SC, SN)
        for j in range(2):
            s5_b[:, j, :, im, :, j, :] = b[:, :, j].transpose(1, 3, 0, 2)
            s5_c[j, :, im, :, j, :] = c[:, j].transpose(2, 0, 1)
    dt = np.broadcast_to(np.asarray(s5_log_dt)[0][:, None], (SG, SN)).reshape(ST, P).T
    causal = np.arange(P)[None, :] <= np.arange(P)[:, None]
    head_order = np.arange(NH * DH).reshape(NG, R, DH).transpose(1, 0, 2).ravel()
    pair_order = np.arange(2 * NG * DH).reshape(2, NG, DH).transpose(1, 0, 2).ravel()
    order = np.concatenate([Q0 + head_order, KV0 + pair_order, np.arange(KV0 + 2 * P, ZS)])
    w_in = np.asarray(w_in)[0]
    w_branch = np.asarray(w_branch)[0].reshape(D, D)
    w_branch = np.concatenate([w_branch[head_order], w_branch[BW:]])
    arrays = {
        "x": x[0], "xt": x[0].T, "pt": p[0, 0].T,
        "g_mix": by_partition(g_mix), "g_mlp": by_partition(g_mlp),
        "g_final": np.broadcast_to(np.asarray(g_final)[None, :], (P, D)),
        "w_in": w_in, "w_mix": w_in[:, order], "w_glu": np.asarray(s5_w_glu)[0], "w_pp": np.asarray(w_ple_proj)[0],
        "w_branch": w_branch, "w_out": np.asarray(w_out)[0],
        "w_up": np.asarray(w_mlp_up)[0], "w_down": np.asarray(w_mlp_down)[0], "w_pg": np.asarray(w_ple_gate)[0],
        "w_pool": np.asarray(pool_w)[0], "pool_scale": by_partition(pool_scale), "w_cmp": w_cmp,
        "s5p": np.stack([states(s5_a_re), states(s5_a_im), dt], axis=1),
        "s5_b": s5_b.reshape(P, 2, 4, P), "s5_c": s5_c.reshape(P, 2, ST, 32), "s5_d": by_partition(s5_d),
        "ident": np.eye(P, dtype=f32), "band": band_matrix(), "rot": rotation(), "decay": decays(),
        "cmask": compressed_mask(), "tri": np.where(causal, 0.0, NEG).astype(f32),
    }
    arrays = {f"in_{k}": np.ascontiguousarray(v) for k, v in arrays.items()}
    nc = bacc.Bacc("TRN2", target_bir_lowering=False, num_devices=1)
    aps = {k[3:]: nc.dram_tensor(k, v.shape, mybir.dt.from_np(v.dtype), kind="ExternalInput").ap()
           for k, v in arrays.items()}
    out = nc.dram_tensor("out", (S, D), F32, kind="ExternalOutput").ap()
    hybrid_layer(nc, aps, out)
    r = run_bass_kernel_spmd(nc, [arrays], core_ids=[0])
    return r.results[0]["out"].reshape(1, S, D)
```

```python
import math
from contextlib import ExitStack

import numpy as np

import concourse.bass as bass
from concourse import mybir

F32 = mybir.dt.float32
F32R = mybir.dt.float32r
ALU = mybir.AluOpType
ACT = mybir.ActivationFunctionType
AX_X = mybir.AxisListType.X

P = 128
D = 2048
S = 256
TT = S // P
KT = D // P
CW = 512
TK = 2
NCH = D // CW
TPU = KT // TK
BW = D // 4
NH, NG, DH = 8, 2, 64
R = NH // NG
NCMP = (S - 32) // 16 + 1
CP = 32
RH, RD = 4, 128
SG, SN, SC = 32, 64, 16
ST = SG * SN // P
TH = P
EPS = 1e-6
NEG = -1e30
FF = 4 * D
NFG = FF // D
PD = 256

Q0 = 0
KV0 = Q0 + NH * DH
NG0 = KV0 + 6 * NG * DH
S50 = NG0 + 3 * NH
PL0 = S50 + BW
RQ0 = PL0 + BW
RK0 = RQ0 + BW
RV0 = RK0 + BW
RG0 = RV0 + BW
ZS = RG0 + BW
NZ = -(-ZS // CW)
ZLAST = ZS - (NZ - 1) * CW

U_MG = NZ
U_GP = U_MG + 4 * NCH
U_BR = U_GP + 1
U_WO = U_BR + NCH
U_FF = U_WO + NCH
U_PG = U_FF + NFG * 2 * NCH
U_END = U_PG + NCH
TILES = U_END * TPU
T_MG = U_MG * TPU
G_MG = NZ
G_GP = G_MG + 4 * NCH
G_BR = G_GP + 2 + NCH
G_WO = G_BR + 4 * NCH
G_FF = G_WO + NCH
G_PG = G_FF + NFG * 2 * NCH
TP_RET, TP_GLU, TP_M = 0, 1, 2
TP_H = TP_M + NCH
TP_FF = TP_H + NCH
TP_P = TP_FF + NFG * NCH
X_LOADS = [(0, TPU - 1), (1, 1)]
X_SQUARES = [(0, TPU - 1), (1, 2)]
X_SCALED = 4
RING = 4
AHEAD = RING - 1
WARM = 4
LOADED = 7

A_BAND, A_POOL, A_QTR, A_KTR, A_CS, A_PCT = 2, 4, 7, 8, 9, 13
A_HEAD = [14 + 4 * i for i in range(NH)]
A_RTR = A_HEAD[-1] + 5
A_RS = [A_RTR + 2 + i for i in range(RH)]
A_U5 = A_RS[-1] + 1
A_RQUAD = A_U5 + 2
A_S5 = [A_RQUAD + 2 + 7 * n + (11 if n >= 4 else 0) for n in range(8)]
A_END = 4 * NCH * TPU


def hybrid_layer(nc, a, out):
    ctx = ExitStack()
    with ctx:
        offset = [-(-nc.sbuf_base // 32) * 32]
        names = [0]

        def at(off, shape, dt=F32):
            names[0] += 1
            return nc.alloc_sbuf_tensor_at(f"sb{names[0]}", [P, *shape], dt, offset=off).ap()

        def size(shape):
            return 4 * int(np.prod(shape))

        class Region:

            def __init__(self, off, nbytes):
                self.off, self.end = off, off + nbytes

            def __call__(self, *shape, dt=F32):
                off, self.off = self.off, -(-(self.off + size(shape)) // 32) * 32
                assert self.off <= self.end, (self.off, self.end)
                return at(off, shape, dt)

        def region(nbytes):
            off = offset[0]
            offset[0] += nbytes
            return off, nbytes

        KB = 1024
        always = Region(*region(54 * KB))
        ra = region(32 * KB)
        rb = region(32 * KB)
        rc = region(ZS * 2 * 4)
        rd = region(nc.sbuf_top - offset[0] - 32)

        raw = always(RING, TK * CW)
        whi = always(RING, TK * CW, dt=F32R)
        wlo = always(RING, TK * CW, dt=F32R)
        ident = always(P)
        g_mix = always(KT)
        g_mlp = always(KT)
        s5_d = always(4)
        rstd = always(3, TT)
        ssq = always(3, TT)
        ssq_last = always(TT, NCH)
        p_raw = always(TK, S)
        s5p = always(3, ST)
        small = always(40, ST)

        r = Region(*ra)
        u_hi, u_lo = r(KT, S, dt=F32R), r(KT, S, dt=F32R)
        r = Region(*ra)
        v_hi, v_lo = r(KT, S, dt=F32R), r(KT, S, dt=F32R)
        r = Region(*rb)
        o_hi, o_lo = r(KT, S, dt=F32R), r(KT, S, dt=F32R)
        r = Region(*rb)
        f_hi, f_lo = r(KT, S, dt=F32R), r(KT, S, dt=F32R)
        r = Region(*rc)
        z = r(TT, ZS)
        r = Region(*rc)
        m_hi, m_lo = r(KT, S, dt=F32R), r(KT, S, dt=F32R)
        r = Region(*rd)
        xin = r(TT, D)
        xt = r(KT, S)
        xsq = r(TT, D)
        r = Region(*rd)
        y_hi, y_lo = r(4, S, dt=F32R), r(4, S, dt=F32R)
        s5_b0 = r(2, 4, P)
        s5_c = r(2, ST, 32)
        gstage = r(2, TT * CW)
        mix_at, mix_end = r.off, rd[0] + rd[1]
        m = Region(rd[0], 20 * KB)
        w_cmp = m(32, P)
        kv_ct = m(NG, S)
        m = Region(rd[0], 8 * KB)
        rot = m(2, TT, P)
        rtmp = m(BW)
        m = Region(mix_at, mix_end - mix_at)
        band = m(4, 2, S)
        w_pool = m(4, P)
        pool_s = m(4)
        pool_t = m(4, S)
        s5_tmp = m(2, 8, TH // 2)
        m = Region(mix_at, mix_end - mix_at)
        q_t = m(4, S)
        k_t = m(2, S)
        kvc = m(NG, R, CP)
        xg = m(NG, P)
        xk = m(P)
        kc_t = m(CP)
        pc = m(TT, NH, CP)
        pc_t = m(NG, TT, P)
        ngate = m(TT, 3 * NH)
        cmask = m(2, TT, CP)
        tri = m(P)
        prob = m(2, 6 * P)
        prob_t = m(2, 6 * P)
        stat = m(NH, 16)
        cstat = m(4, TT, NH)
        m = Region(mix_at, mix_end - mix_at)
        decay = m(RH, 3 * P)
        rq_t = m(RH, S)
        rk_t = m(RH, S)
        rs_t = m(2, 3 * P)
        rgate = m(TT, BW)
        ry = m(TT, BW)
        rjunk = m(P)
        rstat = m(3, TT * RH)
        m = Region(mix_at, mix_end - mix_at)
        u5_t = m(4, S)
        rot_c = [at(rb[0] + size((4, S)), [8, TH]), m(8, TH)]
        rot_s = [at(rb[0] + size((KT + 4, S)), [8, TH]), m(8, TH)]
        vr, vi, t1, t2 = m(4, TH), m(4, TH), m(4, TH), m(4, TH)
        sr, si = m(4, TH), m(4, TH)
        y5 = m(S)
        top = (mix_end - size((2, 4, P))) // 32 * 32
        assert m.off <= top
        s5_b = [s5_b0, at(top, [2, 4, P])]
        r = Region(top, mix_end - top)
        p_hi, p_lo = r(TK, S, dt=F32R), r(TK, S, dt=F32R)
        r = Region(*rd)
        scratch = r(3, TT * CW)
        prodt, merged = scratch[:, 0, :], scratch[:, 1, :]
        relu = [scratch[:, 1, :], scratch[:, 2, :]]
        junk = at(rd[0], [D])
        pp = r(TT, D)
        gates_off = r.off
        gates = r(4, TT * CW)
        glu_s, glu_o = scratch[:, 2, :], r(TT * CW)
        assert r.off <= top
        h = at(gates_off, [TT, D])
        pgate = at(rb[0], [4, TT * CW])
        g_fin = at(rc[0], [D])

        psum = [ctx.enter_context(nc.psum_tensor(f"ps{i}", [P, 2 * CW], F32)) for i in range(4)]
        acc = psum[:2]
        aux = psum[2:]

        def sem(name):
            return ctx.enter_context(nc.semaphore(name))

        raw_in = [sem(f"raw_in{i}") for i in range(RING)]
        hi_done = sem("hi_done")
        lo_done = sem("lo_done")
        tile_used = sem("tile_used")
        grp_free = sem("grp_free")
        tp_in = sem("tp_in")
        tp_hi = sem("tp_hi")
        tp_lo = sem("tp_lo")
        x_in = [sem(f"x_in{i}") for i in range(TT)]
        xt_in = [sem(f"xt_in{i}") for i in range(TPU)]
        g_in = sem("g_in")
        zeros_done = sem("zeros_done")
        x_lo = sem("x_lo")
        x_hi = sem("x_hi")
        p_in = sem("p_in")
        const_in = sem("const_in")
        pool_in = sem("pool_in")
        cmp_in = sem("cmp_in")
        mask_in = sem("mask_in")
        ret_in = sem("ret_in")
        h_in = sem("h_in")
        fin_in = sem("fin_in")
        s5_in = sem("s5_in")
        s5_b_in = [sem(f"s5_b_in{i}") for i in range(2)]
        rot_in = sem("rot_in")
        gate_out = [sem(f"gate_out{i}") for i in range(2)]
        gate_in = [sem(f"gate_in{i}") for i in range(4)]
        gate_used = sem("gate_used")
        h_done = sem("h_done")
        h_weighted = sem("h_weighted")
        last_ssq = sem("last_ssq")
        out_dve = sem("out_dve")
        out_act = sem("out_act")
        out_sem = sem("out_stored")
        ssq_done = sem("ssq_done")
        var_done = sem("var_done")
        std_done = sem("std_done")
        rstd_done = sem("rstd_done")
        pt_hi = sem("pt_hi")
        pt_lo = sem("pt_lo")
        dve = sem("dve_step")
        sg = {n: sem(n) for n in (
            "pool_band pool_copied pool_mixed pool_hi pool_lo "
            "cmp_tr cmp_copied cmp_sum cmp_sb xg_tr xg_sb kc_tr kc_sb q_tr q_sb k_tr k_sb "
            "ngate_done cs_done cs_sub cs_exp pc_done pc_tr pc_sb "
            "sc_done sc_max sc_exp sc_scaled pt_tr pt_sb pv_done nsa_hi nsa_lo "
            "rot_done rq_tr rq_sb rk_tr rk_sb rs_done rs_dec ry_done ry_ssq ry_var ry_std rgate_done ret_done "
            "s5_dt s5_arg s5_exp s5_th s5_sin u5_tr u5_sb bu_done bu_used sh_done c_done y5_done y5_gelu y5_hi y5_lo "
            "glu_done sq_done merged_done").split()}

        C = CW

        def cols(w, r0, c0, width=C):
            rows = slice(r0, r0 + TK * P) if isinstance(r0, int) else bass.ds(r0, TK * P)
            cs = slice(c0, c0 + width) if isinstance(c0, int) else bass.ds(c0, width)
            return w[rows, cs].rearrange("(k p) n -> p k n", p=P)

        def load_tile(sp, u, j, src, width=C):
            if not isinstance(u, int) or u * TPU + j >= RING:
                sp.wait_ge(lo_done, u * TPU + (j - RING + 1))
            s = j % RING
            sp.dma_start(raw[:, s, :].rearrange("p (k n) -> p k n", k=TK)[:, :, 0:width], src)\
                .then_inc(raw_in[s], 16)

        def split_hi(act, u, j):
            if isinstance(u, int) and u * TPU + j >= TILES:
                return
            act.wait_ge(raw_in[j % RING], u * (16 * TPU // RING) + 16 * (j // RING + 1))
            if not isinstance(u, int) or u * TPU + j >= RING:
                act.wait_ge(tile_used, u * TPU + (j - RING + 1))
            act.activation(whi[:, j % RING, :], raw[:, j % RING, :], ACT.Copy).then_inc(hi_done, 1)

        def split_lo(eng, u, j):
            if isinstance(u, int) and u * TPU + j >= TILES:
                return
            eng.wait_ge(hi_done, u * TPU + (j + 1))
            eng.tensor_tensor(wlo[:, j % RING, :], raw[:, j % RING, :], whi[:, j % RING, :].bitcast(F32),
                              ALU.subtract).then_inc(lo_done, 1)

        def products(pe, u, j, g, par, x_hi, x_lo, kt, first, last, width=C):
            if first:
                if not isinstance(g, int) or g >= 2:
                    pe.wait_ge(grp_free, 2 * g - 2)
            pe.wait_ge(lo_done, u * TPU + (j + 1))
            s = j % RING
            for k in range(TK):
                w_h = whi[:, s, k * C:k * C + width]
                w_l = wlo[:, s, k * C:k * C + width]
                for tt in range(TT):
                    o = acc[par][:, tt * C:tt * C + width]
                    xh = x_hi[:, kt + k, tt * P:(tt + 1) * P]
                    xl = x_lo[:, kt + k, tt * P:(tt + 1) * P]
                    pe.matmul(o, xh, w_h, start=first and k == 0, stop=False)
                    pe.matmul(o, xh, w_l, start=False, stop=False)
                    mm = pe.matmul(o, xl, w_h, start=False, stop=last and k == TK - 1)
            mm.then_inc(tile_used, 1)

        def group_ready(eng, u, j):
            eng.wait_ge(tile_used, u * TPU + (j + 1))

        def quad_in(pe, n, par, src):
            if not isinstance(n, int) or n >= 2:
                pe.wait_ge(tp_lo, n - 1)
            for k in range(4):
                for tt in range(TT):
                    mm = pe.transpose(aux[par][:, k * S + tt * P:k * S + (tt + 1) * P], src(k, tt), ident[:, :])
            mm.then_inc(tp_in, 1)

        def quad_hi(act, n, par, dst, scale=None):
            act.wait_ge(tp_in, n + 1)
            if scale is None:
                act.activation(dst.rearrange("p k t -> p (k t)"), aux[par][:, :], ACT.Copy).then_inc(tp_hi, 1)
                return
            for k in range(4):
                i = act.activation(dst[:, k, :], aux[par][:, k * S:(k + 1) * S], ACT.Copy, scale=scale[:, k:k + 1])
            i.then_inc(tp_hi, 1)

        def quad_lo(v, n, par, dst, hi, scale=None):
            v.wait_ge(tp_hi, n + 1)
            if scale is None:
                v.tensor_tensor(dst.rearrange("p k t -> p (k t)"), aux[par][:, :],
                                hi.rearrange("p k t -> p (k t)").bitcast(F32), ALU.subtract).then_inc(tp_lo, 1)
                return
            for k in range(4):
                i = v.scalar_tensor_tensor(out=dst[:, k, :], in0=aux[par][:, k * S:(k + 1) * S],
                                           scalar=scale[:, k:k + 1], in1=hi[:, k, :].bitcast(F32),
                                           op0=ALU.mult, op1=ALU.subtract)
            i.then_inc(tp_lo, 1)

        def features(x, tt, k):
            return x[:, tt, k * P:(k + 1) * P]

        def interleaved(step):
            at_tile = [0]

            def until(n):
                while at_tile[0] < min(n, A_END):
                    step(at_tile[0])
                    at_tile[0] += 1
            return until

        gate_mem = nc.dram_tensor("gate_mem", (4 * NCH, P, TT * CW), F32, kind="Internal").ap()
        block = ctx.enter_context(nc.Block())

        @block.sync
        def _(sp):
            sp.dma_start(g_mix[:, :], a["g_mix"]).then_inc(g_in, 16)
            for i in range(NZ):
                width = C if i < NZ - 1 else ZLAST
                for j in range(TPU):
                    if i == 0:
                        sp.dma_start(xt[:, TK * j:TK * (j + 1), :], cols(a["xt"], j * TK * P, 0, S))\
                            .then_inc(xt_in[j], 16)
                    load_tile(sp, i, j, cols(a["w_mix"], j * TK * P, i * C, width), width)
                    if (i, j) in X_LOADS:
                        tt = X_LOADS.index((i, j))
                        sp.dma_start(xin[:, tt, :], a["x"][tt * P:(tt + 1) * P, :]).then_inc(x_in[tt], 16)
                if i == 1:
                    sp.dma_start(s5p[:, :, :], a["s5p"]).then_inc(const_in, 16)
                    sp.dma_start(ident[:, :], a["ident"]).then_inc(const_in, 16)
                    sp.dma_start(g_mlp[:, :], a["g_mlp"]).then_inc(const_in, 16)
                    sp.dma_start(s5_d[:, :], a["s5_d"]).then_inc(const_in, 16)
                    sp.dma_start(p_raw[:, :, :], a["pt"].rearrange("(k p) t -> p k t", p=P)).then_inc(p_in, 16)
                if i == 3:
                    sp.wait_ge(x_lo, TPU)
                    sp.wait_ge(ssq_done, TT)
                    sp.dma_start(w_cmp[:, :, :], a["w_cmp"]).then_inc(cmp_in, 16)
                    sp.dma_start(pool_s[:, :], a["pool_scale"]).then_inc(pool_in, 16)
                if i == 4:
                    sp.dma_start(band[:, :, :, :], a["band"]).then_inc(pool_in, 16)
                if i == 5:
                    sp.dma_start(w_pool[:, :, :], a["w_pool"].rearrange("g c d -> c g d")).then_inc(pool_in, 16)

            def gate_tile(t):
                i, j = t // TPU, t % TPU
                load_tile(sp, U_MG + i, j, cols(a["w_in"], j * TK * P, ZS + (i % 4) * D + (i // 4) * C))
                if j == LOADED and i:
                    gate_store(i - 1)

            def gate_store(i):
                sp.wait_ge(grp_free, 2 * (G_MG + i + 1))
                sp.dma_start(gate_mem[i], gstage[:, i % 2, :]).then_inc(gate_out[i % 2], 16)

            until = interleaved(gate_tile)
            until(A_QTR + LOADED)
            sp.wait_ge(sg["pool_lo"], 1)
            sp.wait_ge(sg["cmp_sum"], 1)
            sp.dma_start(cmask[:, :, :, :], a["cmask"]).then_inc(mask_in, 16)
            sp.dma_start(tri[:, :], a["tri"]).then_inc(mask_in, 16)
            sp.dma_start(rot[:, :, :, :], a["rot"]).then_inc(rot_in, 16)
            sp.dma_start(s5_b[0][:, :, :, :], a["s5_b"][0]).then_inc(s5_b_in[0], 16)
            sp.dma_start(s5_c[:, :, :, :], a["s5_c"]).then_inc(s5_in, 16)
            until(A_RTR + LOADED - 2)
            sp.wait_ge(sg["nsa_lo"], 2)
            sp.dma_start(decay[:, :, :], a["decay"]).then_inc(ret_in, 16)
            for q in range(1, 4):
                until(A_S5[(0, 1, 3)[q - 1]] + 2)
                if q == 1:
                    sp.wait_ge(tp_lo, TP_RET + 1)
                else:
                    sp.wait_ge(sg["bu_done"], TT * (q - 1))
                sp.dma_start(s5_b[q % 2][:, :, :, :], a["s5_b"][q]).then_inc(s5_b_in[q % 2], 16)
            until(A_END)
            for j in range(TPU):
                if j < 4:
                    src = cols(a["w_glu"], (j % 2) * TK * P, (1 - j // 2) * C)
                else:
                    src = cols(a["w_pp"], 0, (j - 4) * C)
                load_tile(sp, U_GP, j, src)
            gate_store(4 * NCH - 1)

            def gate_load(n, b):
                sp.dma_start(gates[:, b, :], gate_mem[4 * n + b]).then_inc(gate_in[b], 16)

            for n in range(NCH):
                for j in range(TPU):
                    load_tile(sp, U_BR + n, j, cols(a["w_branch"], j * TK * P, n * C))
                    if n == 0 and j == 0:
                        for i in range(2):
                            sp.wait_ge(gate_out[i], 16 * 2 * NCH)
                        sp.wait_ge(sg["y5_lo"], 4)
                    if n == 0 and j < 4:
                        gate_load(0, j)
                    if n and j % 2 == 0:
                        sp.wait_ge(gate_used, 4 * (n - 1) + j // 2 + 1)
                        gate_load(n, j // 2)
            for n in range(NCH):
                for j in range(TPU):
                    load_tile(sp, U_WO + n, j, cols(a["w_out"], j * TK * P, n * C))
                if n == 0:
                    sp.wait_ge(sg["merged_done"], NCH)
                    sp.dma_start(h[:, :, :], a["x"].rearrange("(t p) d -> p t d", p=P)).then_inc(h_in, 16)
            with sp.Fori(0, NFG) as g:
                for n in range(NCH):
                    for j in range(TPU):
                        load_tile(sp, g * (2 * NCH) + (U_FF + n), j, cols(a["w_up"], j * TK * P, g * D + n * C))
                for n in range(NCH):
                    for j in range(TPU):
                        load_tile(sp, g * (2 * NCH) + (U_FF + NCH + n), j,
                                  cols(a["w_down"], g * D + j * TK * P, n * C))
            sp.dma_start(g_fin[:, :], a["g_final"]).then_inc(fin_in, 16)
            for n in range(NCH):
                for j in range(TPU):
                    load_tile(sp, U_PG + n, j, cols(a["w_pg"], j * TK * P, n * C))
            for n in range(NCH):
                for tt in range(TT):
                    sp.wait_ge((out_dve, out_act)[tt], n + 1)
                    sp.dma_start(out[tt * P:(tt + 1) * P, n * C:(n + 1) * C], h[:, tt, n * C:(n + 1) * C])\
                        .then_inc(out_sem, 16)
            sp.wait_ge(out_sem, 16 * TT * NCH)

        @block.tensor
        def _(pe):
            pe.wait_ge(zeros_done, 1)
            for _ in range(WARM):
                pe.matmul(aux[0][:, 0:C], z[:, 0, 0:P], z[:, 0, 0:C], start=True, stop=True)
            for i in range(NZ):
                width = C if i < NZ - 1 else ZLAST
                for j in range(TPU):
                    if i == 0:
                        pe.wait_ge(x_lo, j + 1)
                    products(pe, i, j, i, i % 2, u_hi, u_lo, j * TK, j == 0, j == TPU - 1, width)

            def hidden_in(k):
                pe.wait_ge(grp_free, 2 * (G_WO + k + 1))
                quad_in(pe, TP_H + k, (TP_H + k) % 2, lambda kk, tt: features(h, tt, 4 * k + kk))

            def last_in(k):
                pe.wait_ge(grp_free, 2 * (G_PG - NCH + k + 1))
                quad_in(pe, TP_P + k, (TP_P + k) % 2, lambda kk, tt: features(h, tt, 4 * k + kk))

            def gate_tile(t):
                i, j = t // TPU, t % TPU
                products(pe, U_MG + i, j, G_MG + i, (G_MG + i) % 2, u_hi, u_lo, j * TK, j == 0, j == TPU - 1)

            until = interleaved(gate_tile)
            until(A_BAND)
            pe.wait_ge(grp_free, 2 * NZ)
            pe.wait_ge(const_in, 64)
            pe.wait_ge(pool_in, 48)
            for g in range(4):
                pe.matmul(aux[0][:, g * S:(g + 1) * S], z[:, 0, PL0 + g * P:PL0 + (g + 1) * P],
                          band[:, g, 0, :], start=True, stop=False)
                mm = pe.matmul(aux[0][:, g * S + P:(g + 1) * S], z[:, 1, PL0 + g * P:PL0 + (g + 1) * P],
                               band[:, g, 1, P:S], start=False, stop=True)
            mm.then_inc(sg["pool_band"], 1)
            for g in range(NG):
                for tt in range(TT):
                    mm = pe.transpose(aux[1][:, g * S + tt * P:g * S + (tt + 1) * P],
                                      z[:, tt, KV0 + g * P:KV0 + (g + 1) * P], ident[:, :])
            mm.then_inc(sg["cmp_tr"], 1)
            until(A_POOL)
            pe.wait_ge(sg["pool_copied"], 1)
            for g in range(4):
                mm = pe.matmul(aux[0][:, g * S:(g + 1) * S], w_pool[:, g, :], pool_t[:, g, :], start=True, stop=True)
            mm.then_inc(sg["pool_mixed"], 1)
            pe.wait_ge(cmp_in, 16)
            pe.wait_ge(sg["cmp_copied"], 1)
            o = aux[1][:, C:C + NG * NCMP].rearrange("p (g n) -> p g n", g=NG)
            for l in range(32):
                mm = pe.matmul(o, w_cmp[:, l, :], kv_ct[:, :, l:l + 16 * (NCMP - 1) + 1:16],
                               start=l == 0, stop=l == 31)
            mm.then_inc(sg["cmp_sum"], 1)
            until(A_QTR)
            pe.wait_ge(sg["pool_lo"], 1)
            for k in range(4):
                for tt in range(TT):
                    mm = pe.transpose(aux[0][:, k * S + tt * P:k * S + (tt + 1) * P],
                                      z[:, tt, Q0 + k * P:Q0 + (k + 1) * P], ident[:, :])
            mm.then_inc(sg["q_tr"], 1)
            pe.wait_ge(sg["cmp_sb"], 1)
            for g in range(NG):
                mm = pe.transpose(aux[1][:, g * P:(g + 1) * P], kvc[:, g, :, :], ident[:, :])
            mm.then_inc(sg["xg_tr"], 1)
            until(A_KTR)
            pe.wait_ge(sg["xg_sb"], 1)
            pe.transpose(aux[1][:, C:C + CP], xk[0:CP, :], ident[0:CP, 0:CP]).then_inc(sg["kc_tr"], 1)
            pe.wait_ge(sg["q_sb"], 1)
            for i in range(2):
                c0 = KV0 + (2 + 2 * i) * P
                for tt in range(TT):
                    o = i * S + tt * P
                    mm = pe.transpose(aux[0][:, o:o + P], z[:, tt, c0:c0 + P], ident[:, :])
            mm.then_inc(sg["k_tr"], 1)
            until(A_CS)
            pe.wait_ge(sg["kc_sb"], 1)
            for g in range(NG):
                for tt in range(TT):
                    for rr in range(R):
                        o = g * C + (tt * R + rr) * CP
                        mm = pe.matmul(aux[1][:, o:o + CP], q_t[g * DH:(g + 1) * DH, rr, tt * P:(tt + 1) * P],
                                       kc_t[g * DH:(g + 1) * DH, :], start=True, stop=True)
            mm.then_inc(sg["cs_done"], 1)
            pe.wait_ge(sg["k_sb"], 1)

            def scores(hd):
                lo = DH * (hd % 2)
                if hd >= 1:
                    pe.wait_ge(sg["sc_exp"], 4 * hd)
                for tt in (1, 0):
                    for i in range(2):
                        n = (tt + 1) * P
                        o = (0 if tt else C) + i * n
                        mm = pe.matmul(aux[0][:, o:o + n], q_t[lo:lo + DH, hd // 2, tt * P:(tt + 1) * P],
                                       k_t[lo:lo + DH, i, 0:n], start=True, stop=True)
                mm.then_inc(sg["sc_done"], 1)

            scores(0)
            until(A_PCT)
            pe.wait_ge(sg["pc_done"], 1)
            for g in range(NG):
                for tt in range(TT):
                    o = (g * TT + tt) * P
                    mm = pe.transpose(aux[1][:, o:o + P], pc[:, tt, g * R:(g + 1) * R, :], ident[:, :])
            mm.then_inc(sg["pc_tr"], 1)
            for hd in range(NH):
                until(A_HEAD[hd] + 3)
                pe.wait_ge(sg["sc_scaled"], hd + 1)
                if hd == 0:
                    pe.wait_ge(sg["pc_sb"], 1)
                if hd >= 1:
                    pe.wait_ge(sg["pt_sb"], 2 * hd)
                blocks = [(i, b) for i in range(2) for b in range(3)]
                for n, (i, b) in enumerate(blocks):
                    src = prob[:, hd % 2, :]
                    s0 = 4 * P + i * P if b == 0 else i * 2 * P + (b - 1) * P
                    o = aux[1][:, n * P:(n + 1) * P] if n < 4 else aux[0][:, C + 2 * P + (n - 4) * P:C + 2 * P + (n - 3) * P]
                    mm = pe.transpose(o, src[:, s0:s0 + P], ident[:, :])
                mm.then_inc(sg["pt_tr"], 1)
                until(A_HEAD[hd] + 4)
                pe.wait_ge(sg["pt_sb"], 2 * hd + 2)
                if hd + 1 < NH:
                    scores(hd + 1)
                lo = DH * (hd % 2)
                g = hd % 2
                if hd == 4:
                    pe.wait_ge(sg["nsa_lo"], 1)
                o = aux[1][lo:lo + DH, C + (hd // 2 % 2) * S:C + (hd // 2 % 2 + 1) * S]
                first = True
                for i in range(2):
                    v0 = KV0 + (3 + 2 * i) * P + g * DH
                    for kt in range(2):
                        b = prob_t[:, hd % 2, (3 * i + 2 * kt) * P:(3 * i + 2 + kt) * P]
                        pe.matmul(o[:, kt * P:S], z[:, kt, v0:v0 + DH], b, start=first, stop=False)
                        first = False
                rr = hd // 2
                pe.matmul(o, xg[rr * CP:(rr + 1) * CP, g, DH:P], pc_t[rr * CP:(rr + 1) * CP, g, :, :],
                          start=False, stop=True).then_inc(sg["pv_done"], 1)
            until(A_RTR)
            pe.wait_ge(sg["nsa_lo"], 2)
            pe.wait_ge(sg["rot_done"], 4)
            for k in range(4):
                for tt in range(TT):
                    mm = pe.transpose(aux[0][:, k * S + tt * P:k * S + (tt + 1) * P],
                                      z[:, tt, RQ0 + k * P:RQ0 + (k + 1) * P], ident[:, :])
            mm.then_inc(sg["rq_tr"], 1)
            for k in range(4):
                for tt in range(TT):
                    mm = pe.transpose(aux[1][:, k * S + tt * P:k * S + (tt + 1) * P],
                                      z[:, tt, RK0 + k * P:RK0 + (k + 1) * P], ident[:, :])
            mm.then_inc(sg["rk_tr"], 1)

            def ret_scores(hd):
                if hd >= 2:
                    pe.wait_ge(sg["rs_dec"], hd - 1)
                b = (hd % 2) * C
                pe.matmul(aux[0][:, b:b + S], rk_t[:, hd, 0:P], rq_t[:, hd, :], start=True, stop=True)
                pe.matmul(aux[0][:, b + S:b + 3 * P], rk_t[:, hd, P:S], rq_t[:, hd, P:S],
                          start=True, stop=True).then_inc(sg["rs_done"], 1)

            until(A_RS[0])
            pe.wait_ge(sg["rq_sb"], 1)
            pe.wait_ge(sg["rk_sb"], 1)
            ret_scores(0)
            for hd in range(RH):
                if hd + 1 < RH:
                    ret_scores(hd + 1)
                until(A_RS[hd] + 1)
                pe.wait_ge(sg["rs_dec"], hd + 1)
                if hd:
                    pe.wait_ge(sg["ry_ssq"], TT * hd)
                s_ = rs_t[:, hd % 2, :]
                v = lambda tt: z[:, tt, RV0 + hd * P:RV0 + (hd + 1) * P]
                pe.matmul(aux[1][:, hd * P:(hd + 1) * P], s_[:, 0:P], v(0), start=True, stop=True)
                pe.matmul(aux[1][:, C + hd * P:C + (hd + 1) * P], s_[:, P:2 * P], v(0), start=True, stop=False)
                pe.matmul(aux[1][:, C + hd * P:C + (hd + 1) * P], s_[:, 2 * P:3 * P], v(1),
                          start=False, stop=True).then_inc(sg["ry_done"], 1)
            until(A_U5)
            for k in range(4):
                for tt in range(TT):
                    mm = pe.transpose(aux[0][:, k * S + tt * P:k * S + (tt + 1) * P],
                                      z[:, tt, S50 + k * P:S50 + (k + 1) * P], ident[:, :])
            mm.then_inc(sg["u5_tr"], 1)
            until(A_RQUAD)
            pe.wait_ge(sg["ret_done"], 1)
            quad_in(pe, TP_RET, 1, lambda k, tt: features(ry, tt, k))
            until(A_S5[0] - 1)
            pe.wait_ge(sg["u5_sb"], 1)
            def s5_inputs(n):
                q, hf = n // TT, n % TT
                if n:
                    pe.wait_ge(sg["bu_used"], n)
                if hf == 0:
                    pe.wait_ge(s5_b_in[q % 2], 16 * (q // 2 + 1))
                for i in range(4):
                    for im in range(2):
                        o = im * C + i * P
                        mm = pe.matmul(aux[0][:, o:o + P], s5_b[q % 2][:, im, i, :], u5_t[:, q, hf * P:(hf + 1) * P],
                                       start=True, stop=True)
                mm.then_inc(sg["bu_done"], 1)

            def s5_outputs(n):
                q, hf = n // TT, n % TT
                if n == 0:
                    pe.wait_ge(tp_lo, TP_RET + 1)
                    pe.wait_ge(s5_in, 16)
                if hf == 0 and q >= 2:
                    pe.wait_ge(sg["y5_done"], q - 1)
                pe.wait_ge(sg["sh_done"], n + 1)
                for i in range(4):
                    o = aux[1][32 * i:32 * i + 32, (q % 2) * C + hf * P:(q % 2) * C + (hf + 1) * P]
                    pe.matmul(o, s5_c[:, 0, 4 * q + i, :], vr[:, i, :], start=True, stop=False)
                    mm = pe.matmul(o, s5_c[:, 1, 4 * q + i, :], vi[:, i, :], start=False, stop=True)
                mm.then_inc(sg["c_done"], 1)

            s5_inputs(0)
            for n in range(4 * TT):
                until(A_S5[n] + 4)
                if n + 1 < 4 * TT:
                    s5_inputs(n + 1)
                until(A_S5[n] + (7 if n < 7 else 8))
                s5_outputs(n)
            until(A_END)
            pe.wait_ge(sg["y5_lo"], 4)
            for j in range(TPU):
                if j == 4:
                    pe.wait_ge(pt_lo, 1)
                if j < 4:
                    products(pe, U_GP, j, G_GP + j // 2, (G_GP + j // 2) % 2, y_hi, y_lo, (j % 2) * TK,
                             j % 2 == 0, j % 2 == 1)
                else:
                    products(pe, U_GP, j, G_GP + j - 2, (G_GP + j - 2) % 2, p_hi, p_lo, 0, True, True)
                if j == 6:
                    pe.wait_ge(sg["glu_done"], 1)
                    quad_in(pe, TP_GLU, 1, lambda k, tt: glu_o[:, tt * C + k * P:tt * C + (k + 1) * P])

            def merged_in(n):
                pe.wait_ge(sg["merged_done"], n + 1)
                quad_in(pe, TP_M + n, n % 2, lambda k, tt: merged[:, tt * C + k * P:tt * C + (k + 1) * P])

            for n in range(NCH):
                for j in range(TPU):
                    g = G_BR + 4 * n + j // 2
                    if n == 0 and j == 2:
                        pe.wait_ge(tp_lo, TP_GLU + 1)
                    products(pe, U_BR + n, j, g, g % 2, o_hi, o_lo, j * TK, j % 2 == 0, j % 2 == 1)
                    if j == 1 and n:
                        merged_in(n - 1)
            for n in range(NCH):
                for j in range(TPU):
                    g = G_WO + n
                    if n == 0 and j in (0, TPU - 2):
                        pe.wait_ge(tp_lo, TP_M + (NCH if j else NCH - 1))
                    products(pe, U_WO + n, j, g, g % 2, m_hi, m_lo, j * TK, j == 0, j == TPU - 1)
                    if n == 0 and j == 1:
                        merged_in(NCH - 1)
                    if j == 3 and n:
                        hidden_in(n - 1)
            def mlp_group(g, first, final):
                for n in range(2 * NCH):
                    up = n < NCH
                    for j in range(TPU):
                        if first and n == 0 and j in (0, TPU - 2):
                            pe.wait_ge(tp_lo, TP_H + (NCH if j else NCH - 1))
                        if n == NCH and j in (0, TPU - 2):
                            pe.wait_ge(tp_lo, g * NCH + (TP_FF + (NCH if j else NCH - 1)))
                        products(pe, g * (2 * NCH) + (U_FF + n), j, g * (2 * NCH) + (G_FF + n), (G_FF + n) % 2,
                                 v_hi if up else f_hi, v_lo if up else f_lo, j * TK, j == 0, j == TPU - 1)
                        if first and n == 0 and j == 3:
                            hidden_in(NCH - 1)
                        if j == 3 and 1 <= n <= NCH:
                            pe.wait_ge(sg["sq_done"], g * NCH + n)
                            rl = relu[(n - 1) % 2]
                            quad_in(pe, g * NCH + (TP_FF + n - 1), (TP_FF + n - 1) % 2,
                                    lambda k, tt: rl[:, tt * C + k * P:tt * C + (k + 1) * P])
                        if final and j == 3 and n > NCH:
                            last_in(n - NCH - 1)

            mlp_group(0, True, False)
            with pe.Fori(1, NFG - 1) as g:
                mlp_group(g, False, False)
            mlp_group(NFG - 1, False, True)
            for n in range(NCH):
                for j in range(TPU):
                    g = G_PG + n
                    if n == 0 and j in (0, TPU - 2):
                        pe.wait_ge(tp_lo, TP_P + (NCH if j else NCH - 1))
                    products(pe, U_PG + n, j, g, g % 2, v_hi, v_lo, j * TK, j == 0, j == TPU - 1)
                    if n == 0 and j == 3:
                        last_in(NCH - 1)

        @block.scalar
        def _(act):
            act.wait_ge(zeros_done, 1)
            act.activation(rstd[:, 0, 0:1], z[:, 0, 0:1], ACT.Copy)
            act.wait_ge(g_in, 16)

            def x_high(j):
                act.wait_ge(xt_in[j], 16)
                for k in range(TK * j, TK * (j + 1)):
                    i = act.activation(u_hi[:, k, :], xt[:, k, :], ACT.Copy, scale=g_mix[:, k:k + 1])
                i.then_inc(x_hi, 1)

            def leave(i):
                group_ready(act, i, TPU - 1)
                width = C if i < NZ - 1 else ZLAST
                act.activation(z[:, 0, i * C:i * C + width], acc[i % 2][:, 0:width], ACT.Copy,
                               scale=rstd[:, 0, 0:1]).then_inc(grp_free, 1)

            for j in range(TPU):
                x_high(j)
                split_hi(act, 0, j)
            for i in range(NZ):
                for j in range(TPU):
                    if (i, j) in X_SQUARES:
                        tt = X_SQUARES.index((i, j))
                        act.wait_ge(x_in[tt], 16)
                        act.activation(xsq[:, tt, :], xin[:, tt, :], ACT.Square, accum_out=ssq[:, 0, tt:tt + 1])\
                            .then_inc(ssq_done, 1)
                    if (i, j) == (1, X_SCALED):
                        act.wait_ge(var_done, 1)
                        act.activation(rstd[:, 0, :], ssq[:, 0, :], ACT.Sqrt).then_inc(std_done, 1)
                        act.wait_ge(rstd_done, 1)
                        leave(0)
                    if i or j + AHEAD >= TPU:
                        split_hi(act, i, j + AHEAD)
                if i:
                    leave(i)
                if i == 2:
                    act.wait_ge(const_in, 64)
                    act.activation(small[:, 0, :], s5p[:, 2, :], ACT.Exp).then_inc(sg["s5_dt"], 1)
                if i == 3:
                    act.wait_ge(sg["s5_arg"], 1)
                    act.activation(small[:, 2, :], small[:, 1, :], ACT.Exp).then_inc(sg["s5_exp"], 1)
                if i == 4:
                    act.wait_ge(sg["s5_th"], 1)
                    act.activation(small[:, 8, :], small[:, 6, :], ACT.Sin).then_inc(sg["s5_sin"], 1)
                    act.activation(small[:, 9, :], small[:, 7, :], ACT.Sin).then_inc(sg["s5_sin"], 1)

            def gate_tile(t):
                i, j = t // TPU, t % TPU
                split_hi(act, U_MG + i, j + AHEAD)
                if j == TPU - 1:
                    group_ready(act, U_MG + i, j)
                    if i >= 2:
                        act.wait_ge(gate_out[i % 2], 16 * (i // 2))
                    for tt in range(TT):
                        act.activation(gstage[:, i % 2, tt * C:(tt + 1) * C],
                                       acc[(G_MG + i) % 2][:, tt * C:(tt + 1) * C],
                                       ACT.Sigmoid, scale=rstd[:, 0, tt:tt + 1]).then_inc(grp_free, 1)

            until = interleaved(gate_tile)
            until(A_BAND)
            act.wait_ge(sg["pool_band"], 1)
            act.activation(pool_t[:, :, :].rearrange("p g t -> p (g t)"), aux[0][:, :], ACT.Copy)\
                .then_inc(sg["pool_copied"], 1)
            until(A_POOL)
            act.wait_ge(sg["pool_mixed"], 1)
            for g in range(4):
                act.activation(o_hi[:, 8 + g, :], aux[0][:, g * S:(g + 1) * S], ACT.Copy, scale=pool_s[:, g:g + 1])\
                    .then_inc(sg["pool_hi"], 1)
            until(A_QTR)
            act.wait_ge(sg["q_tr"], 1)
            act.activation(q_t[:, :, :].rearrange("p k t -> p (k t)"), aux[0][:, :], ACT.Copy, scale=DH ** -0.5)\
                .then_inc(sg["q_sb"], 1)
            until(A_KTR)
            act.wait_ge(sg["k_tr"], 1)
            act.activation(k_t[:, :, :].rearrange("p k t -> p (k t)"), aux[0][:, 0:2 * S], ACT.Copy).then_inc(sg["k_sb"], 1)
            act.activation(ngate[:, :, :], z[:, :, NG0:NG0 + 3 * NH], ACT.Sigmoid).then_inc(sg["ngate_done"], 1)
            until(A_CS + 2)
            act.wait_ge(sg["cs_sub"], 1)
            act.activation(pc[:, :, :, :].rearrange("p t h n -> p (t h n)"),
                           pc[:, :, :, :].rearrange("p t h n -> p (t h n)"), ACT.Exp).then_inc(sg["cs_exp"], 1)

            for hd in range(NH):
                until(A_HEAD[hd] + 1)
                act.wait_ge(sg["sc_max"], hd + 1)
                if hd >= 2:
                    act.wait_ge(sg["pt_tr"], hd - 1)
                for n, (o, w) in enumerate(((0, S), (S, S), (C, P), (C + P, P))):
                    act.activation(prob[:, hd % 2, o:o + w], aux[0][:, o:o + w], ACT.Exp, bias=stat[:, hd, n:n + 1],
                                   accum_out=stat[:, hd, 4 + n:5 + n]).then_inc(sg["sc_exp"], 1)
                until(A_HEAD[hd] + 3)
                act.wait_ge(sg["pt_tr"], hd + 1)
                if hd >= 2:
                    act.wait_ge(sg["pv_done"], hd - 1)
                act.activation(prob_t[:, hd % 2, 0:C], aux[1][:, 0:C], ACT.Copy).then_inc(sg["pt_sb"], 1)
                act.activation(prob_t[:, hd % 2, C:6 * P], aux[0][:, C + S:2 * C], ACT.Copy).then_inc(sg["pt_sb"], 1)
                if hd % 4 == 3:
                    until(A_HEAD[hd] + 4)
                    act.wait_ge(sg["pv_done"], hd + 1)
                    k = hd // 4 * 2
                    act.activation(o_hi[:, k:k + 2, :].rearrange("p k t -> p (k t)"), aux[1][:, C:2 * C], ACT.Copy)\
                        .then_inc(sg["nsa_hi"], 1)
                    act.wait_ge(sg["nsa_lo"], hd // 4 + 1)
            until(A_RTR)
            act.wait_ge(sg["rq_tr"], 1)
            act.activation(rq_t[:, :, :].rearrange("p k t -> p (k t)"), aux[0][:, :], ACT.Copy).then_inc(sg["rq_sb"], 1)
            act.wait_ge(sg["rk_tr"], 1)
            act.activation(rk_t[:, :, :].rearrange("p k t -> p (k t)"), aux[1][:, :], ACT.Copy).then_inc(sg["rk_sb"], 1)
            until(A_RTR + 1)
            act.activation(rgate[:, :, :], z[:, :, RG0:RG0 + BW], ACT.Silu).then_inc(sg["rgate_done"], 1)
            for hd in range(RH):
                until(A_RS[hd] + 1)
                act.wait_ge(sg["ry_done"], hd + 1)
                for tt in range(TT):
                    if hd or tt:
                        act.wait_ge(sg["ry_ssq"], hd * TT + tt)
                    act.activation(rjunk[:, :], aux[1][:, tt * C + hd * P:tt * C + (hd + 1) * P], ACT.Square,
                                   accum_out=rstat[:, 0, tt * RH + hd:tt * RH + hd + 1]).then_inc(sg["ry_ssq"], 1)
            act.wait_ge(sg["ry_var"], 1)
            act.activation(rstat[:, 1, :], rstat[:, 0, :], ACT.Sqrt).then_inc(sg["ry_std"], 1)
            until(A_RQUAD)
            act.wait_ge(sg["ret_done"], 1)
            quad_hi(act, TP_RET, 1, o_hi[:, 12:16, :])
            act.wait_ge(tp_lo, TP_RET + 1)
            act.wait_ge(sg["u5_tr"], 1)
            act.activation(u5_t[:, :, :].rearrange("p k t -> p (k t)"), aux[0][:, :], ACT.Copy).then_inc(sg["u5_sb"], 1)
            for q in range(4):
                until(A_S5[2 * q + 2] + 5 if q < 3 else A_S5[7] + 9)
                act.wait_ge(sg["y5_done"], q + 1)
                act.activation(y5[:, :], y5[:, :], ACT.Gelu_apprx_tanh).then_inc(sg["y5_gelu"], 1)
                act.wait_ge(sg["y5_gelu"], q + 1)
                act.activation(y_hi[:, q, :], y5[:, :], ACT.Copy).then_inc(sg["y5_hi"], 1)
            act.wait_ge(p_in, 16)
            act.wait_ge(sg["bu_done"], 4 * TT)
            act.activation(p_hi[:, :, :], p_raw[:, :, :], ACT.Copy).then_inc(pt_hi, 1)
            until(A_END)
            for j in range(TPU):
                split_hi(act, U_GP, j + AHEAD)
                if j == 1:
                    group_ready(act, U_GP, 1)
                    act.activation(glu_s, acc[G_GP % 2][:, :], ACT.Sigmoid).then_inc(grp_free, 2)
            quad_hi(act, TP_GLU, 1, o_hi[:, 4:8, :])

            def merged_hi(n):
                quad_hi(act, TP_M + n, n % 2, m_hi[:, 4 * n:4 * n + 4, :])

            def hidden_hi(k):
                quad_hi(act, TP_H + k, (TP_H + k) % 2, v_hi[:, 4 * k:4 * k + 4, :], g_mlp[:, 4 * k:4 * k + 4])

            def last_hi(k):
                quad_hi(act, TP_P + k, (TP_P + k) % 2, v_hi[:, 4 * k:4 * k + 4, :])

            for n in range(NCH):
                for j in range(TPU):
                    split_hi(act, U_BR + n, j + AHEAD)
                    if j == 2 and n:
                        merged_hi(n - 1)
            for n in range(NCH):
                for j in range(TPU):
                    split_hi(act, U_WO + n, j + AHEAD)
                    if n == 0 and j == 2:
                        merged_hi(NCH - 1)
                    if n and j == 4:
                        hidden_hi(n - 1)

            def mlp_group(g, first, final):
                for n in range(2 * NCH):
                    u = g * (2 * NCH) + (U_FF + n)
                    for j in range(TPU):
                        split_hi(act, u, j + AHEAD)
                        if j == 4 and 1 <= n <= NCH:
                            quad_hi(act, g * NCH + (TP_FF + n - 1), (TP_FF + n - 1) % 2, f_hi[:, 4 * n - 4:4 * n, :])
                        if first and n == 0 and j == 4:
                            hidden_hi(NCH - 1)
                            for tt in range(TT):
                                if tt:
                                    act.wait_ge(ssq_done, TT + tt)
                                act.activation(junk[:, :], h[:, tt, :], ACT.Square, accum_out=ssq[:, 1, tt:tt + 1])\
                                    .then_inc(ssq_done, 1)
                        if first and n == 0 and j == TPU - 1:
                            act.wait_ge(var_done, 2)
                            act.activation(rstd[:, 1, :], ssq[:, 1, :], ACT.Sqrt).then_inc(std_done, 1)
                            act.wait_ge(rstd_done, 2)
                        if final and j == 4 and n > NCH:
                            last_hi(n - NCH - 1)
                    if n < NCH:
                        group_ready(act, u, TPU - 1)
                        for tt in range(TT):
                            act.activation(relu[n % 2][:, tt * C:(tt + 1) * C],
                                           acc[(G_FF + n) % 2][:, tt * C:(tt + 1) * C], ACT.Relu,
                                           scale=rstd[:, 1, tt:tt + 1]).then_inc(grp_free, 1)

            mlp_group(0, True, False)
            with act.Fori(1, NFG - 1) as g:
                mlp_group(g, False, False)
            mlp_group(NFG - 1, False, True)

            def last_squares(n):
                for tt in range(TT):
                    act.wait_ge(h_done, TT * n + tt + 1)
                    act.activation(pp[:, tt, n * C:(n + 1) * C], h[:, tt, n * C:(n + 1) * C], ACT.Square,
                                   accum_out=ssq_last[:, tt, n:n + 1]).then_inc(last_ssq, 1)

            for n in range(NCH):
                for j in range(TPU):
                    split_hi(act, U_PG + n, j + AHEAD)
                    if n == 0 and j == 4:
                        last_hi(NCH - 1)
                    if n and j == 4:
                        last_squares(n - 1)
                group_ready(act, U_PG + n, TPU - 1)
                for tt in range(TT):
                    act.activation(pgate[:, n, tt * C:(tt + 1) * C], acc[(G_PG + n) % 2][:, tt * C:(tt + 1) * C],
                                   ACT.Sigmoid).then_inc(grp_free, 1)
            act.activation(pgate[:, 0, 0:1], rstd[:, 1, 0:1], ACT.Sqrt)
            last_squares(NCH - 1)
            act.wait_ge(var_done, 3)
            act.activation(rstd[:, 2, :], ssq[:, 2, :], ACT.Sqrt).then_inc(std_done, 1)
            act.wait_ge(rstd_done, 3)
            act.wait_ge(h_weighted, TT * NCH)
            for n in range(NCH):
                hc = h[:, 1, n * C:(n + 1) * C]
                act.activation(hc, hc, ACT.Copy, scale=rstd[:, 2, 1:2]).then_inc(out_act, 1)

        @block.gpsimd
        def _(gp):
            gp.memset(z[:, 0, 0:C], 0.0).then_inc(zeros_done, 1)

        @block.vector
        def _(v):
            done = [0]

            def link(ins):
                done[0] += 1
                ins.then_inc(dve, 1)
                v.wait_ge(dve, done[0])

            def mean_square(n):
                v.wait_ge(ssq_done, TT * (n + 1))
                v.tensor_scalar(ssq[:, n, :], ssq[:, n, :], 1.0 / D, EPS, ALU.mult, ALU.add).then_inc(var_done, 1)

            def inverse(n):
                v.wait_ge(std_done, n + 1)
                v.reciprocal(rstd[:, n, :], rstd[:, n, :]).then_inc(rstd_done, 1)

            sm = lambda i: small[:, i, :]

            def s5_angles():
                v.wait_ge(sg["s5_dt"], 1)
                v.tensor_tensor(sm(1), s5p[:, 0, :], sm(0), ALU.mult).then_inc(sg["s5_arg"], 1)
                link(v.tensor_tensor(sm(3), s5p[:, 1, :], sm(0), ALU.mult))
                magic = 1.5 * 2.0 ** 23
                link(v.tensor_scalar(sm(4), sm(3), 1.0 / (2 * math.pi), magic, ALU.mult, ALU.add))
                link(v.tensor_scalar(sm(4), sm(4), -magic, None, ALU.add))
                p1 = 6.28125
                p2 = math.floor((2 * math.pi - p1) * 2 ** 20) / 2 ** 20
                p3 = 2 * math.pi - p1 - p2
                src = 3
                for part in (p1, p2, p3):
                    link(v.scalar_tensor_tensor(out=sm(5), in0=sm(4), scalar=-part, in1=sm(src), op0=ALU.mult, op1=ALU.add))
                    src = 5
                top = float(np.nextafter(np.float32(math.pi), np.float32(0)))
                link(v.tensor_scalar(sm(6), sm(5), top, -top, ALU.min, ALU.max))
                link(v.tensor_scalar(sm(7), sm(6), -1.0, None, ALU.mult))
                link(v.tensor_tensor(sm(7), sm(6), sm(7), ALU.max))
                v.tensor_scalar(sm(7), sm(7), -1.0, math.pi / 2, ALU.mult, ALU.add).then_inc(sg["s5_th"], 1)

            def s5_numerator():
                v.wait_ge(sg["s5_sin"], 2)
                v.wait_ge(sg["s5_exp"], 1)
                link(v.tensor_tensor(sm(10), sm(2), sm(9), ALU.mult))
                link(v.tensor_scalar(sm(10), sm(10), -1.0, None, ALU.add))
                link(v.tensor_tensor(sm(11), sm(2), sm(8), ALU.mult))
                link(v.tensor_tensor(sm(12), s5p[:, 0, :], s5p[:, 0, :], ALU.mult))
                link(v.tensor_tensor(sm(13), s5p[:, 1, :], s5p[:, 1, :], ALU.mult))
                link(v.tensor_tensor(sm(14), sm(12), sm(13), ALU.add))
                link(v.reciprocal(sm(14), sm(14)))

            def s5_coefficients():
                link(v.tensor_tensor(sm(12), sm(10), s5p[:, 0, :], ALU.mult))
                link(v.tensor_tensor(sm(13), sm(11), s5p[:, 1, :], ALU.mult))
                link(v.tensor_tensor(sm(12), sm(12), sm(13), ALU.add))
                link(v.tensor_tensor(sm(15), sm(12), sm(14), ALU.mult))
                link(v.tensor_tensor(sm(12), sm(11), s5p[:, 0, :], ALU.mult))
                link(v.tensor_tensor(sm(13), sm(10), s5p[:, 1, :], ALU.mult))
                link(v.tensor_tensor(sm(12), sm(12), sm(13), ALU.subtract))
                link(v.tensor_tensor(sm(16), sm(12), sm(14), ALU.mult))
                link(v.tensor_copy(sm(20), sm(9)))
                link(v.tensor_copy(sm(21), sm(8)))

            def s5_power(k):
                c0, s0, c1, s1 = (20 + 2 * k + i for i in range(4))
                link(v.tensor_tensor(sm(12), sm(c0), sm(c0), ALU.mult))
                link(v.tensor_tensor(sm(13), sm(s0), sm(s0), ALU.mult))
                link(v.tensor_tensor(sm(c1), sm(12), sm(13), ALU.subtract))
                link(v.tensor_tensor(sm(12), sm(c0), sm(s0), ALU.mult))
                link(v.tensor_scalar(sm(s1), sm(12), 2.0, None, ALU.mult))

            def s5_double(half, k, parts=("cos", "sin")):
                c, s_ = rot_c[half], rot_s[half]
                n = 2 ** k
                pw = lambda i: small[:, i, 8 * half:8 * half + 8].rearrange("p (i o) -> p i o", o=1)\
                    .to_broadcast([P, 8, n])
                ck, sk = pw(20 + 2 * k), pw(21 + 2 * k)
                a_, b_ = s5_tmp[:, 0, :, 0:n], s5_tmp[:, 1, :, 0:n]
                if half:
                    a_, b_ = (t[:, :, :].rearrange("p i (o t) -> p (i o) t", o=2)[:, :, 0:n] for t in (t1, t2))
                if k == 0:
                    link(v.memset(c[:, :, 0:1], 1.0))
                    link(v.memset(s_[:, :, 0:1], 0.0))
                if "cos" in parts:
                    link(v.tensor_tensor(a_, c[:, :, 0:n], ck, ALU.mult))
                    link(v.tensor_tensor(b_, s_[:, :, 0:n], sk, ALU.mult))
                    link(v.tensor_tensor(c[:, :, n:2 * n], a_, b_, ALU.subtract))
                if "sin" in parts:
                    link(v.tensor_tensor(a_, c[:, :, 0:n], sk, ALU.mult))
                    link(v.tensor_tensor(b_, s_[:, :, 0:n], ck, ALU.mult))
                    link(v.tensor_tensor(s_[:, :, n:2 * n], a_, b_, ALU.add))

            def leave(i):
                group_ready(v, i, TPU - 1)
                width = C if i < NZ - 1 else ZLAST
                v.tensor_scalar(z[:, 1, i * C:i * C + width], acc[i % 2][:, C:C + width], rstd[:, 0, 1:2], None,
                                ALU.mult).then_inc(grp_free, 1)

            for j in range(TPU):
                v.wait_ge(x_hi, j + 1)
                for k in range(TK * j, TK * (j + 1)):
                    i = v.scalar_tensor_tensor(out=u_lo[:, k, :], in0=xt[:, k, :], scalar=g_mix[:, k:k + 1],
                                               in1=u_hi[:, k, :].bitcast(F32), op0=ALU.mult, op1=ALU.subtract)
                i.then_inc(x_lo, 1)
                split_lo(v, 0, j)
            for i in range(NZ):
                for j in range(TPU):
                    if (i, j) == (1, X_SCALED - 1):
                        mean_square(0)
                    if (i, j) == (1, X_SCALED):
                        inverse(0)
                        v.wait_ge(rstd_done, 1)
                        leave(0)
                    if i * TPU + j + AHEAD >= TPU:
                        split_lo(v, i, j + AHEAD)
                    if i == 5 and j == 1:
                        s5_numerator()
                    if i == 5 and j == 4:
                        s5_coefficients()
                    if i == 6 and j < 6:
                        s5_power(j)
                    if i == 6 and j >= 6:
                        s5_double(0, j - 6)
                    if i == 7 and j < 3:
                        s5_double(0, j + 2)
                    if i == 7 and 3 <= j < 7:
                        s5_double(0, 5 + (j - 3) // 2, ("sin", "cos")[j % 2])
                if i:
                    leave(i)
                if i == 2:
                    s5_angles()
            def gate_tile(t):
                split_lo(v, U_MG + t // TPU, t % TPU + AHEAD)

            until = interleaved(gate_tile)
            until(A_BAND)
            v.wait_ge(sg["cmp_tr"], 1)
            v.tensor_copy(kv_ct[:, :, :].rearrange("p g t -> p (g t)"), aux[1][:, 0:NG * S]).then_inc(sg["cmp_copied"], 1)
            until(A_POOL)
            v.wait_ge(sg["pool_hi"], 4)
            for g in range(4):
                i = v.scalar_tensor_tensor(out=o_lo[:, 8 + g, :], in0=aux[0][:, g * S:(g + 1) * S],
                                           scalar=pool_s[:, g:g + 1], in1=o_hi[:, 8 + g, :].bitcast(F32),
                                           op0=ALU.mult, op1=ALU.subtract)
            i.then_inc(sg["pool_lo"], 1)
            v.wait_ge(sg["cmp_sum"], 1)
            v.wait_ge(sg["pool_lo"], 1)
            link(v.memset(kvc[:, :, :, :], 0.0))
            for g in range(NG):
                src = aux[1][:, C + g * NCMP:C + (g + 1) * NCMP].rearrange("p (o n) -> p o n", o=1)
                i = v.tensor_copy(kvc[:, g, :, 0:NCMP], src.to_broadcast([P, R, NCMP]))
            i.then_inc(sg["cmp_sb"], 1)
            until(A_QTR)
            v.wait_ge(sg["xg_tr"], 1)
            v.tensor_copy(xg[:, :, :].rearrange("p g e -> p (g e)"), aux[1][:, 0:NG * P])
            v.tensor_copy(xk[0:CP, :].rearrange("p (g e) -> p g e", g=NG),
                          aux[1][0:CP, 0:NG * P].rearrange("p (g e) -> p g e", g=NG)[:, :, 0:DH]).then_inc(sg["xg_sb"], 1)
            until(A_KTR)
            v.wait_ge(sg["kc_tr"], 1)
            v.tensor_copy(kc_t[:, :], aux[1][:, C:C + CP]).then_inc(sg["kc_sb"], 1)
            until(A_CS)
            v.wait_ge(sg["cs_done"], 1)
            v.wait_ge(mask_in, 32)
            sc = aux[1][:, :].rearrange("p (g x) -> p g x", g=NG)[:, :, 0:TT * R * CP]\
                .rearrange("p g (t r n) -> p t g r n", t=TT, r=R)

            def bc_mask(which, tt):
                return cmask[:, which, tt:tt + 1, :].to_broadcast([P, NH, CP])

            for tt in range(TT):
                link(v.tensor_tensor(pc[:, tt, :, :].rearrange("p (g r) n -> p g r n", g=NG), sc[:, tt, :, :, :],
                                     bc_mask(0, tt).rearrange("p (g r) n -> p g r n", g=NG), ALU.add))
            link(v.tensor_reduce(cstat[:, 0, :, :], pc[:, :, :, :], AX_X, ALU.max))
            for tt in range(TT):
                i = v.tensor_tensor(pc[:, tt, :, :], pc[:, tt, :, :],
                                    cstat[:, 0, tt, :].rearrange("p (h o) -> p h o", o=1).to_broadcast([P, NH, CP]),
                                    ALU.subtract)
                link(i)
            v.sem_inc(sg["cs_sub"], 1)
            until(A_CS + 2)
            v.wait_ge(sg["cs_exp"], 1)
            for tt in range(TT):
                link(v.tensor_tensor(pc[:, tt, :, :], pc[:, tt, :, :], bc_mask(1, tt), ALU.mult))
            link(v.tensor_reduce(cstat[:, 1, :, :], pc[:, :, :, :], AX_X, ALU.add))
            link(v.tensor_scalar(cstat[:, 2, :, :], cstat[:, 1, :, :], 1e-30, None, ALU.max))
            link(v.reciprocal(cstat[:, 3, :, :], cstat[:, 2, :, :]))
            v.wait_ge(sg["ngate_done"], 1)
            link(v.tensor_tensor(cstat[:, 2, :, :], cstat[:, 3, :, :], ngate[:, :, 0:NH], ALU.mult))
            for tt in range(TT):
                i = v.tensor_tensor(pc[:, tt, :, :], pc[:, tt, :, :],
                                    cstat[:, 2, tt, :].rearrange("p (h o) -> p h o", o=1).to_broadcast([P, NH, CP]),
                                    ALU.mult)
                link(i)
            v.sem_inc(sg["pc_done"], 1)
            until(A_PCT)
            v.wait_ge(sg["pc_tr"], 1)
            v.tensor_copy(pc_t[:, :, :, :].rearrange("p g t q -> p (g t q)"), aux[1][:, 0:C]).then_inc(sg["pc_sb"], 1)
            def rotate(i):
                c0, tt = (RQ0, RK0)[i // 2], i % 2
                x = z[:, tt, c0:c0 + BW]
                heads = x.rearrange("p (h d) -> p h d", h=RH)
                sw = x.rearrange("p (h i two) -> p h i two", h=RH, two=2)[:, :, :, ::-1]
                cs = rot[:, 0, tt:tt + 1, :].to_broadcast([P, RH, P])
                sn = rot[:, 1, tt:tt + 1, :].to_broadcast([P, RH, P])
                link(v.tensor_tensor(rtmp[:, :].rearrange("p (h i two) -> p h i two", h=RH, two=2), sw,
                                     sn.rearrange("p h (i two) -> p h i two", two=2), ALU.mult))
                link(v.tensor_tensor(heads, heads, cs, ALU.mult))
                v.tensor_tensor(x, x, rtmp[:, :], ALU.add).then_inc(sg["rot_done"], 1)

            for hd in range(NH):
                until(A_HEAD[hd])
                v.wait_ge(sg["sc_done"], hd + 1)
                s1 = aux[0][:, 0:C].rearrange("p (i k) -> p i k", i=2)
                s0 = aux[0][:, C:C + S].rearrange("p (i k) -> p i k", i=2)
                tri2 = tri[:, :].rearrange("p (o k) -> p o k", o=1).to_broadcast([P, 2, P])
                link(v.tensor_tensor(s1[:, :, P:S], s1[:, :, P:S], tri2, ALU.add))
                link(v.tensor_tensor(s0, s0, tri2, ALU.add))
                v.tensor_reduce(stat[:, hd, 0:2], s1, AX_X, ALU.max, negate=True)
                v.tensor_reduce(stat[:, hd, 2:4], s0, AX_X, ALU.max, negate=True).then_inc(sg["sc_max"], 1)
                until(A_HEAD[hd] + 1)
                v.wait_ge(sg["sc_exp"], 4 * hd + 4)
                link(v.reciprocal(stat[:, hd, 8:12], stat[:, hd, 4:8]))
                for n, tt in enumerate((1, 0)):
                    link(v.tensor_tensor(stat[:, hd, 12 + 2 * n:14 + 2 * n], stat[:, hd, 8 + 2 * n:10 + 2 * n],
                                         ngate[:, tt, NH + hd % 2 * R + hd // 2:3 * NH:NH], ALU.mult))
                for n, (o, w) in enumerate(((0, S), (S, S), (C, P), (C + P, P))):
                    i = v.tensor_scalar(prob[:, hd % 2, o:o + w], prob[:, hd % 2, o:o + w], stat[:, hd, 12 + n:13 + n],
                                        None, ALU.mult)
                i.then_inc(sg["sc_scaled"], 1)
                until(A_HEAD[hd] + 2)
                if hd < 4:
                    if hd == 0:
                        v.wait_ge(rot_in, 16)
                    else:
                        v.wait_ge(sg["rot_done"], hd)
                    rotate(hd)
                if hd % 4 == 3:
                    k = hd // 4 * 2
                    until(A_HEAD[hd] + 4)
                    v.wait_ge(sg["nsa_hi"], hd // 4 + 1)
                    v.tensor_tensor(o_lo[:, k:k + 2, :].rearrange("p k t -> p (k t)"), aux[1][:, C:2 * C],
                                    o_hi[:, k:k + 2, :].rearrange("p k t -> p (k t)").bitcast(F32), ALU.subtract)\
                        .then_inc(sg["nsa_lo"], 1)
            v.wait_ge(ret_in, 16)
            for hd in range(RH):
                until(A_RS[hd])
                v.wait_ge(sg["rs_done"], hd + 1)
                if hd >= 2:
                    v.wait_ge(sg["ry_done"], hd - 1)
                b = (hd % 2) * C
                v.tensor_tensor(rs_t[:, hd % 2, :], aux[0][:, b:b + 3 * P], decay[:, hd, :], ALU.mult)\
                    .then_inc(sg["rs_dec"], 1)
            until(A_RS[-1] + 1)
            v.wait_ge(sg["ry_ssq"], TT * RH)
            v.tensor_scalar(rstat[:, 0, :], rstat[:, 0, :], 1.0 / RD, EPS, ALU.mult, ALU.add).then_inc(sg["ry_var"], 1)
            v.wait_ge(sg["ry_std"], 1)
            link(v.reciprocal(rstat[:, 2, :], rstat[:, 1, :]))
            v.wait_ge(sg["rgate_done"], 1)
            for tt in range(TT):
                for hd in range(RH):
                    i = v.scalar_tensor_tensor(out=ry[:, tt, hd * P:(hd + 1) * P],
                                               in0=aux[1][:, tt * C + hd * P:tt * C + (hd + 1) * P],
                                               scalar=rstat[:, 2, tt * RH + hd:tt * RH + hd + 1],
                                               in1=rgate[:, tt, hd * P:(hd + 1) * P], op0=ALU.mult, op1=ALU.mult)
            i.then_inc(sg["ret_done"], 1)
            until(A_RQUAD)
            quad_lo(v, TP_RET, 1, o_lo[:, 12:16, :], o_hi[:, 12:16, :])
            v.wait_ge(tp_lo, TP_RET + 1)

            def s5_sum(q):
                v.wait_ge(sg["c_done"], 2 * q + 2)
                if q:
                    v.wait_ge(sg["y5_lo"], q)
                v.scalar_tensor_tensor(out=y5[:, :], in0=u5_t[:, q, :], scalar=s5_d[:, q:q + 1],
                                       in1=aux[1][:, (q % 2) * C:(q % 2) * C + S], op0=ALU.mult, op1=ALU.add)\
                    .then_inc(sg["y5_done"], 1)

            def s5_low(q):
                v.wait_ge(sg["y5_hi"], q + 1)
                v.tensor_tensor(y_lo[:, q, :], y5[:, :], y_hi[:, q, :].bitcast(F32), ALU.subtract)\
                    .then_inc(sg["y5_lo"], 1)

            v.wait_ge(s5_in, 16)
            by_state = lambda i: sm(i).rearrange("p (i o) -> p i o", o=1).to_broadcast([P, ST, 32])
            wide = lambda x: x[:, :, :].rearrange("p i t -> p (i t)").rearrange("p (i c) -> p i c", c=32)
            c_re, c_im = s5_c[:, 0, :, :], s5_c[:, 1, :, :]
            link(v.tensor_tensor(wide(t1), c_re, by_state(15), ALU.mult))
            link(v.tensor_tensor(wide(t2), c_im, by_state(16), ALU.mult))
            link(v.tensor_tensor(wide(sr), c_re, by_state(16), ALU.mult))
            until(A_S5[0] - 1)
            link(v.tensor_tensor(wide(si), c_im, by_state(15), ALU.mult))
            link(v.tensor_tensor(c_re, wide(t1), wide(t2), ALU.subtract))
            link(v.tensor_tensor(c_im, wide(sr), wide(si), ALU.add))
            A3 = lambda x: x[:, :, :]
            for n in range(4 * TT):
                q, hf = n // TT, n % TT
                if n == 4:
                    for k in range(5):
                        until(A_S5[3] + 8 + k)
                        s5_double(1, k)
                    for k in (5, 6):
                        for m_, part in enumerate(("cos", "sin")):
                            until(A_S5[3] + 13 + 2 * (k - 5) + m_)
                            s5_double(1, k, part)
                until(A_S5[n])
                gr = rot_c[q // 2][:, 4 * (q % 2):4 * (q % 2) + 4, :]
                gi = rot_s[q // 2][:, 4 * (q % 2):4 * (q % 2) + 4, :]
                v.wait_ge(sg["bu_done"], n + 1)
                br = aux[0][:, 0:C].rearrange("p (i t) -> p i t", i=4)
                bi = aux[0][:, C:2 * C].rearrange("p (i t) -> p i t", i=4)
                link(v.tensor_tensor(A3(t1), br, gr, ALU.mult))
                link(v.tensor_tensor(A3(t2), bi, gi, ALU.mult))
                if n:
                    v.wait_ge(sg["c_done"], n)
                until(A_S5[n] + 1)
                link(v.tensor_tensor(A3(vr), A3(t1), A3(t2), ALU.add))
                link(v.tensor_tensor(A3(t1), bi, gr, ALU.mult))
                until(A_S5[n] + 2)
                link(v.tensor_tensor(A3(t2), br, gi, ALU.mult))
                v.sem_inc(sg["bu_used"], 1)
                link(v.tensor_tensor(A3(vi), A3(t1), A3(t2), ALU.subtract))
                until(A_S5[n] + 3)
                if q and hf == 0:
                    s5_sum(q - 1)
                for i in range(4):
                    r_ = small[:, 2, 4 * q + i:4 * q + i + 1].to_broadcast([P, TH])
                    for src, dst, st in ((vr, sr, 34), (vi, si, 35)):
                        init = 0.0 if hf == 0 else small[:, st, i:i + 1]
                        link(v.tensor_tensor_scan(dst[:, i, :], r_, src[:, i, :], init, ALU.mult, ALU.add))
                    if i == 1:
                        until(A_S5[n] + 4)
                until(A_S5[n] + 5)
                link(v.tensor_tensor(A3(t1), gr, A3(sr), ALU.mult))
                link(v.tensor_tensor(A3(t2), gi, A3(si), ALU.mult))
                link(v.tensor_tensor(A3(vr), A3(t1), A3(t2), ALU.subtract))
                until(A_S5[n] + 6)
                if q and hf == 0:
                    s5_low(q - 1)
                link(v.tensor_tensor(A3(t1), gr, A3(si), ALU.mult))
                link(v.tensor_tensor(A3(t2), gi, A3(sr), ALU.mult))
                link(v.scalar_tensor_tensor(out=A3(vi), in0=A3(t1), scalar=-1.0, in1=A3(t2),
                                            op0=ALU.mult, op1=ALU.subtract))
                v.sem_inc(sg["sh_done"], 1)
                if hf == 0:
                    hr, hi_ = vr[:, :, TH - 1], vi[:, :, TH - 1]
                    c1, s1 = small[:, 20, 4 * q:4 * q + 4], small[:, 21, 4 * q:4 * q + 4]
                    a_, b_ = small[:, 36, 0:4], small[:, 37, 0:4]
                    link(v.tensor_tensor(a_, hr, c1, ALU.mult))
                    link(v.tensor_tensor(b_, hi_, s1, ALU.mult))
                    link(v.tensor_tensor(small[:, 34, 0:4], a_, b_, ALU.add))
                    link(v.tensor_tensor(a_, hr, s1, ALU.mult))
                    link(v.tensor_tensor(b_, hi_, c1, ALU.mult))
                    link(v.tensor_tensor(small[:, 35, 0:4], a_, b_, ALU.subtract))
            until(A_S5[7] + 8)
            s5_sum(3)
            until(A_S5[7] + 10)
            s5_low(3)
            v.wait_ge(pt_hi, 1)
            v.tensor_tensor(p_lo[:, :, :], p_raw[:, :, :], p_hi[:, :, :].bitcast(F32), ALU.subtract).then_inc(pt_lo, 1)
            until(A_END)
            for j in range(TPU):
                split_lo(v, U_GP, j + AHEAD)
                if j == 3:
                    v.wait_ge(grp_free, 2 * (G_GP + 1))
                    group_ready(v, U_GP, 3)
                    link(v.tensor_tensor(glu_o, acc[(G_GP + 1) % 2][:, :], glu_s, ALU.mult))
                    v.sem_inc(grp_free, 2)
                    v.sem_inc(sg["glu_done"], 1)
                    for i in range(2):
                        v.wait_ge(gate_out[i], 16 * 2 * NCH)
                if j >= 4:
                    group_ready(v, U_GP, j)
                    g = G_GP + j - 2
                    n = j - 4
                    v.tensor_copy(pp[:, :, n * C:(n + 1) * C], acc[g % 2][:, :].rearrange("p (t n) -> p t n", t=TT))\
                        .then_inc(grp_free, 2)
            quad_lo(v, TP_GLU, 1, o_lo[:, 4:8, :], o_hi[:, 4:8, :])

            def merged_lo(n):
                quad_lo(v, TP_M + n, n % 2, m_lo[:, 4 * n:4 * n + 4, :], m_hi[:, 4 * n:4 * n + 4, :])

            def hidden_lo(k):
                quad_lo(v, TP_H + k, (TP_H + k) % 2, v_lo[:, 4 * k:4 * k + 4, :], v_hi[:, 4 * k:4 * k + 4, :],
                        g_mlp[:, 4 * k:4 * k + 4])

            def last_lo(k):
                quad_lo(v, TP_P + k, (TP_P + k) % 2, v_lo[:, 4 * k:4 * k + 4, :], v_hi[:, 4 * k:4 * k + 4, :])

            for n in range(NCH):
                for j in range(TPU):
                    split_lo(v, U_BR + n, j + AHEAD)
                    if j % 2 == 1:
                        b = j // 2
                        g = G_BR + 4 * n + b
                        group_ready(v, U_BR + n, j)
                        v.wait_ge(gate_in[b], 16 * (n + 1))
                        if b == 0:
                            if n:
                                v.wait_ge(tp_in, TP_M + n)
                            link(v.tensor_tensor(merged[:, :], acc[g % 2][:, :], gates[:, b, :], ALU.mult))
                            v.sem_inc(grp_free, 2)
                            v.sem_inc(gate_used, 1)
                        else:
                            link(v.tensor_tensor(prodt[:, :], acc[g % 2][:, :], gates[:, b, :], ALU.mult))
                            v.sem_inc(grp_free, 2)
                            v.sem_inc(gate_used, 1)
                            link(v.tensor_tensor(merged[:, :], merged[:, :], prodt[:, :], ALU.add))
                    if j == 2 and n:
                        merged_lo(n - 1)
                v.sem_inc(sg["merged_done"], 1)

            def add_residual(n, par):
                hc = h[:, :, n * C:(n + 1) * C]
                v.tensor_tensor(hc, acc[par][:, :].rearrange("p (t n) -> p t n", t=TT), hc, ALU.add)\
                    .then_inc(grp_free, 2)

            for n in range(NCH):
                for j in range(TPU):
                    split_lo(v, U_WO + n, j + AHEAD)
                    if n == 0 and j == 2:
                        merged_lo(NCH - 1)
                    if n and j == 4:
                        hidden_lo(n - 1)
                group_ready(v, U_WO + n, TPU - 1)
                if n == 0:
                    v.wait_ge(h_in, 16)
                add_residual(n, (G_WO + n) % 2)

            def mlp_group(g, first, final):
                for n in range(2 * NCH):
                    u = g * (2 * NCH) + (U_FF + n)
                    for j in range(TPU):
                        split_lo(v, u, j + AHEAD)
                        if j == 4 and 1 <= n <= NCH:
                            quad_lo(v, g * NCH + (TP_FF + n - 1), (TP_FF + n - 1) % 2, f_lo[:, 4 * n - 4:4 * n, :],
                                    f_hi[:, 4 * n - 4:4 * n, :])
                        if first and n == 0 and j == 4:
                            hidden_lo(NCH - 1)
                        if first and n == 0 and j == TPU - 1:
                            mean_square(1)
                            inverse(1)
                        if final and j == 4 and n > NCH:
                            last_lo(n - NCH - 1)
                    if n < NCH:
                        v.wait_ge(grp_free, g * (4 * NCH) + 2 * (G_FF + n + 1))
                        rl = relu[n % 2]
                        v.tensor_tensor(rl[:, :], rl[:, :], rl[:, :], ALU.mult).then_inc(sg["sq_done"], 1)
                    else:
                        group_ready(v, u, TPU - 1)
                        add_residual(n - NCH, (G_FF + n) % 2)

            mlp_group(0, True, False)
            with v.Fori(1, NFG - 1) as g:
                mlp_group(g, False, False)
            mlp_group(NFG - 1, False, True)

            def weigh(n):
                for tt in range(TT):
                    v.wait_ge(last_ssq, TT * n + tt + 1)
                    hc = h[:, tt, n * C:(n + 1) * C]
                    v.tensor_tensor(hc, hc, g_fin[:, n * C:(n + 1) * C], ALU.mult).then_inc(h_weighted, 1)

            for n in range(NCH):
                for j in range(TPU):
                    split_lo(v, U_PG + n, j + AHEAD)
                    if n == 0 and j == 4:
                        last_lo(NCH - 1)
                    if n and j == 5:
                        weigh(n - 1)
                if n == 0:
                    v.wait_ge(fin_in, 16)
                for tt in range(TT):
                    v.wait_ge(grp_free, 2 * (G_PG + n) + tt + 1)
                    ga = pgate[:, n, tt * C:(tt + 1) * C]
                    hc = h[:, tt, n * C:(n + 1) * C]
                    link(v.tensor_tensor(ga, ga, pp[:, tt, n * C:(n + 1) * C], ALU.mult))
                    v.tensor_tensor(hc, hc, ga, ALU.add).then_inc(h_done, 1)
            v.wait_ge(last_ssq, TT * NCH)
            link(v.tensor_reduce(ssq[:, 2, :], ssq_last[:, :, :], AX_X, ALU.add))
            v.tensor_scalar(ssq[:, 2, :], ssq[:, 2, :], 1.0 / D, EPS, ALU.mult, ALU.add).then_inc(var_done, 1)
            weigh(NCH - 1)
            inverse(2)
            v.wait_ge(rstd_done, 3)
            v.wait_ge(h_weighted, TT * NCH)
            for n in range(NCH):
                hc = h[:, 0, n * C:(n + 1) * C]
                v.tensor_scalar(hc, hc, rstd[:, 2, 0:1], None, ALU.mult).then_inc(out_dve, 1)


def band_matrix():
    t = np.arange(S)
    out = np.zeros((S, 4, S), np.float32)
    for g, w in enumerate((2, 4, 8, 16)):
        inside = (t[None, :] >= t[:, None]) & (t[None, :] < t[:, None] + w)
        out[:, g] = inside / np.minimum(t + 1, w)[None, :] - (t[None, :] == t[:, None])
    return np.ascontiguousarray(out.reshape(TT, P, 4, S).transpose(1, 2, 0, 3))


def rotation():
    angle = np.repeat(1.0 / 10000.0 ** np.linspace(0.0, 1.0, RD // 2), 2)
    angle = np.arange(S)[:, None] * angle[None, :]
    sign = np.where(np.arange(RD) % 2 == 0, -1.0, 1.0)
    both = np.stack([np.cos(angle), np.sin(angle) * sign]).reshape(2, TT, P, RD)
    return np.ascontiguousarray(both.transpose(2, 0, 1, 3).astype(np.float32))


def decays():
    gamma = 1.0 - 2.0 ** (-5.0 - np.arange(RH))
    rel = np.arange(S)[None, :] - np.arange(P)[:, None]
    d = np.where(rel >= 0, gamma[:, None, None] ** np.maximum(rel, 0), 0.0) * RD ** -0.5
    d = np.concatenate([d, d[:, :, :P]], axis=2)
    return np.ascontiguousarray(d.transpose(1, 0, 2).astype(np.float32))


def compressed_mask():
    t, n = np.arange(S)[:, None], np.arange(CP)[None, :]
    seen = (n < NCMP) & (16 * n + 31 <= t)
    both = np.stack([np.where(seen, 0.0, NEG), seen.astype(np.float64)]).reshape(2, TT, P, CP)
    return np.ascontiguousarray(both.transpose(2, 0, 1, 3).astype(np.float32))


def kernel(x, p, g_mix, w_in, w_cmp_k, w_cmp_v, s5_a_re, s5_a_im, s5_log_dt, s5_b_re, s5_b_im,
           s5_c_re, s5_c_im, s5_d, s5_w_glu, pool_w, pool_scale, w_branch, w_out, g_mlp,
           w_mlp_up, w_mlp_down, w_ple_gate, w_ple_proj, g_final):
    import concourse.bacc as bacc
    from concourse.bass_utils import run_bass_kernel_spmd

    f32 = np.float32
    x, p = np.asarray(x), np.asarray(p)

    def by_partition(v):
        return np.ascontiguousarray(np.asarray(v).reshape(-1, P).T)

    def states(v):
        return np.asarray(v)[0].reshape(ST, P).T

    w_cmp = np.zeros((P, 32, P), f32)
    w_cmp[:DH, :, :DH] = np.asarray(w_cmp_k)[0].transpose(1, 0, 2)
    w_cmp[DH:, :, DH:] = np.asarray(w_cmp_v)[0].transpose(1, 0, 2)
    s5_b = np.zeros((4, 4, 2, SC, 2, 4, 2, SN), f32)
    s5_c = np.zeros((2, SN, 2, ST, 2, SC), f32)
    for im, (b, c) in enumerate(((s5_b_re, s5_c_re), (s5_b_im, s5_c_im))):
        b = np.asarray(b)[0].reshape(4, 4, 2, SN, SC)
        c = np.asarray(c)[0].reshape(ST, 2, SC, SN)
        for j in range(2):
            for i in range(4):
                s5_b[:, i, j, :, im, i, j, :] = b[:, i, j].transpose(0, 2, 1)
            s5_c[j, :, im, :, j, :] = c[:, j].transpose(2, 0, 1)
    dt = np.broadcast_to(np.asarray(s5_log_dt)[0][:, None], (SG, SN)).reshape(ST, P).T
    causal = np.arange(P)[None, :] <= np.arange(P)[:, None]
    head_order = np.arange(NH * DH).reshape(NG, R, DH).transpose(1, 0, 2).ravel()
    pair_order = np.arange(2 * NG * DH).reshape(2, NG, DH).transpose(1, 0, 2).ravel()
    order = np.concatenate([Q0 + head_order, KV0 + pair_order, np.arange(KV0 + 2 * P, ZS)])
    w_in = np.asarray(w_in)[0]
    w_branch = np.asarray(w_branch)[0].reshape(D, D)
    w_branch = np.concatenate([w_branch[head_order], w_branch[BW:]])
    arrays = {
        "x": x[0], "xt": x[0].T, "pt": p[0, 0].T,
        "g_mix": by_partition(g_mix), "g_mlp": by_partition(g_mlp),
        "g_final": np.broadcast_to(np.asarray(g_final)[None, :], (P, D)),
        "w_in": w_in, "w_mix": w_in[:, order], "w_glu": np.asarray(s5_w_glu)[0], "w_pp": np.asarray(w_ple_proj)[0],
        "w_branch": w_branch, "w_out": np.asarray(w_out)[0],
        "w_up": np.asarray(w_mlp_up)[0], "w_down": np.asarray(w_mlp_down)[0], "w_pg": np.asarray(w_ple_gate)[0],
        "w_pool": np.asarray(pool_w)[0], "pool_scale": by_partition(pool_scale), "w_cmp": w_cmp,
        "s5p": np.stack([states(s5_a_re), states(s5_a_im), dt], axis=1),
        "s5_b": s5_b.reshape(4, P, 2, 4, P), "s5_c": s5_c.reshape(P, 2, ST, 32), "s5_d": by_partition(s5_d),
        "ident": np.eye(P, dtype=f32), "band": band_matrix(), "rot": rotation(), "decay": decays(),
        "cmask": compressed_mask(), "tri": np.where(causal, 0.0, NEG).astype(f32),
    }
    arrays = {f"in_{k}": np.ascontiguousarray(v) for k, v in arrays.items()}
    nc = bacc.Bacc("TRN2", target_bir_lowering=False, num_devices=1)
    aps = {k[3:]: nc.dram_tensor(k, v.shape, mybir.dt.from_np(v.dtype), kind="ExternalInput").ap()
           for k, v in arrays.items()}
    out = nc.dram_tensor("out", (S, D), F32, kind="ExternalOutput").ap()
    hybrid_layer(nc, aps, out)
    r = run_bass_kernel_spmd(nc, [arrays], core_ids=[0])
    return r.results[0]["out"].reshape(1, S, D)
```
